# Optimizing a Trainium2 kernel written in Bass

```python
import math
import jax
import jax.numpy as jnp
from jax import lax
import numpy as np

D_MODEL = 1024
BATCH = 1
SEQ = 256
DEPTH = 1

N_HEADS = 8
HEAD_DIM = 64
ATTN_WIDTH = N_HEADS * HEAD_DIM
ROPE_THETA = 10000.0
MOBA_BLOCK = 256
MOBA_TOPK = 3
Q_CHUNK = 64
SSM_GROUP_SIZE = 16
SSM_GROUPS = 32
SSM_WIDTH = SSM_GROUPS * SSM_GROUP_SIZE
SSM_STATE = 64
DT_MIN = 0.001
DT_MAX = 0.1
IN_WIDTH = SSM_WIDTH + 3 * ATTN_WIDTH + 2 * D_MODEL
N_EXPERTS = 32
TOP_K = 4
D_FF = D_MODEL
SWIGLU_ALPHA = 1.702
SWIGLU_LIMIT = 7.0
MOE_BLOCK = 128
NORM_EPS = 1e-6
NEG_INF = -1e30


def rms_norm(t, g):
    tf = t.astype(jnp.float32)
    tf = tf * lax.rsqrt(jnp.mean(tf * tf, axis=-1, keepdims=True) + NORM_EPS)
    return tf * g.astype(jnp.float32)

def apply_rope(t, positions):
    half = HEAD_DIM // 2
    inv_freq = ROPE_THETA ** (-jnp.arange(half, dtype=jnp.float32) / half)
    ang = positions.astype(jnp.float32)[..., None] * inv_freq
    cos = jnp.cos(ang)[:, :, None, :]
    sin = jnp.sin(ang)[:, :, None, :]
    tf = t.astype(jnp.float32)
    t1, t2 = tf[..., :half], tf[..., half:]
    return jnp.concatenate([t1 * cos - t2 * sin, t2 * cos + t1 * sin], axis=-1)

def _linear_recurrence(left, right):
    a_l, b_l = left
    a_r, b_r = right
    return a_r * a_l, a_r * b_l + b_r

def s5_mixer(u, lam_re, lam_im, log_dt, b_re, b_im, c_re, c_im, d_skip, w_glu):
    bsz, seq, _ = u.shape
    uf = u.astype(jnp.float32)
    ug = uf.reshape(bsz, seq, SSM_GROUPS, SSM_GROUP_SIZE)
    lam = lax.complex(lam_re.astype(jnp.float32), lam_im.astype(jnp.float32))
    dt = jnp.exp(log_dt.astype(jnp.float32))[:, None]
    lam_bar = jnp.exp(lam * dt)
    b_mat = lax.complex(b_re.astype(jnp.float32), b_im.astype(jnp.float32))
    c_mat = lax.complex(c_re.astype(jnp.float32), c_im.astype(jnp.float32))
    b_bar = ((lam_bar - 1.0) / lam)[..., None] * b_mat
    bu = jnp.einsum('gpc,bsgc->bsgp', b_bar, ug.astype(jnp.complex64))
    a = jnp.broadcast_to(lam_bar, bu.shape)
    _, states = lax.associative_scan(_linear_recurrence, (a, bu), axis=1)
    y = jnp.einsum('gcp,bsgp->bsgc', c_mat, states).real.reshape(bsz, seq, SSM_WIDTH)
    y = y + d_skip.astype(jnp.float32) * uf
    y = jax.nn.gelu(y)
    y = y * jax.nn.sigmoid(y @ w_glu.astype(jnp.float32))
    return y

def moba_attention(q, k, v):
    bsz, nh, seq, hd = q.shape
    qf, kf, vf = q.astype(jnp.float32), k.astype(jnp.float32), v.astype(jnp.float32)
    nb = -(-seq // MOBA_BLOCK)
    pad = nb * MOBA_BLOCK - seq
    kb = jnp.pad(kf, ((0, 0), (0, 0), (0, pad), (0, 0))).reshape(bsz, nh, nb, MOBA_BLOCK, hd)
    vb = jnp.pad(vf, ((0, 0), (0, 0), (0, pad), (0, 0))).reshape(bsz, nh, nb, MOBA_BLOCK, hd)
    k_mean = jnp.mean(kb, axis=3)
    n_sel = min(MOBA_TOPK, nb)
    scale = HEAD_DIM ** -0.5
    n_chunks = seq // Q_CHUNK
    q_chunks = qf.reshape(bsz, nh, n_chunks, Q_CHUNK, hd).transpose(2, 0, 1, 3, 4)
    gather_blocks = jax.vmap(jax.vmap(lambda blocks, idx: blocks[idx]))
    block_ids = jnp.arange(nb)
    offs = jnp.arange(MOBA_BLOCK)

    def chunk_attend(args):
        ci, qi = args
        q_pos = ci * Q_CHUNK + jnp.arange(Q_CHUNK)
        q_blk = q_pos // MOBA_BLOCK
        own = (ci * Q_CHUNK) // MOBA_BLOCK
        gate = jnp.einsum('bhqd,bhnd->bhqn', qi, k_mean)
        gate = jnp.where(block_ids[None, :] < q_blk[:, None], gate, NEG_INF)
        _, sel = lax.top_k(gate, n_sel)
        sel_ok = sel < q_blk[:, None]
        k_sel = gather_blocks(kb, sel)
        v_sel = gather_blocks(vb, sel)
        s_sel = jnp.einsum('bhqd,bhqnld->bhqnl', qi, k_sel) * scale
        s_sel = jnp.where(sel_ok[..., None], s_sel, NEG_INF).reshape(bsz, nh, Q_CHUNK, n_sel * MOBA_BLOCK)
        k_own = lax.dynamic_index_in_dim(kb, own, axis=2, keepdims=False)
        v_own = lax.dynamic_index_in_dim(vb, own, axis=2, keepdims=False)
        s_own = jnp.einsum('bhqd,bhld->bhql', qi, k_own) * scale
        k_pos = own * MOBA_BLOCK + offs
        s_own = jnp.where(k_pos[None, :] <= q_pos[:, None], s_own, NEG_INF)
        p = jax.nn.softmax(jnp.concatenate([s_sel, s_own], axis=-1), axis=-1)
        p_sel = p[..., :n_sel * MOBA_BLOCK].reshape(bsz, nh, Q_CHUNK, n_sel, MOBA_BLOCK)
        p_own = p[..., n_sel * MOBA_BLOCK:]
        return (jnp.einsum('bhqnl,bhqnld->bhqd', p_sel, v_sel)
                + jnp.einsum('bhql,bhld->bhqd', p_own, v_own))

    out = lax.map(chunk_attend, (jnp.arange(n_chunks), q_chunks))
    return out.transpose(1, 2, 0, 3, 4).reshape(bsz, nh, seq, hd)

def moe_ffn(h, router_w, router_b, w_gate, b_gate, w_up, b_up, w_down, b_down):
    bsz, seq, d = h.shape
    n_tok = bsz * seq
    hf = h.reshape(n_tok, d).astype(jnp.float32)
    logits = hf @ router_w.astype(jnp.float32) + router_b.astype(jnp.float32)
    top_val, top_idx = lax.top_k(logits, TOP_K)
    top_w = jax.nn.softmax(top_val, axis=-1)
    n_assign = n_tok * TOP_K
    eid = top_idx.reshape(n_assign)
    order = jnp.argsort(eid)
    s_eid = eid[order]
    s_tok = order // TOP_K
    s_w = top_w.reshape(n_assign)[order]
    counts = jnp.bincount(eid, length=N_EXPERTS)
    starts = jnp.cumsum(counts) - counts
    padded = (counts + MOE_BLOCK - 1) // MOE_BLOCK * MOE_BLOCK
    p_ends = jnp.cumsum(padded)
    p_starts = p_ends - padded
    dest = p_starts[s_eid] + jnp.arange(n_assign) - starts[s_eid]
    n_blocks = -(-n_assign // MOE_BLOCK) + N_EXPERTS
    n_rows = n_blocks * MOE_BLOCK
    row_tok = jnp.full((n_rows,), n_tok, dtype=jnp.int32).at[dest].set(s_tok.astype(jnp.int32))
    row_w = jnp.zeros((n_rows,), jnp.float32).at[dest].set(s_w)
    blk_exp = jnp.minimum(jnp.searchsorted(p_ends, jnp.arange(n_blocks) * MOE_BLOCK, side='right'),
                          N_EXPERTS - 1)
    h_pad = jnp.concatenate([hf, jnp.zeros((1, d), jnp.float32)], axis=0)
    xs = h_pad[row_tok].reshape(n_blocks, MOE_BLOCK, d)

    def expert_block(args):
        xb, e = args
        g = xb @ w_gate[e].astype(jnp.float32) + b_gate[e].astype(jnp.float32)
        u = xb @ w_up[e].astype(jnp.float32) + b_up[e].astype(jnp.float32)
        g = jnp.minimum(g, SWIGLU_LIMIT)
        u = jnp.clip(u, -SWIGLU_LIMIT, SWIGLU_LIMIT)
        act = g * jax.nn.sigmoid(SWIGLU_ALPHA * g) * (u + 1.0)
        return act @ w_down[e].astype(jnp.float32) + b_down[e].astype(jnp.float32)

    yb = lax.map(expert_block, (xs, blk_exp)).reshape(n_rows, d)
    y = jnp.zeros((n_tok + 1, d), jnp.float32).at[row_tok].add(yb * row_w[:, None])
    return y[:n_tok].reshape(bsz, seq, d)

def first_inputs(seed: int = 0) -> dict:
    key = jax.random.key(seed)
    ks = jax.random.split(key, 32)
    f32 = jnp.float32
    nrm = lambda k, shape, s: jax.random.normal(k, shape, f32) * s
    L, D, G, P, HG, E, F = DEPTH, D_MODEL, SSM_GROUPS, SSM_STATE, SSM_GROUP_SIZE, N_EXPERTS, D_FF
    x = jax.random.normal(ks[0], (BATCH, SEQ, D), f32)
    c = jax.random.normal(ks[1], (BATCH, D), f32)
    offset = jax.random.randint(ks[2], (BATCH, 1), 0, 1024, dtype=jnp.int32)
    positions = (jnp.arange(SEQ, dtype=jnp.int32)[None, :] + offset).astype(jnp.int32)
    lam_im0 = jnp.pi * jnp.arange(P, dtype=f32)
    return {
        'x': x,
        'c': c,
        'positions': positions,
        'ada_w': nrm(ks[3], (L, D, 6 * D), 0.5 * D ** -0.5),
        'ada_b': nrm(ks[4], (L, 6 * D), 0.01),
        'mix_pre_g': 1.0 + nrm(ks[5], (L, D), 0.05),
        'mix_post_g': 1.0 + nrm(ks[6], (L, D), 0.05),
        'ffn_pre_g': 1.0 + nrm(ks[7], (L, D), 0.05),
        'ffn_post_g': 1.0 + nrm(ks[8], (L, D), 0.05),
        'w_in': nrm(ks[9], (L, D, IN_WIDTH), D ** -0.5),
        'ssm_lam_re': -0.5 + nrm(ks[10], (L, G, P), 0.01),
        'ssm_lam_im': lam_im0 + nrm(ks[11], (L, G, P), 0.01),
        'ssm_log_dt': jax.random.uniform(ks[12], (L, G), f32, math.log(DT_MIN), math.log(DT_MAX)),
        'ssm_b_re': nrm(ks[13], (L, G, P, HG), (2 * HG) ** -0.5),
        'ssm_b_im': nrm(ks[14], (L, G, P, HG), (2 * HG) ** -0.5),
        'ssm_c_re': nrm(ks[15], (L, G, HG, P), (2 * P) ** -0.5),
        'ssm_c_im': nrm(ks[16], (L, G, HG, P), (2 * P) ** -0.5),
        'ssm_d': nrm(ks[17], (L, SSM_WIDTH), 1.0),
        'ssm_w_glu': nrm(ks[18], (L, SSM_WIDTH, SSM_WIDTH), SSM_WIDTH ** -0.5),
        'w_ssm_branch': nrm(ks[19], (L, SSM_WIDTH, D), SSM_WIDTH ** -0.5),
        'w_attn_branch': nrm(ks[20], (L, ATTN_WIDTH, D), ATTN_WIDTH ** -0.5),
        'w_out': nrm(ks[21], (L, D, D), D ** -0.5),
        'router_w': nrm(ks[22], (L, D, E), D ** -0.5),
        'router_b': nrm(ks[23], (L, E), 0.01),
        'w_gate': nrm(ks[24], (L, E, D, F), D ** -0.5),
        'b_gate': nrm(ks[25], (L, E, F), 0.01),
        'w_up': nrm(ks[26], (L, E, D, F), D ** -0.5),
        'b_up': nrm(ks[27], (L, E, F), 0.01),
        'w_down': nrm(ks[28], (L, E, F, D), F ** -0.5),
        'b_down': nrm(ks[29], (L, E, D), 0.01),
    }

def first_block(x, c, positions, ada_w, ada_b, mix_pre_g, mix_post_g, ffn_pre_g, ffn_post_g,
              w_in, ssm_lam_re, ssm_lam_im, ssm_log_dt, ssm_b_re, ssm_b_im, ssm_c_re, ssm_c_im,
              ssm_d, ssm_w_glu, w_ssm_branch, w_attn_branch, w_out,
              router_w, router_b, w_gate, b_gate, w_up, b_up, w_down, b_down):
    bsz, seq, _ = x.shape
    dtype = x.dtype
    cond = jax.nn.silu(c.astype(jnp.float32))
    splits = [SSM_WIDTH, SSM_WIDTH + ATTN_WIDTH, SSM_WIDTH + 2 * ATTN_WIDTH,
              SSM_WIDTH + 3 * ATTN_WIDTH, SSM_WIDTH + 3 * ATTN_WIDTH + D_MODEL]
    for l in range(DEPTH):
        ada = cond @ ada_w[l].astype(jnp.float32) + ada_b[l].astype(jnp.float32)
        sh_m, sc_m, gt_m, sh_f, sc_f, gt_f = [a[:, None, :] for a in jnp.split(ada, 6, axis=-1)]

        h = (rms_norm(x, mix_pre_g[l]) * (1.0 + sc_m) + sh_m).astype(dtype)
        proj = h @ w_in[l]
        u_s, q, k, v, g_s, g_a = jnp.split(proj, splits, axis=-1)
        y_s = s5_mixer(u_s, ssm_lam_re[l], ssm_lam_im[l], ssm_log_dt[l], ssm_b_re[l], ssm_b_im[l],
                       ssm_c_re[l], ssm_c_im[l], ssm_d[l], ssm_w_glu[l])
        q = apply_rope(q.reshape(bsz, seq, N_HEADS, HEAD_DIM), positions).transpose(0, 2, 1, 3)
        k = apply_rope(k.reshape(bsz, seq, N_HEADS, HEAD_DIM), positions).transpose(0, 2, 1, 3)
        v = v.reshape(bsz, seq, N_HEADS, HEAD_DIM).transpose(0, 2, 1, 3)
        y_a = moba_attention(q, k, v).transpose(0, 2, 1, 3).reshape(bsz, seq, ATTN_WIDTH)
        merged = (jax.nn.sigmoid(g_s.astype(jnp.float32)) * (y_s @ w_ssm_branch[l].astype(jnp.float32))
                  + jax.nn.sigmoid(g_a.astype(jnp.float32)) * (y_a @ w_attn_branch[l].astype(jnp.float32)))
        mix = merged @ w_out[l].astype(jnp.float32)
        x = (x.astype(jnp.float32) + gt_m * rms_norm(mix, mix_post_g[l])).astype(dtype)

        h2 = (rms_norm(x, ffn_pre_g[l]) * (1.0 + sc_f) + sh_f).astype(dtype)
        ff = moe_ffn(h2, router_w[l], router_b[l], w_gate[l], b_gate[l], w_up[l], b_up[l],
                     w_down[l], b_down[l])
        x = (x.astype(jnp.float32) + gt_f * rms_norm(ff, ffn_post_g[l])).astype(dtype)
    return x


DEPTH_2 = 2

N_MIXERS = 2
EPS = 1e-6
NEG_INF_2 = -1e30

MIX_WIDTH = D_MODEL
TOK_WIDTH = 3 * MIX_WIDTH // 4
MEM_WIDTH = MIX_WIDTH // 4

DILATED_GROUPS = ((128, 1), (512, 4), (2048, 16))
ATT_HEAD_DIM = 64
ATT_HEADS = TOK_WIDTH // ATT_HEAD_DIM
HEADS_PER_GROUP = ATT_HEADS // len(DILATED_GROUPS)
BAND_BLOCK = 64
REL_BUCKETS = 32
REL_MAX_DIST = 1024

DN_HEAD_DIM = 128
DN_HEADS = TOK_WIDTH // DN_HEAD_DIM
DN_CONV = 5
DN_CHUNK = 64

MEM_LEN = 256
MEM_HEADS = 4
MEM_HEAD_DIM = MEM_WIDTH // MEM_HEADS

_FF_RAW = -(-8 * D_MODEL // 3)
D_FF_2 = -(-_FF_RAW // 256) * 256

ATT_IN = 3 * TOK_WIDTH + MEM_WIDTH
DN_IN = 4 * TOK_WIDTH + 4 * DN_HEADS + MEM_WIDTH


def _rms_norm(x, gain):
    xf = x.astype(jnp.float32)
    y = xf * lax.rsqrt(jnp.mean(xf * xf, axis=-1, keepdims=True) + EPS) * gain.astype(jnp.float32)
    return y.astype(x.dtype)

def _l2norm(t):
    return t * lax.rsqrt(jnp.sum(t * t, axis=-1, keepdims=True) + EPS)

def _t5_bucket(rel):
    half = REL_BUCKETS // 2
    max_exact = half // 2
    n = np.abs(rel)
    large = max_exact + (np.log(np.maximum(n, 1) / max_exact) / math.log(REL_MAX_DIST / max_exact)
                         * (half - max_exact)).astype(np.int64)
    large = np.minimum(large, half - 1)
    return ((rel > 0) * half + np.where(n < max_exact, n, large)).astype(np.int32)

def _dilated_band_attention(q, k, v, bias, dil, half):
    b, s, h, dh = q.shape
    L = s // dil
    nb = -(-L // BAND_BLOCK)
    lp = nb * BAND_BLOCK
    n = b * dil

    def to_sub(t):
        return t.reshape(b, L, dil, h, dh).transpose(0, 2, 1, 3, 4).reshape(n, L, h, dh)

    def key_windows(t):
        t = jnp.pad(to_sub(t), ((0, 0), (BAND_BLOCK, lp - L + BAND_BLOCK), (0, 0), (0, 0)))
        t = t.reshape(n, nb + 2, BAND_BLOCK, h, dh)
        return jnp.concatenate([t[:, :-2], t[:, 1:-1], t[:, 2:]], axis=2)

    qs = jnp.pad(to_sub(q), ((0, 0), (0, lp - L), (0, 0), (0, 0))).reshape(n, nb, BAND_BLOCK, h, dh)
    kw = key_windows(k)
    vw = key_windows(v)

    rel = np.arange(3 * BAND_BLOCK)[None, :] - BAND_BLOCK - np.arange(BAND_BLOCK)[:, None]
    in_band = np.abs(rel) <= half
    kpos = (np.arange(nb)[:, None] - 1) * BAND_BLOCK + np.arange(3 * BAND_BLOCK)[None, :]
    valid = in_band[None] & ((kpos >= 0) & (kpos < L))[:, None, :]
    bias_band = jnp.transpose(bias[np.clip(rel + half, 0, 2 * half)], (2, 0, 1)).astype(jnp.float32)

    logits = jnp.einsum('nbqhd,nbkhd->nbhqk', qs, kw, preferred_element_type=jnp.float32)
    logits = jnp.where(valid[None, :, None], logits + bias_band[None, None], NEG_INF_2)
    m = jnp.max(logits, axis=-1)
    p = jnp.exp(logits - m[..., None])
    den = jnp.sum(p, axis=-1)
    o = jnp.einsum('nbhqk,nbkhd->nbqhd', p.astype(v.dtype), vw, preferred_element_type=jnp.float32)
    o = o / jnp.swapaxes(den, -1, -2)[..., None]

    def from_sub(t):
        rest = t.shape[3:]
        t = t.reshape((b, dil, lp) + rest)[:, :, :L]
        return jnp.swapaxes(t, 1, 2).reshape((b, s) + rest)

    return from_sub(o), from_sub(jnp.swapaxes(m, -1, -2)), from_sub(jnp.swapaxes(den, -1, -2))

def _dilated_mixture(q, k, v, rel_bias):
    b, s = q.shape[:2]
    outs, lses = [], []
    for gi, (window, dil) in enumerate(DILATED_GROUPS):
        half = window // (2 * dil)
        heads = slice(gi * HEADS_PER_GROUP, (gi + 1) * HEADS_PER_GROUP)
        bias = rel_bias[_t5_bucket(np.arange(-half, half + 1) * dil)][:, heads]
        o, m, den = _dilated_band_attention(q[:, :, heads], k[:, :, heads], v[:, :, heads], bias, dil, half)
        outs.append(o)
        lses.append(m + jnp.log(den))
    wts = jax.nn.softmax(jnp.stack(lses), axis=0)
    mixed = jnp.concatenate([o * w[..., None] for o, w in zip(outs, wts)], axis=2)
    return mixed.reshape(b, s, TOK_WIDTH)

def _memory_attention(q_mem, mem_n, w_kv):
    b, s, _ = q_mem.shape
    q = q_mem.reshape(b, s, MEM_HEADS, MEM_HEAD_DIM) * (MEM_HEAD_DIM ** -0.5)
    k, v = jnp.split(mem_n @ w_kv, 2, axis=-1)
    k = k.reshape(b, -1, MEM_HEADS, MEM_HEAD_DIM)
    v = v.reshape(b, -1, MEM_HEADS, MEM_HEAD_DIM)
    logits = jnp.einsum('bshd,bmhd->bhsm', q, k, preferred_element_type=jnp.float32)
    p = jax.nn.softmax(logits, axis=-1)
    o = jnp.einsum('bhsm,bmhd->bshd', p.astype(v.dtype), v)
    return o.reshape(b, s, MEM_WIDTH)

def _gated_delta_chunked(q, k, v, g, beta):
    b, s, h, dk = q.shape
    dv = v.shape[-1]
    nc = s // DN_CHUNK

    def chunks(t):
        t = t.reshape((b, nc, DN_CHUNK, h) + t.shape[3:])
        return jnp.moveaxis(t, 3, 1)

    q, k, v, g, beta = (chunks(t) for t in (q, k, v, g, beta))
    g = jnp.cumsum(g, axis=-1)
    tril = np.tril(np.ones((DN_CHUNK, DN_CHUNK), dtype=bool))
    strict = np.tril(np.ones((DN_CHUNK, DN_CHUNK), dtype=bool), -1)
    decay = jnp.exp(jnp.where(tril, g[..., :, None] - g[..., None, :], NEG_INF_2))
    k_beta = k * beta[..., None]
    lmat = jnp.where(strict, jnp.einsum('bhnik,bhnjk->bhnij', k_beta, k) * decay, 0.0)
    a = lmat + jnp.eye(DN_CHUNK, dtype=jnp.float32)
    rhs = jnp.concatenate([v * beta[..., None], k_beta * jnp.exp(g)[..., None]], axis=-1)
    sol = lax.linalg.triangular_solve(a, rhs, left_side=True, lower=True, unit_diagonal=True)
    u, w = sol[..., :dv], sol[..., dv:]
    intra = jnp.where(tril, jnp.einsum('bhnik,bhnjk->bhnij', q, k) * decay, 0.0)

    def step(state, inp):
        qc, kc, uc, wc, gc, ac = inp
        v_new = uc - jnp.einsum('bhck,bhkv->bhcv', wc, state)
        out = (jnp.einsum('bhck,bhkv->bhcv', qc * jnp.exp(gc)[..., None], state)
               + jnp.einsum('bhij,bhjv->bhiv', ac, v_new))
        g_last = gc[..., -1]
        state = (state * jnp.exp(g_last)[..., None, None]
                 + jnp.einsum('bhck,bhcv->bhkv', kc * jnp.exp(g_last[..., None] - gc)[..., None], v_new))
        return state, out

    xs = tuple(jnp.moveaxis(t, 2, 0) for t in (q, k, u, w, g, intra))
    state0 = jnp.zeros((b, h, dk, dv), jnp.float32)
    _, out = lax.scan(step, state0, xs)
    out = jnp.moveaxis(out, 0, 2)
    return jnp.moveaxis(out, 1, 3).reshape(b, s, h, dv)

def _attention_sublayer(h, mem_n, w_in, w_out, rel_bias, w_mem_kv):
    b, s, _ = h.shape
    q, k, v, q_mem = jnp.split(h @ w_in, [TOK_WIDTH, 2 * TOK_WIDTH, 3 * TOK_WIDTH], axis=-1)
    q = q.reshape(b, s, ATT_HEADS, ATT_HEAD_DIM) * (ATT_HEAD_DIM ** -0.5)
    k = k.reshape(b, s, ATT_HEADS, ATT_HEAD_DIM)
    v = v.reshape(b, s, ATT_HEADS, ATT_HEAD_DIM)
    mixed = _dilated_mixture(q, k, v, rel_bias).astype(h.dtype)
    mem_out = _memory_attention(q_mem, mem_n, w_mem_kv)
    return jnp.concatenate([mixed, mem_out], axis=-1) @ w_out

def _deltanet_sublayer(h, mem_n, w_in, conv_w, a_log, dt_bias, out_norm, w_out, w_mem_kv):
    b, s, _ = h.shape
    qkv, z, gate_in, q_mem = jnp.split(
        h @ w_in, [3 * TOK_WIDTH, 4 * TOK_WIDTH, 4 * TOK_WIDTH + 4 * DN_HEADS], axis=-1)
    qkv = lax.conv_general_dilated(
        qkv, conv_w[:, None, :], window_strides=(1,), padding=[(DN_CONV // 2, DN_CONV // 2)],
        dimension_numbers=('NWC', 'WIO', 'NWC'), feature_group_count=3 * TOK_WIDTH)
    q, k, v = jnp.split(jax.nn.silu(qkv).astype(jnp.float32), 3, axis=-1)
    q = _l2norm(q.reshape(b, s, DN_HEADS, DN_HEAD_DIM)) * (DN_HEAD_DIM ** -0.5)
    k = _l2norm(k.reshape(b, s, DN_HEADS, DN_HEAD_DIM))
    v = v.reshape(b, s, DN_HEADS, DN_HEAD_DIM)
    gate_in = gate_in.astype(jnp.float32).reshape(b, s, 2, 2, DN_HEADS)
    g = -jnp.exp(a_log.astype(jnp.float32)) * jax.nn.softplus(gate_in[:, :, :, 0] + dt_bias.astype(jnp.float32))
    beta = jax.nn.sigmoid(gate_in[:, :, :, 1])
    o_fwd = _gated_delta_chunked(q, k, v, g[:, :, 0], beta[:, :, 0])
    rev = lambda t: jnp.flip(t, axis=1)
    o_bwd = rev(_gated_delta_chunked(rev(q), rev(k), rev(v), rev(g[:, :, 1]), rev(beta[:, :, 1])))
    o = o_fwd + o_bwd
    zf = z.astype(jnp.float32).reshape(b, s, DN_HEADS, DN_HEAD_DIM)
    o = (o * lax.rsqrt(jnp.mean(o * o, axis=-1, keepdims=True) + EPS)
         * out_norm.astype(jnp.float32) * jax.nn.silu(zf))
    o = o.reshape(b, s, TOK_WIDTH).astype(h.dtype)
    mem_out = _memory_attention(q_mem, mem_n, w_mem_kv)
    return jnp.concatenate([o, mem_out], axis=-1) @ w_out

def _swiglu(h, w_gate_up, w_down):
    gate, up = jnp.split(h @ w_gate_up, 2, axis=-1)
    return (jax.nn.silu(gate) * up) @ w_down

def second_inputs(seed: int = 0) -> dict:
    key = jax.random.key(seed)
    ks = jax.random.split(key, 24)
    n_att = (DEPTH_2 + N_MIXERS - 1) // N_MIXERS
    n_dn = DEPTH_2 // N_MIXERS

    def nrm(k, shape, scale):
        return jax.random.normal(k, shape, jnp.float32) * scale

    def gain(k, shape):
        return 1.0 + nrm(k, shape, 0.05)

    dt = jnp.exp(jax.random.uniform(ks[8], (n_dn, 2, DN_HEADS), jnp.float32,
                                    minval=math.log(1e-3), maxval=math.log(1e-1)))
    return {
        "x": nrm(ks[0], (BATCH, SEQ, D_MODEL), 1.0),
        "mem": nrm(ks[1], (BATCH, MEM_LEN, D_MODEL), 1.0),
        "rel_bias": nrm(ks[2], (REL_BUCKETS, ATT_HEADS), 0.5),
        "att_w_in": nrm(ks[3], (n_att, D_MODEL, ATT_IN), D_MODEL ** -0.5),
        "att_w_out": nrm(ks[4], (n_att, MIX_WIDTH, D_MODEL), MIX_WIDTH ** -0.5),
        "dn_w_in": nrm(ks[5], (n_dn, D_MODEL, DN_IN), D_MODEL ** -0.5),
        "dn_conv": nrm(ks[6], (n_dn, DN_CONV, 3 * TOK_WIDTH), DN_CONV ** -0.5),
        "dn_a_log": jnp.log(jax.random.uniform(ks[7], (n_dn, 2, DN_HEADS), jnp.float32, minval=1.0, maxval=16.0)),
        "dn_dt_bias": dt + jnp.log(-jnp.expm1(-dt)),
        "dn_out_norm": gain(ks[9], (n_dn, DN_HEAD_DIM)),
        "dn_w_out": nrm(ks[10], (n_dn, MIX_WIDTH, D_MODEL), MIX_WIDTH ** -0.5),
        "mem_norm": gain(ks[11], (DEPTH_2, D_MODEL)),
        "mem_w_kv": nrm(ks[12], (DEPTH_2, D_MODEL, 2 * MEM_WIDTH), D_MODEL ** -0.5),
        "norm_mix_pre": gain(ks[13], (DEPTH_2, D_MODEL)),
        "norm_mix_post": gain(ks[14], (DEPTH_2, D_MODEL)),
        "norm_ffn_pre": gain(ks[15], (DEPTH_2, D_MODEL)),
        "norm_ffn_post": gain(ks[16], (DEPTH_2, D_MODEL)),
        "ffn_w_gate_up": nrm(ks[17], (DEPTH_2, D_MODEL, 2 * D_FF_2), D_MODEL ** -0.5),
        "ffn_w_down": nrm(ks[18], (DEPTH_2, D_FF_2, D_MODEL), D_FF_2 ** -0.5),
    }

def second_block(x, mem, rel_bias, att_w_in, att_w_out, dn_w_in, dn_conv, dn_a_log, dn_dt_bias,
              dn_out_norm, dn_w_out, mem_norm, mem_w_kv, norm_mix_pre, norm_mix_post,
              norm_ffn_pre, norm_ffn_post, ffn_w_gate_up, ffn_w_down):
    for i in range(DEPTH_2):
        j = i // N_MIXERS
        h = _rms_norm(x, norm_mix_pre[i])
        mem_n = _rms_norm(mem, mem_norm[i])
        if i % N_MIXERS == 0:
            mixed = _attention_sublayer(h, mem_n, att_w_in[j], att_w_out[j], rel_bias, mem_w_kv[i])
        else:
            mixed = _deltanet_sublayer(h, mem_n, dn_w_in[j], dn_conv[j], dn_a_log[j], dn_dt_bias[j],
                                       dn_out_norm[j], dn_w_out[j], mem_w_kv[i])
        x = x + _rms_norm(mixed, norm_mix_post[i])
        h = _rms_norm(x, norm_ffn_pre[i])
        x = x + _rms_norm(_swiglu(h, ffn_w_gate_up[i], ffn_w_down[i]), norm_ffn_post[i])
    return x


def setup_inputs(seed=0):
    out = dict(first_inputs(seed))
    for name, value in second_inputs(seed + 1).items():
        if name != "x":
            out[name + "_2"] = value
    return out


def reference(
    x, c, positions, ada_w, ada_b, mix_pre_g, mix_post_g, ffn_pre_g, ffn_post_g, w_in,
    ssm_lam_re, ssm_lam_im, ssm_log_dt, ssm_b_re, ssm_b_im, ssm_c_re, ssm_c_im, ssm_d,
    ssm_w_glu, w_ssm_branch, w_attn_branch, w_out, router_w, router_b, w_gate, b_gate, w_up,
    b_up, w_down, b_down, mem_2, rel_bias_2, att_w_in_2, att_w_out_2, dn_w_in_2, dn_conv_2,
    dn_a_log_2, dn_dt_bias_2, dn_out_norm_2, dn_w_out_2, mem_norm_2, mem_w_kv_2, norm_mix_pre_2,
    norm_mix_post_2, norm_ffn_pre_2, norm_ffn_post_2, ffn_w_gate_up_2, ffn_w_down_2,
):
    x = first_block(
        x, c, positions, ada_w, ada_b, mix_pre_g, mix_post_g, ffn_pre_g, ffn_post_g, w_in,
        ssm_lam_re, ssm_lam_im, ssm_log_dt, ssm_b_re, ssm_b_im, ssm_c_re, ssm_c_im, ssm_d,
        ssm_w_glu, w_ssm_branch, w_attn_branch, w_out, router_w, router_b, w_gate, b_gate, w_up,
        b_up, w_down, b_down,
    )
    return second_block(
        x, mem_2, rel_bias_2, att_w_in_2, att_w_out_2, dn_w_in_2, dn_conv_2, dn_a_log_2,
        dn_dt_bias_2, dn_out_norm_2, dn_w_out_2, mem_norm_2, mem_w_kv_2, norm_mix_pre_2,
        norm_mix_post_2, norm_ffn_pre_2, norm_ffn_post_2, ffn_w_gate_up_2, ffn_w_down_2,
    )


_drawn_inputs = setup_inputs


def setup_inputs(seed=0):
    import zlib

    import numpy as np

    out = dict(_drawn_inputs(seed))
    spreads = {}
    factors = {'ssm_lam_re': 64.0,
     'b_gate': 8.0,
     'b_up': 8.0,
     'b_down': 8.0,
     'ssm_b_re': 2.752,
     'ssm_c_re': 5.182,
     'ssm_c_im': 3.054}
    for name, (base, spread) in spreads.items():
        noise = np.random.default_rng([zlib.crc32(name.encode()), seed]).standard_normal(out[name].shape)
        drawn = base * np.exp(spread * noise) if base else spread * noise
        out[name] = jnp.asarray(drawn.astype(out[name].dtype))
    for name, factor in factors.items():
        out[name] = (out[name] * factor).astype(out[name].dtype)
    return out
```

```python
from contextlib import ExitStack

import numpy as np
import concourse.bass as bass
from concourse import mybir

P = 128
D = 1024
SEQ = 256
TT = SEQ // P
KD = D // P
EPS = 1e-6
NEG = -1e30
HEADS, HD = 8, 64
AW = HEADS * HD
SSM_G, SSM_C, SSM_P = 32, 16, 64
SW = SSM_G * SSM_C
SJ = SSM_G * SSM_P // P
SQ = SW // P
E, TOPK, CAP = 32, 4, 64
ROUNDS = SEQ // CAP
FF = 1024
ALPHA, LIMIT = 1.702, 7.0
TW, MW = 768, 256
GROUPS = ((128, 1), (512, 4), (2048, 16))
ATT_HEADS, HPG = 12, 4
BUCKETS, MAX_DIST = 32, 1024
DH = 6
DD = 128
TAPS = 5
FF2 = 2816
FC2 = FF2 // P
TWO_PI = 6.2831845
SLOTS, SLOT_W = 6, 4096


def shape_constants():
    i = np.arange(P)
    c = {}
    c["ident"] = np.eye(P)
    c["ones"] = np.ones((P, P))
    c["upto"] = (i[:, None] <= i[None, :])
    c["from"] = (i[:, None] >= i[None, :])
    c["before"] = (i[:, None] < i[None, :])
    c["slots"] = np.tile(np.arange(SEQ).reshape(ROUNDS, 1, CAP), (1, 2, 1)).reshape(1, -1).repeat(P, 0)
    c["steps"] = np.arange(SEQ)[None, :].repeat(P, 0)
    c["experts"] = np.arange(E)[None, :].repeat(P, 0)
    rot = np.zeros((P, P))
    for b in range(0, P, HD):
        for d in range(HD // 2):
            rot[b + d + HD // 2, b + d] = -1.0
            rot[b + d, b + d + HD // 2] = 1.0
    c["rot"] = rot
    c["zero_rows"] = np.zeros((P, P))
    c["flip"] = np.eye(P)[::-1] * HD ** 0.5
    half = HD // 2
    inv = (np.float32(10000.0) ** (-np.arange(half, dtype=np.float32) / np.float32(half))).astype(np.float32)
    c["inv_freq"] = inv[i % half][:, None]
    causal = np.where(np.arange(SEQ)[None, None, :] <= (i[:, None, None] + P * np.arange(TT)[None, :, None]), 0.0, NEG)
    c["causal"] = causal.reshape(P, -1)
    c["mask_b"] = ((i // SSM_P)[:, None] == (np.arange(2 * SSM_C) // SSM_C)[None, :])
    c["mask_c"] = (((i // SSM_C) % 2)[:, None] == (np.arange(P) // SSM_P)[None, :])
    names, cols, at = {}, [], 0
    for k, v in c.items():
        v = np.asarray(v, np.float32)
        names[k] = (at, v.shape[1])
        at += v.shape[1]
        cols.append(v)
    main = np.ascontiguousarray(np.concatenate(cols, 1))
    lev = []
    for n in range(7):
        b = 1 << n
        m = (i[:, None] // (2 * b) == i[None, :] // (2 * b)) & ((i[:, None] // b) % 2 == 1) & ((i[None, :] // b) % 2 == 0)
        lev.append(np.stack([m, m.T], 1))
    levels = np.stack(lev, 1).astype(np.float32).reshape(P, -1)
    rel = np.arange(SEQ - 1, -SEQ, -1) * -1
    hot = np.zeros((BUCKETS + 1, len(GROUPS), 2 * SEQ), np.float32)
    for g, (window, dil) in enumerate(GROUPS):
        h = window // (2 * dil)
        n = np.abs(rel)
        hb = BUCKETS // 2
        me = hb // 2
        large = me + (np.log(np.maximum(n, 1) / me) / np.log(MAX_DIST / me) * (hb - me)).astype(np.int64)
        bucket = (rel > 0) * hb + np.where(n < me, n, np.minimum(large, hb - 1))
        ok = (rel % dil == 0) & (np.abs(rel // dil) <= h)
        for r in range(len(rel)):
            hot[bucket[r] if ok[r] else BUCKETS, g, r] = 1.0
        hot[BUCKETS, g, len(rel)] = 1.0
    return main, names, levels, hot.reshape(BUCKETS + 1, -1)


def paired(w):
    n, d, f2 = w.shape
    return np.ascontiguousarray(w.reshape(n, d, 2, f2 // 512, 256).transpose(0, 1, 3, 2, 4)).reshape(n, d, f2)


def block_kernel(nc, A, out, names):
    f32, i32, u32 = mybir.dt.float32, mybir.dt.int32, mybir.dt.uint32
    ALU, ACT, AX = mybir.AluOpType, mybir.ActivationFunctionType, mybir.AxisListType
    ctx = ExitStack()

    def sem(name):
        return ctx.enter_context(nc.semaphore(name))

    def sb(name, cols, dt=f32, parts=P):
        return ctx.enter_context(nc.sbuf_tensor(name, [parts, cols], dt))

    def spread(ap, *dims):
        return bass.AP(ap.tensor, ap.offset, [list(ap.ap[0])] + [list(d) for d in dims])

    def cols_bc(ap, n):
        return bass.AP(ap.tensor, ap.offset, [list(d) for d in ap.ap] + [[0, n]])

    def rows_bc(ap, n):
        return bass.AP(ap.tensor, ap.offset, [list(ap.ap[0]), [0, n]] + [list(d) for d in ap.ap[1:]])

    class Ordered:

        def __init__(self, eng, own):
            self.eng, self.own, self.n, self.told, self.base = eng, own, 0, {}, None

        def __call__(self, ins, tells=None):
            if tells is None:
                self.n += 1
                ins.then_inc(self.own, 1)
                self.eng.wait_ge(self.own, self.n if self.base is None else self.base + self.n)
            else:
                self.told[tells.name] = self.told.get(tells.name, 0) + 1
                ins.then_inc(tells, 1)
                if self.base is None:
                    self.eng.wait_ge(tells, self.told[tells.name])

    with ctx:
        CON = sb("constants", A["k_main"].shape[1])
        X = sb("x_res", TT * D)
        RING = sb("ring", SLOTS * SLOT_W)
        AR = sb("arena", 22600)
        SM = sb("smalls", 1280)
        x3 = X[:, :].rearrange("p (t d) -> p t d", t=TT)
        PS = ctx.enter_context(nc.psum_tensor("ps", [P, 4096], f32))

        def con(name, rows=P):
            a, n = names[name]
            return CON[0:rows, a:a + n]

        def bank(b, n=1, rows=P):
            return PS[0:rows, b * 512:(b + n) * 512]

        def ar(at, n, rows=P):
            return AR[0:rows, at:at + n]

        def sm(at, n, rows=P):
            return SM[0:rows, at:at + n]

        ident = con("ident")

        slot_ready = [sem(f"slot_ready{i}") for i in range(SLOTS)]
        pieces = []

        def piece(src, used, count):
            pieces.append((src, used, count))
            n = len(pieces) - 1
            shape = [s for s in src.shape][1:]
            w = int(np.prod(shape))
            v = RING[:, (n % SLOTS) * SLOT_W:(n % SLOTS) * SLOT_W + w]
            if len(shape) > 1:
                v = v.rearrange("p (k n) -> p k n", k=shape[0])
            return n, v

        def arrived(pe, pc):
            pe.wait_ge(slot_ready[pc[0] % SLOTS], 16 * (pc[0] // SLOTS + 1))
            return pc[1]

        def by_k(w, c0, c1):
            return w[:, c0:c1].rearrange("(k p) n -> p k n", p=P)

        ada_w = A["ada_w"][0]
        w_in = A["w_in"][0]


        (act_order, dve_order) = (sem(n) for n in (
            "act_order", "dve_order"))
        x_in, con_in, mod_in, ssm_in, rope_in = (sem(n) for n in ("x_in", "con_in", "mod_in", "ssm_in", "rope_in"))
        cond_silu, cond_ready, ada_ps = sem("cond_silu"), sem("cond_ready"), sem("ada_ps")
        bc_ready, bc_ps, bc_ev = sem("bc_ready"), sem("bc_ps"), sem("bc_ev")
        par_in, par_exp, par_red, par_trig = sem("par_in"), sem("par_exp"), sem("par_red"), sem("par_trig")
        ph_ready, tab_ready, rope_red, rope_tab = sem("ph_ready"), sem("tab_ready"), sem("rope_red"), sem("rope_tab")
        sq_done, ms_done, rt_done = sem("sq_done"), sem("ms_done"), sem("rt_done")
        (proj_ps, rot_ps, rope_done) = (sem(n) for n in (
            "proj_ps", "rot_ps", "rope_done"))
        sc_ps, sc_read, sc_sub, sc_exp, pr_ready, prT_ps, prT_ready, pv_ps, pv_ev = (sem(n) for n in (
            "sc_ps", "sc_read", "sc_sub", "sc_exp", "pr_ready", "prT_ps", "prT_ready", "pv_ps", "pv_ev"))
        bu_ps, bu_read, st_ready, y_ps, y_ready, gel_ready = (
            sem(n) for n in ("bu_ps", "bu_read", "st_ready", "y_ps", "y_ready", "gel_ready"))
        ys_ready = sem("ys_ready")
        (gate_ready, x1_ready) = (sem(n) for n in (
            "gate_ready", "x1_ready"))

        (turn_ps, turned, nat_ready, fn_asked, fn_done, proj_ev, out_ps, router_ps) = (sem(n) for n in (
            "turn_ps", "turned", "nat_ready", "fn_asked", "fn_done", "proj_ev", "out_ps", "router_ps"))
        pc_ada = [piece(by_k(ada_w, n * 512, n * 512 + 512), ada_ps, n + 1) for n in range(6)]
        pc_in = [piece(by_k(w_in, n * 512, n * 512 + 512), proj_ps, n + 1) for n in range(4)]
        pc_gate = [piece(by_k(w_in, (4 + n) * 512, (5 + n) * 512), proj_ps, 4 + n + 1) for n in range(4)]
        pc_glu = piece(by_k(A["ssm_w_glu"][0], 0, SW), out_ps, 1)
        pc_ws = piece(by_k(A["w_ssm_branch"][0], 0, D), out_ps, 2)
        pc_wa = piece(by_k(A["w_attn_branch"][0], 0, D), out_ps, 3)
        pc_out = [piece(by_k(A["w_out"][0], n * 512, n * 512 + 512), out_ps, 3 + n + 1) for n in range(2)]

        def ar3(at, n, k):
            return ar(at, n).rearrange("p (k m) -> p k m", k=k)

        shm, Am, GTm = ar(0, D), ar(D, D), ar(2 * D, D)
        condrep = ar3(3072, 1024, KD)
        gpre, gpost = ar(4096, D), ar(5120, D)
        h_nat = ar3(4096, 2048, TT)
        hT = ar3(6144, 2048, KD)
        uT, qT, kT = ar3(8192, 1024, 4), ar3(9216, 1024, 4), ar3(20480, 1024, 4)
        vN = ar3(21504, 1024, TT)
        cosS, sinS = ar3(10240, 4096, SJ), ar3(14336, 4096, SJ)
        BTr, BTi, CTr, CTi = (ar3(18432 + 512 * n, 512, SQ) for n in range(4))
        braw = [ar3(10240 + 256 * n, 256, SJ) for n in range(2)]
        bbar = [ar3(10752 + 256 * n, 256, SJ) for n in range(2)]
        craw = [ar3(11264 + 256 * n, 256, SQ) for n in range(2)]
        btmp = ar3(11776, 256, SJ)
        Bd = [ar(12288 + 512 * n, 512) for n in range(2)]
        Cd = [ar(13312 + 512 * n, 512) for n in range(2)]
        BC = [BTr, BTi, CTr, CTi]
        ph_t, ph_n, ph_f = ar(6144, 2048), ar(8192, 2048), ar(20480, 2048)
        qraw, kraw = ar(0, 1024), ar(1024, 1024)
        rtmp = ar3(4096, 1024, 4)
        prob = [ar(4096, 1024), ar(5120, 1024)]
        prT = [ar(0, 1024), ar(1024, 1024)]
        yaT = ar3(3072, 1024, 4)
        sA, sB, sT, sU = ar3(0, 1024, 4), ar3(1024, 1024, 4), ar3(4096, 1024, 4), ar3(5120, 1024, 4)
        yT = ar3(9216, 1024, SQ)
        sgs, sga = ar3(20480, 2048, TT), ar3(14336, 2048, TT)
        gel, sglu, ysT = ar3(10240, 1024, SQ), ar3(11264, 1024, SQ), ar3(12288, 1024, SQ)
        mgd, mtmp = ar3(16384, 2048, TT), ar(18432, 1024)
        mgT = ar3(6144, 2048, KD)

        c_col, cond = sm(0, KD), sm(8, KD)
        (lam_re, lam_im, dt_c, mag, th, frq, tc, lbr, lbi, cr, ci, den, fhi, flo) = (sm(16 + 16 * n, SJ) for n in range(14))
        dcol, ssq, rms = sm(256, SQ), sm(260, TT), sm(262, TT)
        cosR, sinR = sm(320, SEQ), sm(576, SEQ)
        tc2, intc = sm(832, SJ), sm(848, SJ)
        amax, aden = sm(864, HPG), sm(868, HPG)

        def dma(eng, dst, src, s):
            eng.dma_start(dst, src, allow_slow_non_contiguous=True).then_inc(s, 16)

        def row(ap1):
            return bass.AP(ap1.tensor, ap1.offset, [[0, P]] + [list(d) for d in ap1.ap])

        def stream(sp, first, last):
            for n in range(first, last):
                if n >= SLOTS:
                    sp.wait_ge(pieces[n - SLOTS][1], pieces[n - SLOTS][2])
                src = pieces[n][0]
                shape = list(src.shape)[1:]
                v = RING[:, (n % SLOTS) * SLOT_W:(n % SLOTS) * SLOT_W + int(np.prod(shape))]
                if len(shape) > 1:
                    v = v.rearrange("p (k n) -> p k n", k=shape[0])
                sp.dma_start(v, src).then_inc(slot_ready[n % SLOTS], 16)

        def pool_s0(pool):
            dma(pool, c_col, A["c"].rearrange("a (k p) -> p (a k)", p=P), mod_in)
            dma(pool, CON[:, :], A["k_main"], con_in)
            dma(pool, X[:, :].rearrange("p (t d) -> p t d", t=TT), A["x"][0].rearrange("(t p) d -> p t d", p=P), x_in)
            for s, a in ((lam_re, "ssm_lam_re"), (lam_im, "ssm_lam_im")):
                dma(pool, s, A[a][0].rearrange("(j g) s -> (g s) j", g=2), par_in)
            for g in range(2):
                src = A["ssm_log_dt"][0]
                dma(pool, dt_c[g * SSM_P:(g + 1) * SSM_P, :],
                    bass.AP(src.tensor, src.offset + g, [[0, SSM_P], [2, SJ]]), par_in)
            for n, a in enumerate(("ssm_b_re", "ssm_b_im")):
                dma(pool, braw[n], A[a][0].rearrange("(j g) s c -> (g s) j c", g=2), ssm_in)
            for n, a in enumerate(("ssm_c_re", "ssm_c_im")):
                dma(pool, craw[n], A[a][0].rearrange("(q r) c s -> (r c) q s", q=SQ), ssm_in)
            dma(pool, dcol, A["ssm_d"][0].rearrange("(q p) -> p q", p=P), ssm_in)
            for n, d in enumerate((shm, Am, GTm)):
                dma(pool, d, row(A["ada_b"][0][n * D:(n + 1) * D]), mod_in)
            dma(pool, gpre, row(A["mix_pre_g"][0]), mod_in)
            dma(pool, gpost, row(A["mix_post_g"][0]), mod_in)
            dma(pool, sinR.bitcast(i32), row(A["positions"][0]), rope_in)

        def act_s0(act, o):
            act.wait_ge(mod_in, 16 * 6)
            o(act.activation(cond, c_col, ACT.Silu), cond_silu)
            act.wait_ge(par_in, 16 * 4)
            o(act.activation(dt_c, dt_c, ACT.Exp), par_exp)
            act.wait_ge(par_red, 1)
            o(act.activation(mag, mag, ACT.Exp), par_exp)
            act.wait_ge(par_red, 2)
            o(act.activation(lbi, frq, ACT.Sin, scale=TWO_PI))
            o(act.activation(lbr, tc, ACT.Sin, scale=TWO_PI), par_trig)
            act.wait_ge(rope_red, 1)
            o(act.activation(cosR, cosR, ACT.Sin))
            o(act.activation(sinR, sinR, ACT.Sin), rope_tab)
            for n in range(4):
                act.wait_ge(bc_ps, n + 1)
                o(act.copy(BC[n], bank(6 + n % 2).rearrange("p (q m) -> p q m", q=SQ)), bc_ev)
            for h in range(2):
                act.wait_ge(ph_ready, h + 1)
                o(act.activation(sinS[:, 8 * h:8 * h + 8, :], ph_f.rearrange("p (j s) -> p j s", j=8), ACT.Sin, scale=TWO_PI))
                o(act.activation(cosS[:, 8 * h:8 * h + 8, :], ph_t.rearrange("p (j s) -> p j s", j=8), ACT.Sin, scale=TWO_PI), tab_ready)

        def turn(dve, o, x, n_int, n_f):
            o(dve.tensor_copy(n_int, x))
            o(dve.tensor_copy(n_f, n_int))
            return dve.tensor_tensor(x, x, n_f, ALU.subtract)

        def quarter_on(dve, o, outp, x, tmp):
            o(dve.tensor_scalar(tmp, x, 0.25, None, ALU.is_gt))
            return dve.scalar_tensor_tensor(outp, x, 0.25, tmp, ALU.add, ALU.subtract)

        def dve_s0(dve, o):
            dve.wait_ge(cond_silu, 1)
            o(dve.tensor_copy(condrep, cols_bc(cond, P)), cond_ready)
            dve.wait_ge(rope_in, 16)
            dve.wait_ge(con_in, 16)
            o(dve.tensor_copy(cosR, sinR.bitcast(i32)))
            o(dve.tensor_scalar(sinR, cosR, con("inv_freq"), None, ALU.mult))
            turns, whole = ph_t[:, 0:SEQ], ph_n[:, 0:SEQ]
            o(dve.tensor_scalar(turns, sinR, float(1 / (2 * np.pi)), None, ALU.mult))
            o(dve.tensor_copy(whole.bitcast(i32), turns))
            o(dve.tensor_copy(turns, whole.bitcast(i32)))
            o(dve.scalar_tensor_tensor(sinR, turns, -6.28125, sinR, ALU.mult, ALU.add))
            o(dve.scalar_tensor_tensor(sinR, turns, float(-(2 * np.pi - 6.28125)), sinR, ALU.mult, ALU.add))
            o(dve.tensor_scalar(whole, sinR, float(np.pi / 2), float(-2 * np.pi), ALU.is_gt, ALU.mult))
            o(dve.scalar_tensor_tensor(cosR, sinR, float(np.pi / 2), whole, ALU.add, ALU.add))
            for r in (sinR, cosR):
                last = dve.tensor_scalar(r, r, 3.1415925, -3.1415925, ALU.min, ALU.max)
                o(last, rope_red if r is cosR else None)
            dve.wait_ge(par_exp, 1)
            o(dve.tensor_tensor(mag, lam_re, dt_c, ALU.mult), par_red)
            o(dve.tensor_tensor(th, lam_im, dt_c, ALU.mult))
            o(dve.tensor_scalar(frq, th, float(1 / (2 * np.pi)), None, ALU.mult))
            o(turn(dve, o, frq, intc.bitcast(i32), tc2))
            o(quarter_on(dve, o, tc, frq, tc2), par_red)
            o(dve.tensor_scalar(tc2, frq, 4096.0, None, ALU.mult))
            o(dve.tensor_copy(intc.bitcast(i32), tc2))
            o(dve.tensor_copy(tc2, intc.bitcast(i32)))
            o(dve.tensor_scalar(fhi, tc2, 1.0 / 4096, None, ALU.mult))
            o(dve.tensor_tensor(flo, frq, fhi, ALU.subtract))
            dve.wait_ge(par_exp, 2)
            dve.wait_ge(par_trig, 1)
            o(dve.tensor_tensor(lbr, lbr, mag, ALU.mult))
            o(dve.tensor_tensor(lbi, lbi, mag, ALU.mult))
            o(dve.tensor_scalar(lbr, lbr, -1.0, None, ALU.add))
            o(dve.tensor_tensor(den, lam_re, lam_re, ALU.mult))
            o(dve.tensor_tensor(tc2, lam_im, lam_im, ALU.mult))
            o(dve.tensor_tensor(den, den, tc2, ALU.add))
            o(dve.reciprocal(den, den))
            o(dve.tensor_tensor(cr, lbr, lam_re, ALU.mult))
            o(dve.tensor_tensor(tc2, lbi, lam_im, ALU.mult))
            o(dve.tensor_tensor(cr, cr, tc2, ALU.add))
            o(dve.tensor_tensor(cr, cr, den, ALU.mult))
            o(dve.tensor_tensor(ci, lbi, lam_re, ALU.mult))
            o(dve.tensor_tensor(tc2, lbr, lam_im, ALU.mult))
            o(dve.tensor_tensor(ci, ci, tc2, ALU.subtract))
            o(dve.tensor_tensor(ci, ci, den, ALU.mult))
            dve.wait_ge(ssm_in, 16 * 5)
            crb, cib = cols_bc(cr, SSM_C), cols_bc(ci, SSM_C)
            o(dve.tensor_tensor(bbar[0], braw[0], crb, ALU.mult))
            o(dve.tensor_tensor(btmp, braw[1], cib, ALU.mult))
            o(dve.tensor_tensor(bbar[0], bbar[0], btmp, ALU.subtract))
            o(dve.tensor_tensor(bbar[1], braw[1], crb, ALU.mult))
            o(dve.tensor_tensor(btmp, braw[0], cib, ALU.mult))
            o(dve.tensor_tensor(bbar[1], bbar[1], btmp, ALU.add))
            mb = spread(con("mask_b"), [0, SJ], [SSM_C, 2], [1, SSM_C])
            mc = spread(con("mask_c"), [0, SQ], [SSM_P, 2], [1, SSM_P])
            for n in range(2):
                o(dve.tensor_tensor(Bd[n].rearrange("p (j g c) -> p j g c", g=2, c=SSM_C),
                                    spread(bbar[n], [SSM_C, SJ], [0, 2], [1, SSM_C]), mb, ALU.mult), bc_ready)
            for n in range(2):
                o(dve.tensor_tensor(Cd[n].rearrange("p (q g s) -> p q g s", g=2, s=SSM_P),
                                    spread(craw[n], [SSM_P, SQ], [0, 2], [1, SSM_P]), mc, ALU.mult), bc_ready)
            for h in range(2):
                if h == 0:
                    dve.wait_ge(bc_ps, 4)
                else:
                    dve.wait_ge(tab_ready, 1)
                steps = spread(con("steps"), [0, 8], [1, SEQ])
                f3, t3 = ph_f.rearrange("p (j s) -> p j s", j=8), ph_t.rearrange("p (j s) -> p j s", j=8)
                o(dve.tensor_tensor(f3, steps, cols_bc(fhi[:, 8 * h:8 * h + 8], SEQ), ALU.mult))
                o(turn(dve, o, ph_f, ph_n.bitcast(i32), ph_t))
                o(dve.tensor_tensor(t3, steps, cols_bc(flo[:, 8 * h:8 * h + 8], SEQ), ALU.mult))
                o(dve.tensor_tensor(ph_f, ph_f, ph_t, ALU.add))
                o(turn(dve, o, ph_f, ph_n.bitcast(i32), ph_t))
                o(quarter_on(dve, o, ph_t, ph_f, ph_n), ph_ready)
            dve.wait_ge(mod_in, 16 * 6)
            dve.wait_ge(ada_ps, 6)
            o(dve.tensor_tensor(shm, shm, bank(0, 2), ALU.add))
            o(dve.scalar_tensor_tensor(Am, bank(2, 2), 1.0, Am, ALU.add, ALU.add))
            o(dve.tensor_tensor(Am, Am, gpre, ALU.mult))
            o(dve.tensor_tensor(GTm, GTm, bank(4, 2), ALU.add))
            o(dve.tensor_tensor(GTm, GTm, gpost, ALU.mult))

        def pe_ada(pe, pcs, base):
            for n, pc in enumerate(pcs):
                w = arrived(pe, pc)
                for k in range(KD):
                    m = pe.matmul(bank(base + n), condrep[:, k, :], w[:, k, :], start=(k == 0), stop=(k == KD - 1))
                m.then_inc(ada_ps, 1)

        def pe_s0(pe):
            pe.wait_ge(cond_ready, 1)
            pe_ada(pe, pc_ada, 0)
            for n in range(4):
                pe.wait_ge(bc_ready, n + 1)
                if n >= 2:
                    pe.wait_ge(bc_ev, n - 1)
                src = (Bd + Cd)[n]
                for q in range(SQ):
                    m = pe.transpose(bank(6 + n % 2)[:, q * P:(q + 1) * P], src[:, q * P:(q + 1) * P], ident)
                m.then_inc(bc_ps, 1)

        norms = [0]

        def act_rms(act, o, srcs, junk, n):
            for t in range(TT):
                o(act.activation(junk, srcs[t], ACT.Square, accum_out=ssq[:, t:t + 1]), sq_done if t == TT - 1 else None)
            act.wait_ge(ms_done, n)
            o(act.activation(rms, rms, ACT.Sqrt), rt_done)

        def dve_rms(dve, o, n, width=D):
            dve.wait_ge(sq_done, n)
            o(dve.tensor_scalar(rms, ssq, 1.0 / width, EPS, ALU.mult, ALU.add), ms_done)
            dve.wait_ge(rt_done, n)
            o(dve.reciprocal(rms, rms))

        TURNS = ("mixer", "merged", "experts", "memory0", "attention", "ffn0", "memory1", "delta", "ffn1")
        NT, QT, OT = 9, 6, 3

        def turn_base(which):
            return 4 * TURNS.index(which) + (NT + QT + OT if which == "ffn1" else 0)

        D_BASE = 4 * (TURNS.index("delta") + 1)

        def pe_turn(pe, src3, which):
            for t in range(TT):
                pe.wait_ge(nat_ready, TT * TURNS.index(which) + t + 1)
                for b in range(2):
                    for k in range(4):
                        kk = 4 * b + k
                        m = pe.transpose(bank(2 * t + b)[:, k * P:(k + 1) * P], src3[:, t, kk * P:(kk + 1) * P], ident)
                    m.then_inc(turn_ps, 1)

        def act_turned(act, o, dst3, which):
            for t in range(TT):
                for b in range(2):
                    act.wait_ge(turn_ps, turn_base(which) + 2 * t + b + 1)
                    o(act.copy(dst3[:, 4 * b:4 * b + 4, t * P:(t + 1) * P],
                               bank(2 * t + b).rearrange("p (k m) -> p k m", k=4)), turned)

        def pe_after_turn(pe, which):
            pe.wait_ge(turned, turn_base(which) + 4)

        def act_s1(act, o):
            act.wait_ge(x_in, 16)
            act_rms(act, o, [x3[:, t, :] for t in range(TT)], hT[:, 0:4, :].rearrange("p k m -> p (k m)"), 1)
            act_turned(act, o, hT, "mixer")

        def dve_s1(dve, o):
            dve_rms(dve, o, 1)
            for t in range(TT):
                o(dve.scalar_tensor_tensor(h_nat[:, t, :], x3[:, t, :], rms[:, t:t + 1], Am, ALU.mult, ALU.mult))
                o(dve.tensor_tensor(h_nat[:, t, :], h_nat[:, t, :], shm, ALU.add), nat_ready)

        def pe_s1(pe):
            pe_turn(pe, h_nat, "mixer")

        def pe_cols(pe, w, b0, src3, kn, done):
            for c in range(4):
                for k in range(kn):
                    m = pe.matmul(bank(b0 + c // 2)[:, (c % 2) * SEQ:(c % 2 + 1) * SEQ], w[:, k, c * P:(c + 1) * P],
                                  src3[:, k, :], start=(k == 0), stop=(k == kn - 1))
            m.then_inc(done, 1)

        def pe_rows(pe, w, banks, src3, kn, done):
            for t in range(TT):
                for k in range(kn):
                    m = pe.matmul(bank(banks[t]), src3[:, k, t * P:(t + 1) * P], w[:, k, :], start=(k == 0), stop=(k == kn - 1))
            m.then_inc(done, 1)

        def pe_s2(pe):
            pe_after_turn(pe, "mixer")
            pe.wait_ge(bc_ev, 4)
            pe_cols(pe, arrived(pe, pc_in[0]), 4, hT, KD, proj_ps)
            pe_cols(pe, arrived(pe, pc_in[1]), 6, hT, KD, proj_ps)
            pe_cols(pe, arrived(pe, pc_in[2]), 0, hT, KD, proj_ps)
            pe_rows(pe, arrived(pe, pc_in[3]), (2, 3), hT, KD, proj_ps)
            for n, raw in enumerate((qraw, kraw)):
                pe.wait_ge(proj_ev, n + 2)
                for b in range(2):
                    m = pe.matmul(bank(4 + 2 * n + b), con("rot"), raw[:, b * 512:(b + 1) * 512], start=True, stop=True)
                m.then_inc(rot_ps, 1)

        def act_s2(act, o):
            act.wait_ge(proj_ps, 1)
            o(act.copy(uT.rearrange("p c s -> p (c s)"), bank(4, 2)), proj_ev)
            for n, raw in enumerate((qraw, kraw)):
                act.wait_ge(proj_ps, 2 + n)
                o(act.copy(raw, bank(6 if n == 0 else 0, 2)), proj_ev)
            act.wait_ge(proj_ps, 4)
            o(act.copy(vN.rearrange("p t n -> p (t n)"), bank(2, 2)), proj_ev)

        def dve_s2(dve, o):
            dve.wait_ge(rope_tab, 1)
            for n, (raw, dst) in enumerate(((qraw, qT), (kraw, kT))):
                dve.wait_ge(rot_ps, n + 1)
                o(dve.tensor_tensor(dst, raw.rearrange("p (c s) -> p c s", c=4), rows_bc(cosR, 4), ALU.mult))
                o(dve.tensor_tensor(rtmp, bank(4 + 2 * n, 2).rearrange("p (c s) -> p c s", c=4), rows_bc(sinR, 4), ALU.mult))
                o(dve.tensor_tensor(dst, dst, rtmp, ALU.add), rope_done)

        def at(i):
            return (i % 2) * 2 + i // 2

        def probs_of(n):
            return prob3[(n - 4) % 3] if 4 <= n < 10 else prob[n % 2]

        def pe_scores(pe, u, q_of, k_of, bias=None):
            if bias is not None:
                for a in range(2):
                    pe.matmul(bank(2 * (u % 2) + a), con("flip"), bias[:, 2 * a:2 * a + 2, :], start=True, stop=False, skip_group_check=True)
            for i in range(HPG):
                m = pe.matmul(bank(2 * (u % 2) + i % 2)[:, (i // 2) * SEQ:(i // 2 + 1) * SEQ], q_of(i), k_of(i), start=bias is None, stop=True,
                              skip_group_check=bias is not None)
            m.then_inc(sc_ps, 1)

        def pe_probs(pe, u, n, v_of):
            pe.wait_ge(pr_ready, n + 1)
            if n:
                pe.wait_ge(prT_ready, n)
            for kb in range(2):
                for i in range(HPG):
                    m = pe.transpose(bank(4 + kb)[:, i * P:(i + 1) * P], probs_of(n)[:, at(i) * SEQ + kb * P:at(i) * SEQ + (kb + 1) * P], ident)
            m.then_inc(prT_ps, 1)
            pe.wait_ge(prT_ready, n + 1)
            if n >= 2:
                pe.wait_ge(pv_ev, n - 1)
            for i in range(HPG):
                for kb in range(2):
                    r = HD * (i % 2)
                    m = pe.matmul(bank(6 + n % 2)[r:r + HD, (i // 2) * P:(i // 2 + 1) * P], v_of(kb, i),
                                  prT[n % 2][:, kb * 512 + i * P:kb * 512 + (i + 1) * P], start=(kb == 0), stop=(kb == 1))
            m.then_inc(pv_ps, 1)

        def dve_softmax(dve, o, u, n, scale, bias, weigh=None):
            S = probs_of(n)
            s3 = S.rearrange("p (h k) -> p h k", h=HPG)
            dve.wait_ge(sc_ps, n + 1)
            if n >= 2:
                dve.wait_ge(prT_ps, n - 1)
            if bias is None:
                o(dve.tensor_scalar(S, bank(2 * (n % 2), 2), scale, None, ALU.mult), sc_read)
            else:
                o(dve.scalar_tensor_tensor(s3, bank(2 * (n % 2), 2).rearrange("p (h k) -> p h k", h=HPG), scale, bias,
                                           ALU.mult, ALU.add), sc_read)
            o(dve.tensor_reduce(amax, s3, AX.X, ALU.max))
            o(dve.tensor_tensor(s3, s3, cols_bc(amax, SEQ), ALU.subtract), sc_sub)
            dve.wait_ge(sc_exp, n + 1)
            o(dve.tensor_reduce(aden, s3, AX.X, ALU.add))
            o(dve.reciprocal(aden, aden))
            if weigh is not None:
                weigh()
            o(dve.tensor_tensor(s3, s3, cols_bc(aden, SEQ), ALU.mult), pr_ready)

        def dve_pv(dve, o, u, n, dst):
            dve.wait_ge(pv_ps, n + 1)
            o(dve.tensor_copy(dst, bank(6 + n % 2)[:, 0:SEQ].rearrange("p (c m) -> p c m", c=2)), pv_ev)

        def act_probs(act, o, u, n):
            act.wait_ge(sc_sub, n + 1)
            o(act.activation(probs_of(n), probs_of(n), ACT.Exp), sc_exp)
            act_probsT(act, o, n)

        def act_probsT(act, o, n):
            act.wait_ge(prT_ps, n + 1)
            if n >= 2:
                act.wait_ge(pv_ps, n - 1)
            o(act.copy(prT[n % 2], bank(4, 2)), prT_ready)

        U1 = [(g, t) for g in range(HEADS // HPG) for t in range(TT)]

        def pe_s4(pe):
            def scores(u):
                g, t = U1[u]
                pe.wait_ge(rope_done, 2)
                if u == 1:
                    pe.wait_ge(proj_ev, 4)
                if u >= 2:
                    pe.wait_ge(sc_read, u - 1)
                def half(x, i):
                    return x[HD * (i % 2):HD * (i % 2) + HD, 2 * g + i // 2, :]
                pe_scores(pe, u, lambda i: half(qT, i)[:, t * P:(t + 1) * P], lambda i: half(kT, i))
            scores(0)
            for u, (g, t) in enumerate(U1):
                if u + 1 < len(U1):
                    scores(u + 1)
                pe_probs(pe, u, u, lambda kb, i: vN[:, kb, (HPG * g + i) * HD:(HPG * g + i + 1) * HD])

        def act_s4(act, o):
            for u in range(len(U1)):
                act_probs(act, o, u, u)

        def dve_s4(dve, o):
            for u, (g, t) in enumerate(U1):
                causal = spread(con("causal")[:, t * SEQ:(t + 1) * SEQ], [0, HPG], [1, SEQ])
                dve_softmax(dve, o, u, u, HD ** -0.5, causal)
                if u:
                    g0, t0 = U1[u - 1]
                    dve_pv(dve, o, u - 1, u - 1, yaT[:, 2 * g0:2 * g0 + 2, t0 * P:(t0 + 1) * P])
            dve_pv(dve, o, u, u, yaT[:, 2 * g:2 * g + 2, t * P:(t + 1) * P])

        def pe_s3(pe):
            def drive(q):
                if q:
                    pe.wait_ge(bu_read, q)
                for n, m_ in enumerate((BTr, BTi)):
                    for j in range(4):
                        m = pe.matmul(bank(j)[:, n * SEQ:(n + 1) * SEQ], m_[32 * j:32 * j + 32, q, :],
                                      uT[32 * j:32 * j + 32, q, :], start=True, stop=True, tile_position=(32 * j, 0))
                m.then_inc(bu_ps, 1)
            pe.wait_ge(sc_read, len(U1))
            pe.wait_ge(pv_ev, len(U1))
            drive(0)
            for n in range(2):
                if n:
                    pe.wait_ge(gate_ready, n)
                pe_rows(pe, arrived(pe, pc_gate[n]), (4, 5), hT, KD, proj_ps)
            for q in range(SQ):
                if q + 1 < SQ:
                    drive(q + 1)
                pe.wait_ge(st_ready, q + 1)
                if q >= 2:
                    pe.wait_ge(y_ready, q - 1)
                for j in range(4):
                    for n, (c_, x_) in enumerate(((CTr, sT), (CTi, sU))):
                        m = pe.matmul(bank(6 + q % 2)[32 * j:32 * j + 32, 0:SEQ], c_[:, q, 32 * j:32 * j + 32], x_[:, j, :],
                                      start=(n == 0), stop=(n == 1), tile_position=(0, 32 * j))
                m.then_inc(y_ps, 1)
            for n in range(2, 4):
                pe.wait_ge(gate_ready, n)
                pe_rows(pe, arrived(pe, pc_gate[n]), (4, 5), hT, KD, proj_ps)
            pe.wait_ge(gate_ready, 4)
            pe.wait_ge(gel_ready, 1)
            pe_cols(pe, arrived(pe, pc_glu), 4, gel, SQ, out_ps)

        def act_s3(act, o):
            def gate(n):
                act.wait_ge(proj_ps, 4 + n + 1)
                dst = (sgs if n < 2 else sga)[:, :, (n % 2) * 512:(n % 2 + 1) * 512]
                o(act.activation(dst, bank(4, 2).rearrange("p (t m) -> p t m", t=TT), ACT.Sigmoid), gate_ready)
            gate(0)
            gate(1)
            act.wait_ge(y_ready, SQ)
            gate(2)
            gate(3)
            o(act.activation(gel.rearrange("p q s -> p (q s)"), yT.rearrange("p q s -> p (q s)"), ACT.Gelu_apprx_tanh), gel_ready)
            act.wait_ge(out_ps, 1)
            o(act.activation(sglu.rearrange("p q s -> p (q s)"), bank(4, 2), ACT.Sigmoid), gel_ready)

        def dve_s3(dve, o):
            dve.wait_ge(tab_ready, 2)

            def y_out(q):
                dve.wait_ge(y_ps, q + 1)
                o(dve.scalar_tensor_tensor(yT[:, q, :], uT[:, q, :], dcol[:, q:q + 1], bank(6 + q % 2)[:, 0:SEQ],
                                           ALU.mult, ALU.add), y_ready)
            for q in range(SQ):
                cq, sq = cosS[:, 4 * q:4 * q + 4, :], sinS[:, 4 * q:4 * q + 4, :]
                re, im = (bank(0, 4).rearrange("p (j c s) -> p j c s", j=4, c=2)[:, :, n, :] for n in range(2))
                dve.wait_ge(bu_ps, q + 1)
                if q:
                    y_out(q - 1)
                o(dve.tensor_tensor(sA, re, cq, ALU.mult))
                o(dve.tensor_tensor(sT, im, sq, ALU.mult))
                o(dve.tensor_tensor(sA, sA, sT, ALU.add))
                o(dve.tensor_tensor(sB, im, cq, ALU.mult))
                o(dve.tensor_tensor(sT, re, sq, ALU.mult), bu_read)
                o(dve.tensor_tensor(sB, sB, sT, ALU.subtract))
                for x_ in (sA, sB):
                    for j in range(4):
                        o(dve.tensor_tensor_scan(x_[:, j, :], cols_bc(mag[:, 4 * q + j], SEQ), x_[:, j, :], 0.0, ALU.mult, ALU.add))
                o(dve.tensor_tensor(sT, sA, cq, ALU.mult))
                o(dve.tensor_tensor(sU, sB, sq, ALU.mult))
                o(dve.tensor_tensor(sT, sT, sU, ALU.subtract))
                o(dve.tensor_tensor(sU, sA, sq, ALU.mult))
                o(dve.tensor_tensor(sB, sB, cq, ALU.mult))
                o(dve.scalar_tensor_tensor(sU, sU, -1.0, sB, ALU.mult, ALU.subtract), st_ready)
            y_out(SQ - 1)
            dve.wait_ge(gel_ready, 2)
            o(dve.tensor_tensor(ysT, gel, sglu, ALU.mult), ys_ready)

        def pe_s5(pe):
            pe.wait_ge(ys_ready, 1)
            for n, (pc, src) in enumerate(((pc_ws, ysT), (pc_wa, yaT))):
                w = arrived(pe, pc)
                for t in range(TT):
                    for c in range(2):
                        for k in range(4):
                            m = pe.matmul(bank(4 * n + 2 * t + c), src[:, k, t * P:(t + 1) * P], w[:, k, c * 512:(c + 1) * 512],
                                          start=(k == 0), stop=(k == 3))
                m.then_inc(out_ps, 1)
            pe_turn(pe, mgd, "merged")
            pe_after_turn(pe, "merged")
            for n, pc in enumerate(pc_out):
                pe_rows(pe, arrived(pe, pc), (4 + n, 6 + n), mgT, KD, out_ps)

        def dve_s5(dve, o):
            dve.wait_ge(out_ps, 2)
            dve.wait_ge(gate_ready, 4)
            for t in range(TT):
                o(dve.tensor_tensor(mgd[:, t, :], sgs[:, t, :], bank(2 * t, 2), ALU.mult))
            dve.wait_ge(out_ps, 3)
            for t in range(TT):
                o(dve.tensor_tensor(mtmp, sga[:, t, :], bank(4 + 2 * t, 2), ALU.mult))
                o(dve.tensor_tensor(mgd[:, t, :], mgd[:, t, :], mtmp, ALU.add), nat_ready)
            dve_rms(dve, o, 2)
            for t in range(TT):
                o(dve.scalar_tensor_tensor(mtmp, bank(4 + 2 * t, 2), rms[:, t:t + 1], GTm, ALU.mult, ALU.mult))
                o(dve.tensor_tensor(x3[:, t, :], x3[:, t, :], mtmp, ALU.add), x1_ready)

        def act_s5(act, o):
            act_turned(act, o, mgT, "merged")
            act.wait_ge(out_ps, 5)
            act_rms(act, o, [bank(4 + 2 * t, 2) for t in range(TT)], ar(10240, D), 2)
        pc_ada2 = [piece(by_k(ada_w, n * 512, n * 512 + 512), ada_ps, n + 1) for n in range(6, 12)]
        FIRST = len(pieces)
        E_SLOT = [(FIRST + i) % SLOTS for i in range(SLOTS)]
        E_USED = [(FIRST - s + SLOTS - 1) // SLOTS for s in E_SLOT]
        assert SLOTS == 6
        (cond2_ready, rout_in) = (sem(n) for n in (
            "cond2_ready", "rout_in"))
        (mk_ready, pos_ready, wT_ready, bias_in) = (sem(n) for n in (
            "mk_ready", "pos_ready", "wT_ready", "bias_in"))
        ff_ps, x2_ready = sem("ff_ps"), sem("x2_ready")

        class Steps:

            def __init__(self, kind):
                self.p_ready = sem(kind + "_p_ready")
                self.pw_ready = sem(kind + "_pw_ready")
                self.x_ps = sem(kind + "_x_ps")
                self.x_ready = sem(kind + "_x_ready")
                self.pwT_ps = sem(kind + "_pwT_ps")
                self.pwT_ready = sem(kind + "_pwT_ready")
                self.g_ps = sem(kind + "_g_ps")
                self.u_ps = sem(kind + "_u_ps")
                self.gm_ready = sem(kind + "_gm_ready")
                self.sg_ready = sem(kind + "_sg_ready")
                self.a_ready = sem(kind + "_a_ready")
                self.aT_ps = sem(kind + "_aT_ps")
                self.aT_ready = sem(kind + "_aT_ready")
                self.d_ps = sem(kind + "_d_ps")
                self.y_out = sem(kind + "_y_out")
                self.s_ps = sem(kind + "_s_ps")

        main, extra = Steps("first"), Steps("further")

        Bf, Af, GTf = ar(0, D), ar(D, D), ar(3072, D)
        condrep2 = ar3(4096, 1024, KD)
        gpre2, gpost2 = ar(11264, D), ar(12288, D)
        h2 = ar3(6144, 2048, TT)
        h2T = ar3(8192, 2048, KD)
        rw, rb = ar3(13312, 256, KD), ar(13568, E)
        lg, top8, idx8, idxf = ar3(13600, 64, TT), ar3(13664, 16, TT), ar3(13680, 16, TT), ar3(13696, 16, TT)
        ew, esum, eqt = ar3(13712, 8, TT), ar(13720, TT), ar(13728, E)
        mk, wt, posm = ar3(13792, 64, TT), ar3(13856, 64, TT), ar3(13920, 64, TT)
        cnt = ar(14016, E).bitcast(i32)
        wT = ar(14048, SEQ, E)
        bgs, bus, bds = ar(14336, FF, E), ar(15360, FF, E), ar(16384, D, E)
        Psel, Pw = ar3(17408, 256, TT), ar3(17664, 256, TT)
        PwT, Ee = ar(17920, SEQ), ar(18176, CAP, E)
        XT = ar3(18432, 1024, KD)
        gm, um, sg, act_, actT, Yb = (ar(19456 + 512 * n, 512) for n in range(6))

        def pool_s6(pool):
            pool.wait_ge(out_ps, 3)
            for n, d in enumerate((Bf, Af, GTf)):
                dma(pool, d, row(A["ada_b"][0][(3 + n) * D:(4 + n) * D]), rout_in)
            dma(pool, gpre2, row(A["ffn_pre_g"][0]), rout_in)
            dma(pool, gpost2, row(A["ffn_post_g"][0]), rout_in)
            dma(pool, rw, A["router_w"][0].rearrange("(k p) e -> p k e", p=P), rout_in)
            dma(pool, rb, row(A["router_b"][0]), rout_in)
            pool.wait_ge(x1_ready, 1)
            for d, a in ((bgs, "b_gate"), (bus, "b_up"), (bds, "b_down")):
                dma(pool, d, A[a][0], bias_in)

        def pe_s6(pe):
            pe.wait_ge(cond2_ready, 1)
            for n, pc in enumerate(pc_ada2):
                if n == 4:
                    pe.wait_ge(x1_ready, 2)
                w = arrived(pe, pc)
                for k in range(KD):
                    m = pe.matmul(bank(n), condrep2[:, k, :], w[:, k, :], start=(k == 0), stop=(k == KD - 1))
                m.then_inc(ada_ps, 1)
            pe_turn(pe, h2, "experts")
            pe_after_turn(pe, "experts")
            pe.wait_ge(rout_in, 16 * 7)
            for t in range(TT):
                for k in range(KD):
                    m = pe.matmul(bank(6)[:, t * E:(t + 1) * E], h2T[:, k, t * P:(t + 1) * P], rw[:, k, :],
                                  start=(k == 0), stop=(k == KD - 1))
            m.then_inc(router_ps, 1)
            pe.wait_ge(mk_ready, 1)
            pe.matmul(bank(7)[:, 0:E], con("before"), mk[:, 0, :], start=True, stop=True)
            pe.matmul(bank(7)[:, E:2 * E], con("before"), mk[:, 1, :], start=True, stop=False)
            pe.matmul(bank(7)[:, E:2 * E], con("ones"), mk[:, 0, :], start=False, stop=True)
            for t in range(TT):
                m = pe.matmul(bank(7)[:, 2 * E:3 * E], con("ones"), mk[:, t, :], start=(t == 0), stop=(t == 1))
            m.then_inc(router_ps, 1)
            for t in range(TT):
                m = pe.transpose(bank(0, 1, E)[:, t * P:(t + 1) * P], wt[:, t, :], ident)
            m.then_inc(router_ps, 1)
            pe.wait_ge(wT_ready, 1)
            pe.wait_ge(pos_ready, 1)
            pe.wait_ge(bias_in, 48)
            for t in range(TT):
                for d in range(2):
                    m = pe.matmul(bank(4 + 2 * t + d), wT[:, t * P:(t + 1) * P], bds[:, d * 512:(d + 1) * 512],
                                  start=True, stop=False, skip_group_check=True)
            m.then_inc(extra.s_ps, 1)

        def act_s6(act, o):
            act.wait_ge(x1_ready, 2)
            act_rms(act, o, [x3[:, t, :] for t in range(TT)], ar(10240, D), 3)
            act_turned(act, o, h2T, "experts")
            act.wait_ge(fn_asked, 1)
            o(act.activation(ew, ew, ACT.Exp), fn_done)
            act.wait_ge(router_ps, 3)
            o(act.copy(wT, bank(0, 1, E)[:, 0:SEQ]), wT_ready)

        def dve_cond2(dve, o):
            o(dve.tensor_copy(condrep2, cols_bc(cond, P)), cond2_ready)

        def dve_s6(dve, o):
            dve.wait_ge(rout_in, 16 * 7)
            dve.wait_ge(ada_ps, 12)
            o(dve.tensor_tensor(Bf, Bf, bank(0, 2), ALU.add))
            o(dve.scalar_tensor_tensor(Af, bank(2, 2), 1.0, Af, ALU.add, ALU.add))
            o(dve.tensor_tensor(Af, Af, gpre2, ALU.mult))
            o(dve.tensor_tensor(GTf, GTf, bank(4, 2), ALU.add))
            o(dve.tensor_tensor(GTf, GTf, gpost2, ALU.mult))
            dve_rms(dve, o, 3)
            for t in range(TT):
                o(dve.scalar_tensor_tensor(h2[:, t, :], x3[:, t, :], rms[:, t:t + 1], Af, ALU.mult, ALU.mult))
                o(dve.tensor_tensor(h2[:, t, :], h2[:, t, :], Bf, ALU.add), nat_ready)
            dve.wait_ge(router_ps, 1)
            o(dve.tensor_tensor(lg, bank(6)[:, 0:2 * E].rearrange("p (t e) -> p t e", t=TT), rows_bc(rb, TT), ALU.add))
            for t in range(TT):
                o(dve.max(top8[:, t, :], lg[:, t, :]))
                o(dve.max_index(idx8[:, t, :].bitcast(u32), top8[:, t, :], lg[:, t, :]))
            o(dve.tensor_copy(idxf, idx8.bitcast(u32)))
            for t in range(TT):
                o(dve.tensor_scalar(ew[:, t, :], top8[:, t, 0:TOPK], top8[:, t, 0:1], None, ALU.subtract),
                  fn_asked if t == TT - 1 else None)
            for t in range(TT):
                o(dve.tensor_scalar(mk[:, t, :], con("experts"), idxf[:, t, 0:1], None, ALU.is_equal))
                for k in range(1, TOPK):
                    o(dve.scalar_tensor_tensor(mk[:, t, :], con("experts"), idxf[:, t, k:k + 1], mk[:, t, :], ALU.is_equal, ALU.add))
            dve.wait_ge(fn_done, 1)
            o(dve.tensor_reduce(esum, ew, AX.X, ALU.add))
            o(dve.reciprocal(esum, esum))
            o(dve.tensor_tensor(ew, ew, cols_bc(esum, TOPK), ALU.mult))
            for t in range(TT):
                o(dve.tensor_scalar(wt[:, t, :], con("experts"), idxf[:, t, 0:1], ew[:, t, 0:1], ALU.is_equal, ALU.mult))
                for k in range(1, TOPK):
                    o(dve.tensor_scalar(eqt, con("experts"), idxf[:, t, k:k + 1], ew[:, t, k:k + 1], ALU.is_equal, ALU.mult))
                    last = dve.tensor_tensor(wt[:, t, :], wt[:, t, :], eqt, ALU.add)
                    o(last, mk_ready if (t, k) == (TT - 1, TOPK - 1) else None)
            dve.wait_ge(router_ps, 2)
            o(dve.scalar_tensor_tensor(posm, bank(7)[:, 0:2 * E].rearrange("p (t e) -> p t e", t=TT), 1.0, mk, ALU.add, ALU.mult))
            o(dve.tensor_scalar(posm, posm, -1.0, None, ALU.add))
            o(dve.tensor_copy(cnt, bank(7)[:, 2 * E:3 * E]), pos_ready)

        W7 = [RING[:, i * SLOT_W:(i + 1) * SLOT_W] for i in E_SLOT]
        gate_w = [W7[h].rearrange("p (k n) -> p k n", k=KD) for h in range(2)]
        up_w = [W7[2 + h].rearrange("p (k n) -> p k n", k=KD) for h in range(2)]
        down_w = [W7[4 + h].rearrange("p (k n) -> p k n", k=4) for h in range(2)]

        def slot_iota(r, n):
            a = names["slots"][0] + r * 2 * CAP
            return CON[:, a:a + n]

        def dve_round(dve, s, n, e, r):
            for t in range(TT):
                dve.tensor_scalar(Psel[:, t, :], slot_iota(r, 2 * CAP), posm[:, t, bass.ds(e, 1)], None, ALU.is_equal)
            dve.drain()
            dve.tensor_copy(Ee, ident[0:E, bass.ds(e, 1)].to_broadcast([E, CAP])).then_inc(s.p_ready, 1)
            for t in range(TT):
                m = dve.tensor_scalar(Pw[:, t, :], slot_iota(r, 2 * CAP), posm[:, t, bass.ds(e, 1)], wt[:, t, bass.ds(e, 1)],
                                      ALU.is_equal, ALU.mult)
                if t == 0:
                    dve.drain()
            m.then_inc(s.pw_ready, 1)
            dve.wait_ge(s.g_ps, n)
            dve.tensor_scalar(gm, bank(0), LIMIT, None, ALU.min).then_inc(s.gm_ready, 1)
            dve.wait_ge(s.u_ps, n)
            dve.tensor_scalar(um, bank(1), LIMIT, -LIMIT, ALU.min, ALU.max)
            dve.drain()
            dve.scalar_tensor_tensor(um, um, 1.0, gm, ALU.add, ALU.mult)
            dve.drain()
            dve.wait_ge(s.sg_ready, n)
            dve.tensor_tensor(act_, um, sg, ALU.mult).then_inc(s.a_ready, 1)

        def act_round(act, s, n):
            act.wait_ge(s.x_ps, n)
            act.copy(XT.rearrange("p k m -> p (k m)"), bank(2, 2)).then_inc(s.x_ready, 1)
            act.wait_ge(s.pwT_ps, n)
            act.copy(PwT, bank(3)[:, 0:SEQ]).then_inc(s.pwT_ready, 1)
            act.wait_ge(s.gm_ready, n)
            act.activation(sg, gm, ACT.Sigmoid, scale=ALPHA).then_inc(s.sg_ready, 1)
            act.wait_ge(s.aT_ps, n)
            act.copy(actT, bank(3)).then_inc(s.aT_ready, 1)
            act.wait_ge(s.d_ps, n)
            act.copy(Yb, bank(2)).then_inc(s.y_out, 1)

        def pe_round(pe, s, n, weights):
            pe.wait_ge(s.p_ready, n)
            for k in range(KD):
                for t in range(TT):
                    m = pe.matmul(bank(2 + k // 4)[:, (k % 4) * P:(k % 4 + 1) * P], h2[:, t, k * P:(k + 1) * P], Psel[:, t, :],
                                  start=(t == 0), stop=(t == 1))
            m.then_inc(s.x_ps, 1)
            pe.wait_ge(s.pw_ready, n)
            pe.wait_ge(s.x_ready, n)
            for t in range(TT):
                m = pe.transpose(bank(3)[:, t * P:(t + 1) * P], Pw[:, t, :], ident)
            m.then_inc(s.pwT_ps, 1)
            for i, (w, b_, done) in enumerate(((gate_w, bgs, s.g_ps), (up_w, bus, s.u_ps))):
                weights(i)
                for k in range(KD):
                    for h in range(2):
                        pe.matmul(bank(i)[h * CAP:(h + 1) * CAP, :], XT[:, k, 0:CAP], w[h][:, k, :], start=(k == 0), stop=False)
                for h in range(2):
                    m = pe.matmul(bank(i)[h * CAP:(h + 1) * CAP, :], Ee, b_[:, h * 512:(h + 1) * 512], start=False, stop=True)
                m.then_inc(done, 1)
            pe.wait_ge(s.a_ready, n)
            pe.wait_ge(s.pwT_ready, n)
            for j in range(4):
                m = pe.transpose(bank(3)[:, j * P:(j + 1) * P], act_[:, j * P:(j + 1) * P], ident)
            m.then_inc(s.aT_ps, 1)
            weights(2)
            pe.wait_ge(s.aT_ready, n)
            for h in range(2):
                for j in range(4):
                    for d in range(2):
                        m = pe.matmul(bank(2)[d * CAP:(d + 1) * CAP, :], actT[:, j * P + h * CAP:j * P + (h + 1) * CAP],
                                      down_w[h][:, j, d * 512:(d + 1) * 512], start=(h + j == 0), stop=(h + j == 4))
            m.then_inc(s.d_ps, 1)
            pe.wait_ge(s.y_out, n)
            for t in range(TT):
                for d in range(2):
                    m = pe.matmul(bank(4 + 2 * t + d), PwT[d * CAP:(d + 1) * CAP, t * P:(t + 1) * P], Yb[d * CAP:(d + 1) * CAP, :],
                                  start=False, stop=False, skip_group_check=True)
            m.then_inc(s.s_ps, 1)

        def further(eng, e, rounds_of, body=None):
            n_e = eng.value_load(cnt[0:1, bass.ds(e, 1)], min_val=0, max_val=SEQ)

            def deeper(r):
                with eng.If(n_e > r * CAP):
                    eng.reg_add(rounds_of, rounds_of, 1)
                    if body is not None:
                        body(r, eng.snap(rounds_of))
                    if r + 1 < ROUNDS:
                        deeper(r + 1)
            deeper(1)

        def expert_rounds(eng, first_round, extra_round):
            eng.wait_ge(pos_ready, 1)
            taken = eng.alloc_register(f"further_{eng.engine.name}")
            eng.reg_mov(taken, 0)
            with eng.Fori(0, E) as e:
                first_round(e)
                further(eng, e, taken, lambda r, n: extra_round(e, r, n))

        def pe_s7(pe):
            def first(e):
                def weights(i):
                    for h in range(2):
                        n = 2 * i + h
                        pe.wait_ge(slot_ready[E_SLOT[n]], e * 16 + 16 * (E_USED[n] + 1))
                pe_round(pe, main, e + 1, weights)
            expert_rounds(pe, first, lambda e, r, n: pe_round(pe, extra, n, lambda i: None))
            pe.wait_ge(main.y_out, E)

        def dve_s7(dve):
            expert_rounds(dve, lambda e: dve_round(dve, main, e + 1, e, 0), lambda e, r, n: dve_round(dve, extra, n, e, r))

        def act_s7(act):
            expert_rounds(act, lambda e: act_round(act, main, e + 1), lambda e, r, n: act_round(act, extra, n))

        def load_expert(sp, e, free):
            for i, name in enumerate(("w_gate", "w_up")):
                free(i)
                for h in range(2):
                    w = A[name][0][e, :, h * 512:(h + 1) * 512] if isinstance(e, int) else A[name][0][bass.ds(e, 1), :, h * 512:(h + 1) * 512]
                    w = w.rearrange("(k p) n -> p k n", p=P) if isinstance(e, int) else w.rearrange("a (k p) n -> p (a k) n", p=P)
                    sp.dma_start((gate_w, up_w)[i][h], w).then_inc(slot_ready[E_SLOT[2 * i + h]], 16)
            free(2)
            for h in range(2):
                w = A["w_down"][0][e, h * 512:(h + 1) * 512, :] if isinstance(e, int) else A["w_down"][0][bass.ds(e, 1), h * 512:(h + 1) * 512, :]
                w = w.rearrange("(k p) n -> p k n", p=P) if isinstance(e, int) else w.rearrange("a (k p) n -> p (a k) n", p=P)
                sp.dma_start(down_w[h], w).then_inc(slot_ready[E_SLOT[4 + h]], 16)

        def sp_s7(sp):
            def free_first(i):
                for h in range(2):
                    used = pieces[FIRST - SLOTS + 2 * i + h]
                    sp.wait_ge(used[1], used[2])
            load_expert(sp, 0, free_first)
            sp.wait_ge(pos_ready, 1)
            taken = sp.alloc_register("further_SP")
            sp.reg_mov(taken, 1)
            with sp.Fori(1, E) as e:
                further(sp, e - 1, taken)

                def free(i):
                    sp.wait_ge((main.g_ps, main.u_ps, main.d_ps)[i], e)
                    if i == 0:
                        sp.wait_ge(extra.s_ps, taken)
                load_expert(sp, e, free)

        def post(dve, o, n, b0, gain, tells, tmp):
            dve_rms(dve, o, n)
            for t in range(TT):
                o(dve.scalar_tensor_tensor(tmp, bank(b0 + 2 * t, 2), rms[:, t:t + 1], gain, ALU.mult, ALU.mult))
                o(dve.tensor_tensor(x3[:, t, :], x3[:, t, :], tmp, ALU.add), tells)

        def act_s8(act, o):
            act.wait_ge(ff_ps, 1)
            act.wait_ge(bv_stored, 16)
            act_rms(act, o, [bank(4 + 2 * t, 2) for t in range(TT)], ar(10240, D), 4)

        def dve_s8(dve, o):
            post(dve, o, 4, 4, GTf, x2_ready, ar(4096, D))

        def pe_s8(pe):
            for t in range(TT):
                for d in range(2):
                    m = pe.matmul(bank(4 + 2 * t + d), con("zero_rows", E), bds[:, d * 512:(d + 1) * 512],
                                  start=False, stop=True, skip_group_check=True)
            m.then_inc(ff_ps, 1)
        (mem_in, mkv_ps, mkv_ready, gain_in) = (sem(n) for n in (
            "mem_in", "mkv_ps", "mkv_ready", "gain_in"))
        (post_done, gu_ps, gu_silu, gu_done, dn_ps, ffn_done) = (sem(n) for n in (
            "post_done", "gu_ps", "gu_silu", "gu_done", "dn_ps", "ffn_done"))
        (hot_in, bv_ready, bv_stored, bm_in) = (sem(n) for n in (
            "hot_in", "bv_ready", "bv_stored", "bm_in"))
        out_stored, neg_ready = sem("out_stored"), sem("neg_ready")
        pc_at_ffn = []
        pc_mem, pc_ao, pc_gu, pc_dn = [], [], [], []
        MOE_PIECES = SLOTS
        LAST = FIRST + MOE_PIECES

        def moe_last():
            for i in range(SLOTS):
                pieces.append((None, (main.g_ps, main.u_ps, main.d_ps)[i // 2], E))
        moe_last()
        E_MORE = E - 1

        def arrived2(pe, pc):
            pe.wait_ge(slot_ready[pc[0] % SLOTS], 16 * (pc[0] // SLOTS + 1 + E_MORE))
            return pc[1]

        def layer_pieces(i):
            pc_mem.append(piece(by_k(A["mem_w_kv_2"][i], 0, 2 * MW), mkv_ps, i + 1))
            if i == 0:
                w = A["att_w_in_2"][0]
                pc_at.extend(piece(by_k(w, n * 512, n * 512 + 512), proj_ps, 8 + n + 1) for n in range(5))
                w = A["att_w_out_2"][0]
            else:
                w = A["dn_w_in_2"][0]
                pc_dw.extend(piece(by_k(w, n * 512, min(n * 512 + 512, w.shape[1])), proj_ps, 13 + n + 1) for n in range(7))
                w = A["dn_w_out_2"][0]
            pc_ao.append([piece(by_k(w, n * 512, n * 512 + 512), out_ps, 5 + 2 * i + n + 1) for n in range(2)])
            w = A["ffn_w_gate_up_2"][i]
            pc_gu.append([piece(by_k(w, n * 512, n * 512 + 512), gu_ps, 11 * i + n + 1) for n in range(11)])
            w = A["ffn_w_down_2"][i].rearrange("(k p) n -> p k n", p=P)
            pc_dn.append([piece(w[:, n * 4:min(n * 4 + 4, FC2), :], dn_ps, 6 * i + n + 1) for n in range(6)])
        pc_at, pc_dw = [], []
        layer_pieces(0)
        layer_pieces(1)

        gA, gB = ar(2048, D), ar(3072, D)
        hn = ar3(6144, 2048, TT)
        yA = ar3(6144, 2048, KD)
        hT2 = ar3(8192, 2048, KD)
        mem_nat, mem_n, mem_T, mem_g = ar3(15360, 2048, TT), ar3(17408, 2048, TT), ar3(19456, 2048, KD), ar(4096, D)
        kmT, vm = ar3(21504, 512, 2), ar3(22016, 512, TT)
        prob3 = [ar(4096, 1024), ar(5120, 1024), ar(8192, 1024)]
        qkA = ar3(10240, 3072, 12)
        vA = ar3(13312, 1536, TT)
        qmA = ar3(14848, 512, 2)
        BM = [[ar3(15360 + 1024 * (3 * t + g), 1024, HPG) for g in range(3)] for t in range(TT)]
        hotS, relS, bvS = ar(8192, 3 * 2 * SEQ, BUCKETS + 1), ar(9728, ATT_HEADS, BUCKETS + 1), ar3(10240, 1536, 3)[0:HPG]
        mx3, dn3, em3, mxx = ar3(9216, 12, 3), ar3(9228, 12, 3), ar3(9240, 12, 3), ar(9252, HPG)
        actF = ar3(10240, FC2 * SEQ, FC2)
        sil = [ar(16384, 512), ar(16896, 512)]
        tmpP = ar(4096, D)
        tmpJ = ar(5120, D)

        PRE = ("attention", "ffn0", "delta", "ffn1")

        def act_pre(act, o, n_rms, k):
            act_rms(act, o, [x3[:, t, :] for t in range(TT)], tmpJ, n_rms)
            act_turned(act, o, hT2, PRE[k])

        def dve_pre(dve, o, n_rms, k, gains):
            dve_rms(dve, o, n_rms)
            dve.wait_ge(gain_in, 16 * gains)
            for t in range(TT):
                o(dve.scalar_tensor_tensor(hn[:, t, :], x3[:, t, :], rms[:, t:t + 1], gA, ALU.mult, ALU.mult), nat_ready)

        def pe_pre(pe, k):
            pe_turn(pe, hn, PRE[k])
            pe_after_turn(pe, PRE[k])

        def pool_gains(pool, i, names2):
            for d, a in zip((gA, gB), names2):
                dma(pool, d, row(A[a][i]), gain_in)

        def pool_mem(pool, i):
            dma(pool, mem_nat, A["mem_2"][0].rearrange("(t p) d -> p t d", p=P), mem_in)
            dma(pool, mem_g, row(A["mem_norm_2"][i]), mem_in)

        def act_mem(act, o, i, n_rms):
            act.wait_ge(mem_in, 32 * (i + 1))
            act_rms(act, o, [mem_nat[:, t, :] for t in range(TT)], tmpJ, n_rms)
            act_turned(act, o, mem_T, f"memory{i}")
            act.wait_ge(mkv_ps, i + 1)
            o(act.copy(kmT.rearrange("p c s -> p (c s)"), bank(4)))
            o(act.copy(vm.rearrange("p t n -> p (t n)"), bank(5)), mkv_ready)

        def dve_mem(dve, o, i, n_rms):
            dve.wait_ge(mem_in, 32 * (i + 1))
            dve_rms(dve, o, n_rms)
            for t in range(TT):
                o(dve.scalar_tensor_tensor(mem_n[:, t, :], mem_nat[:, t, :], rms[:, t:t + 1], mem_g, ALU.mult, ALU.mult), nat_ready)

        def pe_mem(pe, i):
            pe_turn(pe, mem_n, f"memory{i}")
            pe_after_turn(pe, f"memory{i}")
            w = arrived2(pe, pc_mem[i])
            for c in range(2):
                for k in range(KD):
                    pe.matmul(bank(4)[:, c * SEQ:(c + 1) * SEQ], w[:, k, c * P:(c + 1) * P], mem_T[:, k, :], start=(k == 0), stop=(k == KD - 1))
            for t in range(TT):
                for k in range(KD):
                    m = pe.matmul(bank(5)[:, t * MW:(t + 1) * MW], mem_T[:, k, t * P:(t + 1) * P], w[:, k, MW:2 * MW],
                                  start=(k == 0), stop=(k == KD - 1))
            m.then_inc(mkv_ps, 1)

        def half_head(x, c0, i):
            return x[HD * (i % 2):HD * (i % 2) + HD, c0 + i // 2, :]

        def pe_mem_attention(pe, i, qm):
            for t in range(TT):
                n = 10 + 2 * i + t
                pe.wait_ge(sc_read, n - 1)
                pe_scores(pe, n, lambda i_: half_head(qm, 0, i_)[:, t * P:(t + 1) * P], lambda i_: half_head(kmT, 0, i_))
            for t in range(TT):
                pe_probs(pe, 10 + 2 * i + t, 10 + 2 * i + t, lambda kb, i_: vm[:, kb, i_ * HD:(i_ + 1) * HD])

        def act_mem_attention(act, o, i):
            for t in range(TT):
                act_probs(act, o, 10 + 2 * i + t, 10 + 2 * i + t)

        def dve_mem_attention(dve, o, i):
            for t in range(TT):
                dve_softmax(dve, o, t, 10 + 2 * i + t, HD ** -0.5, None)
            for t in range(TT):
                dve_pv(dve, o, t, 10 + 2 * i + t, yA[:, 6:8, t * P:(t + 1) * P])

        def pe_out(pe, i):
            for n, pc in enumerate(pc_ao[i]):
                pe_rows(pe, arrived2(pe, pc), (4 + n, 6 + n), yA, KD, out_ps)

        def pe_ffn(pe, i):
            pe_pre(pe, 2 * i + 1)
            pe.wait_ge(post_done, 2 * (i + 1))
            for n, pc in enumerate(pc_gu[i]):
                w = arrived2(pe, pc)
                if n >= 2:
                    pe.wait_ge(gu_done, 11 * i + n - 1)
                b0 = 4 + 2 * (n % 2)
                for g in range(2):
                    for c in range(2):
                        for k in range(KD):
                            m = pe.matmul(bank(b0 + g)[:, c * SEQ:(c + 1) * SEQ], w[:, k, (2 * g + c) * P:(2 * g + c + 1) * P], hT2[:, k, :],
                                          start=(k == 0), stop=(k == KD - 1))
                m.then_inc(gu_ps, 1)
            for n, pc in enumerate(pc_dn[i]):
                w = arrived2(pe, pc)
                if n in (0, 5):
                    pe.wait_ge(gu_done, 11 * i + (10 if n == 0 else 11))
                for j in range(w.shape[1]):
                    f = 4 * n + j
                    for t in range(TT):
                        for d in range(2):
                            m = pe.matmul(bank(2 * t + d), actF[:, f, t * P:(t + 1) * P], w[:, j, d * 512:(d + 1) * 512],
                                          start=(f == 0), stop=(f == FC2 - 1))
                m.then_inc(dn_ps, 1)

        def act_ffn(act, o, i, n_rms):
            act.wait_ge(post_done, 2 * (i + 1))
            act_pre(act, o, n_rms, 2 * i + 1)
            for n in range(11):
                act.wait_ge(gu_ps, 11 * i + n + 1)
                if n >= 2:
                    act.wait_ge(gu_done, 11 * i + n - 1)
                o(act.activation(sil[n % 2], bank(4 + 2 * (n % 2)), ACT.Silu), gu_silu)
            act.wait_ge(dn_ps, 6 * (i + 1))
            act_rms(act, o, [bank(2 * t, 2) for t in range(TT)], tmpJ, n_rms + 1)

        def dve_ffn(dve, o, i, n_rms):
            dve_pre(dve, o, n_rms, 2 * i + 1, 4 * (i + 1))
            for n in range(11):
                dve.wait_ge(gu_silu, 11 * i + n + 1)
                o(dve.tensor_tensor(actF[:, 2 * n:2 * n + 2, :].rearrange("p c s -> p (c s)"), sil[n % 2], bank(5 + 2 * (n % 2)), ALU.mult), gu_done)
            post(dve, o, n_rms + 1, 0, gB, ffn_done, tmpP)

        def pool_ffn(pool, i):
            pool.wait_ge(post_done, 2 * (i + 1))
            pool_gains(pool, i, ("norm_ffn_pre_2", "norm_ffn_post_2"))

        bv_dram = nc.dram_tensor("band_bias", [ATT_HEADS, 2 * SEQ], f32, kind="Internal").ap()

        def pool_bias(pool):
            pool.wait_ge(pos_ready, 1)
            pool.wait_ge(neg_ready, 1)
            dma(pool, hotS, A["k_hot"], hot_in)
            dma(pool, relS[0:BUCKETS, :], A["rel_bias_2"], hot_in)
            pool.wait_ge(bv_ready, 1)
            dma(pool, bv_dram.rearrange("(g h) r -> h g r", g=3), bvS, bv_stored)
            pool.wait_ge(bv_stored, 16)

        def pool_s9(pool):
            pool.wait_ge(x2_ready, 2)
            pool_gains(pool, 0, ("norm_mix_pre_2", "norm_mix_post_2"))
            pool_mem(pool, 0)
            pool.wait_ge(mkv_ready, 1)
            for t in range(TT):
                for g in range(3):
                    for a in range(2):
                        src = bass.AP(bv_dram.tensor, bv_dram.offset + (HPG * g + a) * 2 * SEQ + SEQ - (t + 1) * P,
                                      [[1, P], [2 * 2 * SEQ, 2], [1, SEQ]])
                        dma(pool, BM[t][g][:, 2 * a:2 * a + 2, :], src, bm_in)

        def dve_bias(dve, o):
            o(dve.memset(relS, NEG), neg_ready)

        def pe_bias(pe):
            pe.wait_ge(hot_in, 32)
            for g in range(3):
                m = pe.matmul(bank(g, 1, HPG), relS[:, HPG * g:HPG * g + HPG], hotS[:, g * 2 * SEQ:(g + 1) * 2 * SEQ], start=True, stop=True)
            m.then_inc(router_ps, 1)
            pe.wait_ge(bv_ready, 1)

        def act_bias(act, o):
            act.wait_ge(router_ps, 4)
            o(act.copy(bvS.rearrange("h g r -> h (g r)"), bank(0, 3, HPG)), bv_ready)

        def pe_s9(pe):
            pe.wait_ge(x2_ready, 2)
            pe_mem(pe, 0)
            pe_pre(pe, 0)
            pe.wait_ge(mkv_ready, 1)
            pe_cols(pe, arrived2(pe, pc_at[0]), 4, hT2, KD, proj_ps)
            pe_cols(pe, arrived2(pe, pc_at[1]), 6, hT2, KD, proj_ps)
            pe_cols(pe, arrived2(pe, pc_at[2]), 0, hT2, KD, proj_ps)
            pe_rows(pe, arrived2(pe, pc_at[3]), (2, 3), hT2, KD, proj_ps)
            w = arrived2(pe, pc_at[4])
            pe.wait_ge(proj_ev, 4 + 1)
            for t in range(TT):
                for k in range(KD):
                    pe.matmul(bank(4)[:, t * SEQ:(t + 1) * SEQ], hT2[:, k, t * P:(t + 1) * P], w[:, k, 0:256], start=(k == 0), stop=(k == KD - 1))
            for c in range(2):
                for k in range(KD):
                    m = pe.matmul(bank(5)[:, c * SEQ:(c + 1) * SEQ], w[:, k, 256 + c * P:256 + (c + 1) * P], hT2[:, k, :], start=(k == 0), stop=(k == KD - 1))
            m.then_inc(proj_ps, 1)
            pe.wait_ge(proj_ev, 4 + 6)
            pe.wait_ge(bm_in, 16 * 12)
            for t in range(TT):
                for g in range(3):
                    n = 4 + 3 * t + g
                    pe.wait_ge(sc_read, n - 1)
                    pe_scores(pe, n, lambda i: half_head(qkA, 2 * g, i)[:, t * P:(t + 1) * P], lambda i: half_head(qkA, 6 + 2 * g, i), BM[t][g])
                for g in range(3):
                    pe_probs(pe, 4 + 3 * t + g, 4 + 3 * t + g, lambda kb, i: vA[:, kb, (HPG * g + i) * HD:(HPG * g + i + 1) * HD])
            pe_mem_attention(pe, 0, qmA)
            pe.wait_ge(pv_ev, 12)
            pe_out(pe, 0)

        def act_s9(act, o):
            act_mem(act, o, 0, 5)
            act_pre(act, o, 6, 0)
            for n in range(3):
                act.wait_ge(proj_ps, 8 + n + 1)
                o(act.copy(qkA[:, 4 * n:4 * n + 4, :].rearrange("p c s -> p (c s)"), bank((4, 6, 0)[n], 2)), proj_ev)
            act.wait_ge(proj_ps, 8 + 4)
            o(act.copy(vA[:, :, 0:512], bank(2, 2).rearrange("p (t n) -> p t n", t=TT)), proj_ev)
            act.wait_ge(proj_ps, 8 + 5)
            o(act.copy(vA[:, :, 512:768], bank(4).rearrange("p (t n) -> p t n", t=TT)), proj_ev)
            o(act.copy(qmA.rearrange("p c s -> p (c s)"), bank(5)), proj_ev)
            for t in range(TT):
                for g in range(3):
                    act.wait_ge(sc_sub, 4 + 3 * t + g + 1)
                    b = probs_of(4 + 3 * t + g)
                    o(act.activation(b, b, ACT.Exp), sc_exp)
                act.wait_ge(fn_asked, t + 2)
                o(act.activation(em3, em3, ACT.Exp), fn_done)
                for g in range(3):
                    act_probsT(act, o, 4 + 3 * t + g)
            act_mem_attention(act, o, 0)
            act.wait_ge(out_ps, 7)
            act_rms(act, o, [bank(4 + 2 * t, 2) for t in range(TT)], tmpJ, 7)

        def dve_s9(dve, o):
            dve_mem(dve, o, 0, 5)
            dve_pre(dve, o, 6, 0, 2)
            for t in range(TT):
                for g in range(3):
                    n = 4 + 3 * t + g
                    s3 = probs_of(n).rearrange("p (h k) -> p h k", h=HPG)
                    dve.wait_ge(sc_ps, n + 1)
                    if g == 0:
                        dve.wait_ge(prT_ps, n)
                    o(dve.tensor_scalar(probs_of(n), bank(2 * (n % 2), 2), HD ** -0.5, None, ALU.mult), sc_read)
                    o(dve.tensor_reduce(mx3[:, g, :], s3, AX.X, ALU.max))
                    o(dve.tensor_tensor(s3, s3, cols_bc(mx3[:, g, :], SEQ), ALU.subtract), sc_sub)
                o(dve.tensor_tensor(mxx, mx3[:, 0, :], mx3[:, 1, :], ALU.max))
                o(dve.tensor_tensor(mxx, mxx, mx3[:, 2, :], ALU.max))
                o(dve.tensor_tensor(em3, mx3, rows_bc(mxx, 3), ALU.subtract), fn_asked)
                for g in range(3):
                    n = 4 + 3 * t + g
                    dve.wait_ge(sc_exp, n + 1)
                    o(dve.tensor_reduce(dn3[:, g, :], probs_of(n).rearrange("p (h k) -> p h k", h=HPG), AX.X, ALU.add))
                dve.wait_ge(fn_done, t + 2)
                o(dve.tensor_tensor(dn3, dn3, em3, ALU.mult))
                o(dve.tensor_tensor(mxx, dn3[:, 0, :], dn3[:, 1, :], ALU.add))
                o(dve.tensor_tensor(mxx, mxx, dn3[:, 2, :], ALU.add))
                o(dve.reciprocal(mxx, mxx))
                o(dve.tensor_tensor(em3, em3, rows_bc(mxx, 3), ALU.mult))
                for g in range(3):
                    s3 = probs_of(4 + 3 * t + g).rearrange("p (h k) -> p h k", h=HPG)
                    o(dve.tensor_tensor(s3, s3, cols_bc(em3[:, g, :], SEQ), ALU.mult), pr_ready)
                for g in range(3):
                    dve_pv(dve, o, None, 4 + 3 * t + g, yA[:, 2 * g:2 * g + 2, t * P:(t + 1) * P])
            dve_mem_attention(dve, o, 0)
            post(dve, o, 7, 4, gB, post_done, tmpP)

        (dl_in, cv_ready, cs_ready, qk_ready) = (sem(n) for n in (
            "dl_in", "cv_ready", "cs_ready", "qk_ready"))
        (g_done, gc_ps, gr_in, gr_ps, df_ready, df_exp, kk_ps, kq_ps, kq_read) = (sem(n) for n in (
            "g_done", "gc_ps", "gr_in", "gr_ps", "df_ready", "df_exp", "kk_ps", "kq_ps", "kq_read"))
        (lm_ready, la_ps, la_ready, lx_ps, rhs_ready, uw_ps, uw_ready, kl_ready, st_ps, s_out, vn_ps, un_ready, o_ps, o_read) = (sem(n) for n in (
            "lm_ready", "la_ps", "la_ready", "lx_ps", "rhs_ready", "uw_ps", "uw_ready", "kl_ready", "st_ps", "s_out", "vn_ps", "un_ready", "o_ps", "o_read"))
        (onorm_in, on_ready, lev_in) = (sem(n) for n in (
            "onorm_in", "on_ready", "lev_in"))
        NM = TT * DH
        CH = 3 * DH
        PADW = SEQ + TAPS - 1
        rawP = ar3(10240, CH * PADW, CH)
        conv = ar3(14920, CH * SEQ, CH)
        nat = ar3(10240, TT * CH * DD, TT * CH)
        qkT = ar3(14848, 2 * DH * SEQ, 2 * DH)
        zN = ar3(19528, TT * TW, TT)
        oN = ar3(21064, NM * DD, NM)
        qmD = ar3(8192, 512, 2)
        Lm = ar3(0, NM * P, NM)
        Tm, TTm = ar3(4096, NM * P, NM), ar3(8192, NM * P, NM)
        intra = ar3(17920, NM * P, NM)
        scr = ar3(1536, NM * P, NM)
        Ab = [ar(6144 + 512 * n, 512) for n in range(3)]
        uD, wTD = ar3(0, NM * P, NM), ar3(4096, DH * P, DH)
        rhsD = ar3(1536, NM * P, DH)
        klD, stD = ar3(1536, DH * P, DH), ar3(2304, DH * P, DH)
        LEVELS = 7
        lev_at = names["before"][0]
        levC = CON[:, lev_at:lev_at + LEVELS * 2 * P]

        def level(n, d):
            return levC[:, (2 * n + d) * P:(2 * n + d + 1) * P]

        taps = sm(900, CH * TAPS).rearrange("p (c k) -> p c k", c=CH)
        gin = sm(990, TT * 4 * DH).rearrange("p (t d b h) -> p t d b h", t=TT, d=2, b=2)
        alog, dtb = sm(1038, 12), sm(1050, 12)
        gdl, gab, beta = (sm(1062 + 24 * n, 24).rearrange("p (t d h) -> p t d h", t=TT, d=2) for n in range(3))
        gcs, egc, ekl = (sm(1134 + 24 * n, 24).rearrange("p (t d h) -> p t d h", t=TT, d=2) for n in range(3))
        ssn = sm(1206, 24).rearrange("p (t h) -> p t h", t=TT)
        sso = sm(1230, 12)
        onr = ar(9728, DD)

        def merge4(x):
            return x.rearrange("p a b -> p (a b)")

        def pool_s11(pool):
            pool.wait_ge(ffn_done, 2)
            pool_gains(pool, 1, ("norm_mix_pre_2", "norm_mix_post_2"))
            pool_mem(pool, 1)
            for c in range(CH):
                dma(pool, taps[:, c, :], A["dn_conv_2"][0][:, c * P:(c + 1) * P].rearrange("k p -> p k"), dl_in)
            dma(pool, alog, row(A["dn_a_log_2"][0].rearrange("d h -> (d h)")), dl_in)
            dma(pool, dtb, row(A["dn_dt_bias_2"][0].rearrange("d h -> (d h)")), dl_in)
            dma(pool, levC, A["k_levels"], lev_in)
            pool.wait_ge(o_read, 2)
            dma(pool, onr, row(A["dn_out_norm_2"][0]), onorm_in)
        DL_IN = 16 * (CH + 2)

        def pe_s11(pe):
            pe.wait_ge(ffn_done, 2)
            pe_mem(pe, 1)
            pe_pre(pe, 2)
            pe.wait_ge(mkv_ready, 2)
            bk = [4, 6, 0, 2]
            for n in range(4):
                pe_cols(pe, arrived2(pe, pc_dw[n]), bk[n], hT2, KD, proj_ps)
            w = arrived2(pe, pc_dw[4])
            pe.wait_ge(proj_ev, 10 + 1)
            for c in range(2):
                for k in range(KD):
                    pe.matmul(bank(4)[:, c * SEQ:(c + 1) * SEQ], w[:, k, c * P:(c + 1) * P], hT2[:, k, :], start=(k == 0), stop=(k == KD - 1))
            for t in range(TT):
                for k in range(KD):
                    m = pe.matmul(bank(5)[:, t * SEQ:(t + 1) * SEQ], hT2[:, k, t * P:(t + 1) * P], w[:, k, 256:512], start=(k == 0), stop=(k == KD - 1))
            m.then_inc(proj_ps, 1)
            pe.wait_ge(proj_ev, 10 + 2)
            pe_rows(pe, arrived2(pe, pc_dw[5]), (6, 7), hT2, KD, proj_ps)
            w = arrived2(pe, pc_dw[6])
            pe.wait_ge(proj_ev, 10 + 3)
            for t in range(TT):
                for k in range(KD):
                    pe.matmul(bank(0)[:, t * 24:(t + 1) * 24], hT2[:, k, t * P:(t + 1) * P], w[:, k, 0:24], start=(k == 0), stop=(k == KD - 1))
            for c in range(2):
                for k in range(KD):
                    m = pe.matmul(bank(1)[:, c * SEQ:(c + 1) * SEQ], w[:, k, 24 + c * P:24 + (c + 1) * P], hT2[:, k, :], start=(k == 0), stop=(k == KD - 1))
            m.then_inc(proj_ps, 1)
            pe.wait_ge(proj_ev, 15 + 4)
            pe_mem_attention(pe, 1, qmD)
            pe.wait_ge(pv_ev, 14)
            for b in range(NT):
                pe.wait_ge(cs_ready, 3)
                if b >= 8:
                    pe.wait_ge(turned, D_BASE + b - 7)
                for j in range(4):
                    n = 4 * b + j
                    t, c = n // CH, n % CH
                    m = pe.transpose(bank(b % 8)[:, j * P:(j + 1) * P], conv[:, c, t * P:(t + 1) * P], ident)
                m.then_inc(turn_ps, 1)
            pe.wait_ge(g_done, 1)
            pe.wait_ge(turned, D_BASE + NT)
            for t in range(TT):
                pe.matmul(bank(7)[:, t * 12:t * 12 + 6], con("upto"), gdl[:, t, 0, :], start=True, stop=True)
                pe.matmul(bank(7)[:, t * 12 + 6:t * 12 + 12], con("from"), gdl[:, t, 1, :], start=True, stop=True)
            m = pe.matmul(bank(7)[:, 24:48], con("ones"), gdl.rearrange("p t d h -> p (t d h)"), start=True, stop=True)
            m.then_inc(gc_ps, 1)
            pe.wait_ge(qk_ready, 1)
            for b in range(6):
                for j in range(4):
                    n = 4 * b + j
                    t, c = n // (2 * DH), n % (2 * DH)
                    m = pe.transpose(bank(b)[:, j * P:(j + 1) * P], nat[:, t * CH + c, :], ident)
                m.then_inc(turn_ps, 1)
            pe.wait_ge(turned, D_BASE + NT + QT)
            pe.wait_ge(fn_asked, 5)
            for d in range(2):
                pe_delta(pe, d)
            pe.wait_ge(on_ready, 1)
            for b in range(3):
                for j in range(4):
                    t, h = (4 * b + j) // DH, (4 * b + j) % DH
                    m = pe.transpose(bank(b)[:, j * P:(j + 1) * P], oN[:, t * DH + h, :], ident)
                m.then_inc(turn_ps, 1)
            pe.wait_ge(turned, D_BASE + NT + QT + OT)
            pe_out(pe, 1)

        def mh(m):
            return m // DH, m % DH

        def pe_delta(pe, d):
            first, second = (0, 1) if d == 0 else (1, 0)
            pe.wait_ge(gr_in, d + 1)
            for b in range(3):
                m = pe.matmul(bank(b), con("ones"), merge4(scr[:, 4 * b:4 * b + 4, :]), start=True, stop=True)
            m.then_inc(gr_ps, 1)
            for b in range(3):
                for j in range(4):
                    t, h = mh(4 * b + j)
                    m = pe.matmul(bank(3 + b)[:, j * P:(j + 1) * P], qkT[:, DH + h, t * P:(t + 1) * P], qkT[:, h, t * P:(t + 1) * P], start=True, stop=True)
            m.then_inc(kq_ps, 1)
            pe.wait_ge(df_ready, 2 * d + 2)
            for b in range(3):
                for j in range(4):
                    t, h = mh(4 * b + j)
                    m = pe.matmul(bank(b)[:, j * P:(j + 1) * P], qkT[:, DH + h, t * P:(t + 1) * P], qkT[:, DH + h, t * P:(t + 1) * P], start=True, stop=True)
            m.then_inc(kk_ps, 1)
            pe.wait_ge(kq_read, d + 1)
            for n in range(7):
                g = 7 * d + n
                pe.wait_ge(lm_ready, g + 1)
                for b in range(3):
                    for j in range(4):
                        m_ = 4 * b + j
                        m = pe.matmul(bank(b)[:, j * P:(j + 1) * P], scr[:, m_, :], TTm[:, m_, :], start=True, stop=True)
                    m.then_inc(la_ps, 1)
                for b in range(3):
                    pe.wait_ge(la_ready, 3 * g + b + 1)
                    for j in range(4):
                        m_ = 4 * b + j
                        m = pe.matmul(bank(3 + b)[:, j * P:(j + 1) * P], Tm[:, m_, :], Ab[b][:, j * P:(j + 1) * P], start=True, stop=True)
                    for j in range(4):
                        m_ = 4 * b + j
                        if n < 6:
                            m = pe.matmul(bank(b)[:, j * P:(j + 1) * P], Ab[b][:, j * P:(j + 1) * P], Tm[:, m_, :], start=True, stop=True)
                m.then_inc(lx_ps, 1)
            for t in range(TT):
                pe.wait_ge(rhs_ready, 2 * d + t + 1)
                for h in range(DH):
                    m_ = t * DH + h
                    m = pe.matmul(bank(m_ // 4)[:, (m_ % 4) * P:(m_ % 4 + 1) * P], TTm[:, m_, :], rhsD[:, h, 0:P], start=True, stop=True)
                if t == second:
                    for h in range(DH):
                        m = pe.matmul(bank(3 + h // 4)[:, (h % 4) * P:(h % 4 + 1) * P], rhsD[:, h, P:2 * P], TTm[:, t * DH + h, :], start=True, stop=True)
                m.then_inc(uw_ps, 1)
            pe.wait_ge(uw_ready, d + 1)
            pe.wait_ge(kl_ready, d + 1)
            for h in range(DH):
                m = pe.matmul(bank(5 + h // 4)[:, (h % 4) * P:(h % 4 + 1) * P], klD[:, h, :], uD[:, first * DH + h, :], start=True, stop=True)
            m.then_inc(st_ps, 1)
            pe.wait_ge(s_out, d + 1)
            for h in range(DH):
                m = pe.matmul(bank(3 + h // 4)[:, (h % 4) * P:(h % 4 + 1) * P], wTD[:, h, :], stD[:, h, :], start=True, stop=True)
            for h in range(DH):
                m = pe.matmul(bank(h // 4)[:, (h % 4) * P:(h % 4 + 1) * P], qkT[:, h, second * P:(second + 1) * P], stD[:, h, :], start=True, stop=True)
            m.then_inc(vn_ps, 1)
            pe.wait_ge(un_ready, d + 1)
            for i, t in enumerate((first, second)):
                for h in range(DH):
                    m = pe.matmul(bank(4 + 2 * i + h // 4)[:, (h % 4) * P:(h % 4 + 1) * P], intra[:, t * DH + h, :], uD[:, t * DH + h, :], start=True, stop=True)
            m.then_inc(o_ps, 1)
            pe.wait_ge(o_read, d + 1)

        def act_s11(act, o):
            act.wait_ge(ffn_done, 2)
            act_mem(act, o, 1, 10)
            act_pre(act, o, 11, 2)
            bk = [4, 6, 0, 2]
            for n in range(4):
                act.wait_ge(proj_ps, 13 + n + 1)
                o(act.copy(rawP[:, 4 * n:4 * n + 4, 2:2 + SEQ], bank(bk[n], 2).rearrange("p (c s) -> p c s", c=4)), proj_ev)
            act.wait_ge(proj_ps, 8 + 10)
            o(act.copy(rawP[:, 16:18, 2:2 + SEQ], bank(4).rearrange("p (c s) -> p c s", c=2)), proj_ev)
            o(act.copy(zN[:, :, 0:256], bank(5).rearrange("p (t n) -> p t n", t=TT)), proj_ev)
            act.wait_ge(proj_ps, 8 + 11)
            o(act.copy(zN[:, :, 256:768], bank(6, 2).rearrange("p (t n) -> p t n", t=TT)), proj_ev)
            act.wait_ge(proj_ps, 8 + 12)
            o(act.copy(gin.rearrange("p t d b h -> p (t d b h)"), bank(0)[:, 0:48]), proj_ev)
            o(act.copy(qmD.rearrange("p c s -> p (c s)"), bank(1)), proj_ev)
            act_mem_attention(act, o, 1)
            act.wait_ge(fn_asked, 4)
            o(act.activation(beta, gin[:, :, :, 1, :], ACT.Sigmoid))
            o(act.activation(alog, alog, ACT.Exp))
            o(act.activation(gab, gab, ACT.Exp, scale=-1.0))
            o(act.activation(gab, gab, ACT.Ln, bias=1.0), fn_done)
            for n in range(3):
                act.wait_ge(cv_ready, DH * (n + 1))
                c = conv[:, DH * n:DH * (n + 1), :]
                o(act.activation(c, c, ACT.Silu), cs_ready)
            for b in range(NT):
                act.wait_ge(turn_ps, D_BASE + b + 1)
                o(act.copy(merge4(nat[:, 4 * b:4 * b + 4, :]), bank(b % 8)), turned)
            act.wait_ge(fn_asked, 5)
            o(act.activation(egc, gcs, ACT.Exp))
            o(act.activation(ekl, ekl, ACT.Exp), fn_done)
            act.wait_ge(fn_asked, 6)
            o(act.activation(ssn, ssn, ACT.Sqrt), fn_done)
            for b in range(6):
                act.wait_ge(turn_ps, D_BASE + NT + b + 1)
                n = 4 * b
                t, c = n // (2 * DH), n % (2 * DH)
                o(act.copy(qkT[:, c:c + 4, t * P:(t + 1) * P], bank(b).rearrange("p (c s) -> p c s", c=4)), turned)
            for d in range(2):
                act_delta(act, o, d)
            act.wait_ge(fn_asked, 7)
            o(act.activation(sso, sso, ACT.Sqrt), fn_done)
            o(act.activation(zN, zN, ACT.Silu), fn_done)
            for b in range(3):
                act.wait_ge(turn_ps, D_BASE + NT + QT + b + 1)
                for j in range(4):
                    t, h = (4 * b + j) // DH, (4 * b + j) % DH
                    o(act.copy(yA[:, h, t * P:(t + 1) * P], bank(b)[:, j * P:(j + 1) * P]), turned if j == 3 else None)
            act.wait_ge(out_ps, 9)
            act_rms(act, o, [bank(4 + 2 * t, 2) for t in range(TT)], tmpJ, 12)

        def act_delta(act, o, d):
            second = 1 - d
            act.wait_ge(df_ready, 2 * d + 1)
            o(act.activation(intra, intra, ACT.Exp), df_exp)
            act.wait_ge(df_ready, 2 * d + 2)
            o(act.activation(Lm, Lm, ACT.Exp, scale=-1.0), df_exp)
            for n in range(7):
                g = 7 * d + n
                for b in range(3):
                    act.wait_ge(la_ps, 3 * g + b + 1)
                    if g and b == 0:
                        act.wait_ge(lx_ps, g)
                    o(act.copy(Ab[b], bank(b)), la_ready)
            act.wait_ge(uw_ps, 2 * d + 2)
            o(act.copy(merge4(uD), bank(0, 3)))
            o(act.copy(merge4(wTD), bank(3, 2)[:, 0:DH * P]), uw_ready)
            act.wait_ge(st_ps, d + 1)
            o(act.copy(merge4(stD), bank(5, 2)[:, 0:DH * P]), s_out)

        def dve_s11(dve, o):
            dve.wait_ge(dl_in, DL_IN)
            dve_mem(dve, o, 1, 10)
            dve_pre(dve, o, 11, 2, 6)
            o(dve.memset(spread(rawP[:, 0, 0:1], [PADW, CH], [1, TAPS // 2]), 0.0))
            o(dve.memset(spread(rawP[:, 0, SEQ + TAPS // 2:SEQ + TAPS // 2 + 1], [PADW, CH], [1, TAPS // 2]), 0.0))
            dve_mem_attention(dve, o, 1)
            dve.wait_ge(proj_ev, 15 + 3)
            o(dve.tensor_tensor(gdl, gin[:, :, :, 0, :], rows_bc(dtb.rearrange("p (d h) -> p d h", d=2), TT), ALU.add))
            o(dve.tensor_scalar(gab, gdl, -1.0, None, ALU.mult))
            o(dve.tensor_tensor(gab, gab, gdl, ALU.max), fn_asked)
            o(dve.tensor_scalar(gdl, gdl, 0.0, None, ALU.max))
            dve.wait_ge(fn_done, 4)
            o(dve.tensor_tensor(gdl, gdl, gab, ALU.add))
            o(dve.tensor_tensor(gdl, gdl, rows_bc(alog.rearrange("p (d h) -> p d h", d=2), TT), ALU.mult))
            o(dve.tensor_scalar(gdl, gdl, -1.0, None, ALU.mult), g_done)
            for c in range(CH):
                dve.wait_ge(proj_ev, 10 + min(c // 4, 4) + 1)
                o(dve.tensor_scalar(conv[:, c, :], rawP[:, c, 0:SEQ], taps[:, c, 0:1], None, ALU.mult))
                for k in range(1, TAPS):
                    o(dve.scalar_tensor_tensor(conv[:, c, :], rawP[:, c, k:k + SEQ], taps[:, c, k:k + 1], conv[:, c, :], ALU.mult, ALU.add),
                      cv_ready if k == TAPS - 1 else None)
            dve.wait_ge(gc_ps, 1)
            o(dve.tensor_copy(gcs.rearrange("p t d h -> p (t d h)"), bank(7)[:, 0:24]))
            o(dve.tensor_tensor(ekl.rearrange("p t d h -> p (t d h)"), bank(7)[:, 24:48], gcs.rearrange("p t d h -> p (t d h)"), ALU.subtract), fn_asked)
            sq = Tm
            for t in range(TT):
                x = nat[:, t * CH:t * CH + 2 * DH, :]
                o(dve.tensor_tensor(sq, x, x, ALU.mult))
                o(dve.tensor_reduce(ssn[:, t, :], sq, AX.X, ALU.add))
            o(dve.tensor_scalar(ssn, ssn, EPS, None, ALU.add), fn_asked)
            dve.wait_ge(fn_done, 6)
            o(dve.reciprocal(ssn, ssn))
            o(dve.tensor_scalar(ssn[:, :, 0:DH], ssn[:, :, 0:DH], DD ** -0.5, None, ALU.mult))
            for t in range(TT):
                x = nat[:, t * CH:t * CH + 2 * DH, :]
                o(dve.tensor_tensor(x, x, cols_bc(ssn[:, t, :], DD), ALU.mult), qk_ready if t == TT - 1 else None)
            o(dve.memset(oN, 0.0))
            dve.wait_ge(fn_done, 5)
            dve.wait_ge(turned, D_BASE + NT + QT)
            for d in range(2):
                dve_delta(dve, o, d)
            sq = Lm
            o(dve.tensor_tensor(sq, oN, oN, ALU.mult))
            o(dve.tensor_reduce(sso, sq, AX.X, ALU.add))
            o(dve.tensor_scalar(sso, sso, 1.0 / DD, EPS, ALU.mult, ALU.add), fn_asked)
            dve.wait_ge(fn_done, 7)
            o(dve.reciprocal(sso, sso))
            o(dve.tensor_tensor(oN, oN, cols_bc(sso, DD), ALU.mult))
            dve.wait_ge(onorm_in, 16)
            o(dve.tensor_tensor(oN, oN, rows_bc(onr, NM), ALU.mult))
            dve.wait_ge(fn_done, 8)
            o(dve.tensor_tensor(merge4(oN), merge4(oN), merge4(zN), ALU.mult), on_ready)
            post(dve, o, 12, 4, gB, post_done, tmpP)

        def dve_delta(dve, o, d):
            first, second = (0, 1) if d == 0 else (1, 0)
            def per(x):
                return bass.AP(x.tensor, x.offset + d * DH, [list(x.ap[0]), [2 * DH, TT], [1, DH]])
            def wide(x):
                y = per(x)
                return bass.AP(y.tensor, y.offset, [list(v) for v in y.ap] + [[0, P]])
            def four(x):
                return x.rearrange("p (t h) n -> p t h n", t=TT)
            tri = con("upto") if d == 0 else con("from")
            tri4 = bass.AP(tri.tensor, tri.offset, [list(tri.ap[0]), [0, TT], [0, DH], [1, P]])
            o(dve.tensor_tensor(four(scr), tri4, wide(gdl), ALU.mult), gr_in)
            dve.wait_ge(gr_ps, d + 1)
            o(dve.tensor_tensor(four(Tm), bank(0, 3).rearrange("p (t h n) -> p t h n", t=TT, h=DH), wide(gcs), ALU.subtract))
            o(dve.tensor_scalar(intra, Tm, 0.0, None, ALU.min), df_ready)
            o(dve.tensor_scalar(Lm, Tm, 0.0, None, ALU.max), df_ready)
            idb = rows_bc(ident, NM)
            o(dve.tensor_copy(Tm, idb))
            o(dve.tensor_copy(TTm, idb))
            dve.wait_ge(df_exp, 2 * d + 1)
            o(dve.tensor_tensor(intra, intra, rows_bc(tri, NM), ALU.mult))
            dve.wait_ge(kq_ps, d + 1)
            o(dve.tensor_tensor(merge4(intra), merge4(intra), bank(3, 3), ALU.mult), kq_read)
            dve.wait_ge(df_exp, 2 * d + 2)
            o(dve.tensor_tensor(four(Lm), four(Lm), wide(beta), ALU.mult))
            dve.wait_ge(kk_ps, d + 1)
            o(dve.tensor_tensor(merge4(Lm), merge4(Lm), bank(0, 3), ALU.mult))
            dve.wait_ge(lev_in, 16)
            for n in range(7):
                g = 7 * d + n
                if n:
                    dve.wait_ge(la_ps, 3 * g)
                o(dve.tensor_tensor(scr, Lm, rows_bc(level(n, d), NM), ALU.mult), lm_ready)
                dve.wait_ge(lx_ps, g + 1)
                o(dve.tensor_tensor(merge4(TTm), merge4(TTm), bank(3, 3), ALU.subtract))
                if n < 6:
                    o(dve.tensor_tensor(merge4(Tm), merge4(Tm), bank(0, 3), ALU.subtract))
            for t in range(TT):
                if t:
                    dve.wait_ge(uw_ps, 2 * d + t)
                b3 = beta[:, t, d, :]
                o(dve.tensor_tensor(rhsD[:, :, 0:P], nat[:, t * CH + 2 * DH:(t + 1) * CH, :], cols_bc(b3, P), ALU.mult))
                o(dve.tensor_tensor(sso[:, 0:DH], b3, egc[:, t, d, :], ALU.mult))
                o(dve.tensor_tensor(rhsD[:, :, P:2 * P], nat[:, t * CH + DH:t * CH + 2 * DH, :], cols_bc(sso[:, 0:DH], P), ALU.mult), rhs_ready)
            dve.wait_ge(uw_ps, 2 * d + 2)
            o(dve.tensor_tensor(klD, nat[:, first * CH + DH:first * CH + 2 * DH, :], cols_bc(ekl[:, first, d, :], P), ALU.mult), kl_ready)
            dve.wait_ge(vn_ps, d + 1)
            u2 = merge4(uD[:, second * DH:(second + 1) * DH, :])
            o(dve.tensor_tensor(u2, u2, bank(3, 2)[:, 0:DH * P], ALU.subtract), un_ready)
            inter = klD
            o(dve.tensor_tensor(inter, bank(0, 2)[:, 0:DH * P].rearrange("p (h n) -> p h n", h=DH), cols_bc(egc[:, second, d, :], P), ALU.mult))
            def o_of(t):
                return oN[:, t * DH:(t + 1) * DH, :]
            o(dve.tensor_tensor(o_of(second), o_of(second), inter, ALU.add))
            dve.wait_ge(o_ps, d + 1)
            o(dve.tensor_tensor(merge4(o_of(first)), merge4(o_of(first)), bank(4, 2)[:, 0:DH * P], ALU.add))
            o(dve.tensor_tensor(merge4(o_of(second)), merge4(o_of(second)), bank(6, 2)[:, 0:DH * P], ALU.add), o_read)

        def store_out(sp):
            for t in range(TT):
                sp.wait_ge(ffn_done, 2 + t + 1)
                sp.dma_start(out[0, t * P:(t + 1) * P, :], x3[:, t, :]).then_inc(out_stored, 16)
            sp.wait_ge(out_stored, 16 * TT)

        block = ctx.enter_context(nc.Block())

        @block.sync
        def _(sp):
            stream(sp, 0, FIRST)
            sp_s7(sp)
            sp.wait_ge(ff_ps, 1)
            stream(sp, LAST, len(pieces))
            store_out(sp)

        @block.gpsimd
        def _(pool):
            pool_s0(pool)
            pool_s6(pool)
            pool_bias(pool)
            pool_s9(pool)
            pool_ffn(pool, 0)
            pool_s11(pool)
            pool_ffn(pool, 1)


        @block.scalar
        def _(act):
            o = Ordered(act, act_order)
            act_s0(act, o)
            act_s1(act, o)
            act_s2(act, o)
            act_s4(act, o)
            act_s3(act, o)
            act_s5(act, o)
            act_s6(act, o)
            act_bias(act, o)
            act_s7(act)
            act_s8(act, o)
            act_s9(act, o)
            act_ffn(act, o, 0, 8)
            act_s11(act, o)
            act_ffn(act, o, 1, 13)


        @block.vector
        def _(dve):
            o = Ordered(dve, dve_order)
            dve_s0(dve, o)
            dve_s1(dve, o)
            dve_s2(dve, o)
            dve_s4(dve, o)
            dve_s3(dve, o)
            dve_cond2(dve, o)
            dve_s5(dve, o)
            dve_s6(dve, o)
            dve_bias(dve, o)
            dve_s7(dve)
            dve_s8(dve, o)
            dve_s9(dve, o)
            dve_ffn(dve, o, 0, 8)
            dve_s11(dve, o)
            dve_ffn(dve, o, 1, 13)


        @block.tensor
        def _(pe):
            pe_s0(pe)
            pe_s1(pe)
            pe_s2(pe)
            pe_s4(pe)
            pe_s3(pe)
            pe_s5(pe)
            pe_s6(pe)
            pe_bias(pe)
            pe_s7(pe)
            pe_s8(pe)
            pe_s9(pe)
            pe_ffn(pe, 0)
            pe_s11(pe)
            pe_ffn(pe, 1)



def kernel(**inputs):
    import concourse.bacc as bacc
    from concourse.bass_utils import run_bass_kernel_spmd

    nc = bacc.Bacc("TRN2", target_bir_lowering=False, num_devices=1)
    arrays = {name: np.ascontiguousarray(a) for name, a in inputs.items()}
    arrays["ffn_w_gate_up_2"] = paired(arrays["ffn_w_gate_up_2"])
    arrays["k_main"], names, arrays["k_levels"], arrays["k_hot"] = shape_constants()
    A, fed = {}, {}
    for name, a in arrays.items():
        fed[f"in_{name}"] = a
        A[name] = nc.dram_tensor(f"in_{name}", a.shape, mybir.dt.from_np(a.dtype), kind="ExternalInput").ap()
    out = nc.dram_tensor("out", (1, SEQ, D), mybir.dt.float32, kind="ExternalOutput").ap()
    block_kernel(nc, A, out, names)
    r = run_bass_kernel_spmd(nc, [fed], core_ids=[0])
    return r.results[0]["out"]
```

```python
from contextlib import ExitStack

import numpy as np
import concourse.bass as bass
from concourse import mybir

P = 128
D = 1024
SEQ = 256
TT = SEQ // P
KD = D // P
EPS = 1e-6
NEG = -1e30
HEADS, HD = 8, 64
AW = HEADS * HD
SSM_G, SSM_C, SSM_P = 32, 16, 64
SW = SSM_G * SSM_C
SJ = SSM_G * SSM_P // P
SQ = SW // P
E, TOPK, CAP = 32, 4, 64
ROUNDS = SEQ // CAP
FF = 1024
ALPHA, LIMIT = 1.702, 7.0
TW, MW = 768, 256
GROUPS = ((128, 1), (512, 4), (2048, 16))
ATT_HEADS, HPG = 12, 4
BUCKETS, MAX_DIST = 32, 1024
DH = 6
DD = 128
TAPS = 5
FF2 = 2816
FC2 = FF2 // P
TWO_PI = 6.2831845
SLOTS, SLOT_W = 6, 4096


def shape_constants():
    i = np.arange(P)
    c = {}
    c["ident"] = np.eye(P)
    c["ones"] = np.ones((P, P))
    c["upto"] = (i[:, None] <= i[None, :])
    c["from"] = (i[:, None] >= i[None, :])
    c["before"] = (i[:, None] < i[None, :])
    c["slots"] = np.tile(np.arange(SEQ).reshape(ROUNDS, 1, CAP), (1, 2, 1)).reshape(1, -1).repeat(P, 0)
    c["steps"] = np.arange(SEQ)[None, :].repeat(P, 0)
    c["experts"] = np.arange(E)[None, :].repeat(P, 0)
    rot = np.zeros((P, P))
    for b in range(0, P, HD):
        for d in range(HD // 2):
            rot[b + d + HD // 2, b + d] = -1.0
            rot[b + d, b + d + HD // 2] = 1.0
    c["rot"] = rot
    c["zero_rows"] = np.zeros((P, P))
    c["flip"] = np.eye(P)[::-1] * HD ** 0.5
    half = HD // 2
    inv = (np.float32(10000.0) ** (-np.arange(half, dtype=np.float32) / np.float32(half))).astype(np.float32)
    c["inv_freq"] = inv[i % half][:, None]
    causal = np.where(np.arange(SEQ)[None, None, :] <= (i[:, None, None] + P * np.arange(TT)[None, :, None]), 0.0, NEG)
    c["causal"] = causal.reshape(P, -1)
    c["mask_b"] = ((i // SSM_P)[:, None] == (np.arange(2 * SSM_C) // SSM_C)[None, :])
    c["mask_c"] = (((i // SSM_C) % 2)[:, None] == (np.arange(P) // SSM_P)[None, :])
    names, cols, at = {}, [], 0
    for k, v in c.items():
        v = np.asarray(v, np.float32)
        names[k] = (at, v.shape[1])
        at += v.shape[1]
        cols.append(v)
    main = np.ascontiguousarray(np.concatenate(cols, 1))
    lev = []
    for n in range(7):
        b = 1 << n
        m = (i[:, None] // (2 * b) == i[None, :] // (2 * b)) & ((i[:, None] // b) % 2 == 1) & ((i[None, :] // b) % 2 == 0)
        lev.append(np.stack([m, m.T], 1))
    levels = np.stack(lev, 1).astype(np.float32).reshape(P, -1)
    rel = np.arange(SEQ - 1, -SEQ, -1) * -1
    hot = np.zeros((BUCKETS + 1, len(GROUPS), 2 * SEQ), np.float32)
    for g, (window, dil) in enumerate(GROUPS):
        h = window // (2 * dil)
        n = np.abs(rel)
        hb = BUCKETS // 2
        me = hb // 2
        large = me + (np.log(np.maximum(n, 1) / me) / np.log(MAX_DIST / me) * (hb - me)).astype(np.int64)
        bucket = (rel > 0) * hb + np.where(n < me, n, np.minimum(large, hb - 1))
        ok = (rel % dil == 0) & (np.abs(rel // dil) <= h)
        for r in range(len(rel)):
            hot[bucket[r] if ok[r] else BUCKETS, g, r] = 1.0
        hot[BUCKETS, g, len(rel)] = 1.0
    return main, names, levels, hot.reshape(BUCKETS + 1, -1)


def paired(w):
    n, d, f2 = w.shape
    return np.ascontiguousarray(w.reshape(n, d, 2, f2 // 512, 256).transpose(0, 1, 3, 2, 4)).reshape(n, d, f2)


def block_kernel(nc, A, out, names):
    f32, i32, u32 = mybir.dt.float32, mybir.dt.int32, mybir.dt.uint32
    ALU, ACT, AX = mybir.AluOpType, mybir.ActivationFunctionType, mybir.AxisListType
    ctx = ExitStack()

    def sem(name):
        return ctx.enter_context(nc.semaphore(name))

    def sb(name, cols, dt=f32, parts=P):
        return ctx.enter_context(nc.sbuf_tensor(name, [parts, cols], dt))

    def spread(ap, *dims):
        return bass.AP(ap.tensor, ap.offset, [list(ap.ap[0])] + [list(d) for d in dims])

    def cols_bc(ap, n):
        return bass.AP(ap.tensor, ap.offset, [list(d) for d in ap.ap] + [[0, n]])

    def rows_bc(ap, n):
        return bass.AP(ap.tensor, ap.offset, [list(ap.ap[0]), [0, n]] + [list(d) for d in ap.ap[1:]])

    class Ordered:

        def __init__(self, eng, own):
            self.eng, self.own, self.n, self.told, self.base = eng, own, 0, {}, None

        def __call__(self, ins, tells=None):
            if tells is None:
                self.n += 1
                ins.then_inc(self.own, 1)
                self.eng.wait_ge(self.own, self.n if self.base is None else self.base + self.n)
            else:
                self.told[tells.name] = self.told.get(tells.name, 0) + 1
                ins.then_inc(tells, 1)
                if self.base is None:
                    self.eng.wait_ge(tells, self.told[tells.name])

    with ctx:
        CON = sb("constants", A["k_main"].shape[1])
        X = sb("x_res", TT * D)
        RING = sb("ring", SLOTS * SLOT_W)
        AR = sb("arena", 22600)
        SM = sb("smalls", 1280)
        x3 = X[:, :].rearrange("p (t d) -> p t d", t=TT)
        PS = ctx.enter_context(nc.psum_tensor("ps", [P, 4096], f32))

        def con(name, rows=P):
            a, n = names[name]
            return CON[0:rows, a:a + n]

        def bank(b, n=1, rows=P):
            return PS[0:rows, b * 512:(b + n) * 512]

        def ar(at, n, rows=P):
            return AR[0:rows, at:at + n]

        def sm(at, n, rows=P):
            return SM[0:rows, at:at + n]

        ident = con("ident")

        slot_ready = [sem(f"slot_ready{i}") for i in range(SLOTS)]
        pieces = []
        filled = [0] * SLOTS

        def hold(used, count):
            pieces.append((None, used, count))
            return RING[:, (len(pieces) - 1) % SLOTS * SLOT_W:((len(pieces) - 1) % SLOTS + 1) * SLOT_W]

        def piece(src, used, count):
            pieces.append((src, used, count))
            n = len(pieces) - 1
            filled[n % SLOTS] += 1
            shape = [s for s in src.shape][1:]
            w = int(np.prod(shape))
            v = RING[:, (n % SLOTS) * SLOT_W:(n % SLOTS) * SLOT_W + w]
            if len(shape) > 1:
                v = v.rearrange("p (k n) -> p k n", k=shape[0])
            return n, v, filled[n % SLOTS]

        def arrived(pe, pc):
            n, place, loads = pc
            pe.wait_ge(slot_ready[n % SLOTS], 16 * loads)
            return place

        def by_k(w, c0, c1):
            return w[:, c0:c1].rearrange("(k p) n -> p k n", p=P)

        ada_w = A["ada_w"][0]
        w_in = A["w_in"][0]


        (act_order, dve_order) = (sem(n) for n in (
            "act_order", "dve_order"))
        x_in, con_in, mod_in, ssm_in, rope_in = (sem(n) for n in ("x_in", "con_in", "mod_in", "ssm_in", "rope_in"))
        cond_silu, cond_ready, ada_ps = sem("cond_silu"), sem("cond_ready"), sem("ada_ps")
        bc_ready, bc_ps, bc_ev = sem("bc_ready"), sem("bc_ps"), sem("bc_ev")
        par_in, par_exp, par_red, par_trig = sem("par_in"), sem("par_exp"), sem("par_red"), sem("par_trig")
        ph_ready, tab_ready, rope_red, rope_tab = sem("ph_ready"), sem("tab_ready"), sem("rope_red"), sem("rope_tab")
        sq_done, ms_done, rt_done = sem("sq_done"), sem("ms_done"), sem("rt_done")
        (proj_ps, rot_ps, rope_done) = (sem(n) for n in (
            "proj_ps", "rot_ps", "rope_done"))
        sc_ps, sc_read, sc_sub, sc_exp, pr_ready, prT_ps, prT_ready, pv_ps, pv_ev = (sem(n) for n in (
            "sc_ps", "sc_read", "sc_sub", "sc_exp", "pr_ready", "prT_ps", "prT_ready", "pv_ps", "pv_ev"))
        bu_ps, bu_read, st_ready, y_ps, y_ready, gel_ready = (
            sem(n) for n in ("bu_ps", "bu_read", "st_ready", "y_ps", "y_ready", "gel_ready"))
        ys_ready = sem("ys_ready")
        (gate_ready, x1_ready) = (sem(n) for n in (
            "gate_ready", "x1_ready"))
        (gate_ps, mod_ps, mod_read, rows_ready, c_in) = (sem(n) for n in ("gate_ps", "mod_ps", "mod_read", "rows_ready", "c_in"))

        (turn_ps, turned, nat_ready, fn_asked, fn_done, proj_ev, out_ps, router_ps) = (sem(n) for n in (
            "turn_ps", "turned", "nat_ready", "fn_asked", "fn_done", "proj_ev", "out_ps", "router_ps"))
        pc_ada = [piece(by_k(ada_w, n * 512, n * 512 + 512), ada_ps, n + 1) for n in range(6)]
        pc_in = [piece(by_k(w_in, n * 512, n * 512 + 512), proj_ps, n + 1) for n in range(4)]
        pc_ada2 = [piece(by_k(ada_w, n * 512, n * 512 + 512), ada_ps, 6 + 1 + (n - 6) // 4) for n in range(6, 12)]
        pc_gate = [piece(by_k(w_in, (4 + n) * 512, (5 + n) * 512), gate_ps, TT * (n + 1)) for n in range(4)]
        HELD = hold(mod_ps, 2)
        pc_wa = piece(by_k(A["w_attn_branch"][0], 0, D), out_ps, 1)
        pc_glu = piece(by_k(A["ssm_w_glu"][0], 0, SW), out_ps, 2)
        pc_ws = piece(by_k(A["w_ssm_branch"][0], 0, D), out_ps, 3)
        pc_out = [piece(by_k(A["w_out"][0], n * 512, n * 512 + 512), out_ps, 3 + n + 1) for n in range(2)]

        def ar3(at, n, k):
            return ar(at, n).rearrange("p (k m) -> p k m", k=k)

        shm, Am, GTm = ar(0, D), ar(D, D), ar(2 * D, D)
        condrep = ar3(3072, 1024, KD)
        gpre, gpost = ar(4096, D), ar(5120, D)
        h_nat = ar3(4096, 2048, TT)
        hT = ar3(6144, 2048, KD)
        uT, qT, kT = ar3(8192, 1024, 4), ar3(9216, 1024, 4), ar3(20480, 1024, 4)
        vN = ar3(21504, 1024, TT)
        cosS, sinS = ar3(10240, 4096, SJ), ar3(14336, 4096, SJ)
        BTr, BTi, CTr, CTi = (ar3(18432 + 512 * n, 512, SQ) for n in range(4))
        braw = [ar3(10240 + 256 * n, 256, SJ) for n in range(2)]
        bbar = [ar3(10752 + 256 * n, 256, SJ) for n in range(2)]
        craw = [ar3(11264 + 256 * n, 256, SQ) for n in range(2)]
        btmp = ar3(11776, 256, SJ)
        Bd = [ar(12288 + 512 * n, 512) for n in range(2)]
        Cd = [ar(13312 + 512 * n, 512) for n in range(2)]
        BC = [BTr, BTi, CTr, CTi]
        ph_n = ar(3072, 1024)
        qraw, kraw = ar(0, 1024), ar(1024, 1024)
        rtmp = ar3(4096, 1024, 4)
        prob = [ar(4096, 1024), ar(5120, 1024)]
        prT = [ar(0, 1024), ar(1024, 1024)]
        yaT = ar3(3072, 1024, 4)
        sA, sB, sT, sU = ar3(0, 1024, 4), ar3(1024, 1024, 4), ar3(4096, 1024, 4), ar3(5120, 1024, 4)
        yT = ar3(9216, 1024, SQ)
        sgs, sga = ar3(20480, 2048, TT), HELD[:, 0:2048].rearrange("p (t d) -> p t d", t=TT)
        adaS = HELD[:, 2048:3072]
        gel, sglu, ysT = ar3(10240, 1024, SQ), ar3(11264, 1024, SQ), ar3(12288, 1024, SQ)
        mgd, mtmp = ar3(16384, 2048, TT), ar(18432, 1024)
        mgT = ar3(6144, 2048, KD)

        c_col, cond = sm(0, KD), sm(8, KD)
        (lam_re, lam_im, dt_c, mag, th, frq, tc, lbr, lbi, cr, ci, den, fhi, flo) = (sm(16 + 16 * n, SJ) for n in range(14))
        dcol, ssq, rms = sm(256, SQ), sm(260, TT), sm(262, TT)
        cosR, sinR = sm(320, SEQ), sm(576, SEQ)
        tc2, intc = sm(832, SJ), sm(848, SJ)
        cond32 = sm(880, 32 * KD).rearrange("p (k m) -> p k m", k=KD)
        amax, aden = sm(864, HPG), sm(868, HPG)

        def dma(eng, dst, src, s):
            eng.dma_start(dst, src, allow_slow_non_contiguous=True).then_inc(s, 16)

        def row(ap1):
            return bass.AP(ap1.tensor, ap1.offset, [[0, P]] + [list(d) for d in ap1.ap])

        def stream(sp, first, last):
            for n in range(first, last):
                if n >= SLOTS:
                    sp.wait_ge(pieces[n - SLOTS][1], pieces[n - SLOTS][2])
                src = pieces[n][0]
                if src is None:
                    continue
                shape = list(src.shape)[1:]
                v = RING[:, (n % SLOTS) * SLOT_W:(n % SLOTS) * SLOT_W + int(np.prod(shape))]
                if len(shape) > 1:
                    v = v.rearrange("p (k n) -> p k n", k=shape[0])
                sp.dma_start(v, src).then_inc(slot_ready[n % SLOTS], 16)

        def pool_s0(pool):
            for s, a in ((lam_re, "ssm_lam_re"), (lam_im, "ssm_lam_im")):
                dma(pool, s, A[a][0].rearrange("(j g) s -> (g s) j", g=2), par_in)
            for g in range(2):
                src = A["ssm_log_dt"][0]
                dma(pool, dt_c[g * SSM_P:(g + 1) * SSM_P, :],
                    bass.AP(src.tensor, src.offset + g, [[0, SSM_P], [2, SJ]]), par_in)
            for n, a in enumerate(("ssm_b_re", "ssm_b_im")):
                dma(pool, braw[n], A[a][0].rearrange("(j g) s c -> (g s) j c", g=2), ssm_in)
            for n, a in enumerate(("ssm_c_re", "ssm_c_im")):
                dma(pool, craw[n], A[a][0].rearrange("(q r) c s -> (r c) q s", q=SQ), ssm_in)
            dma(pool, dcol, A["ssm_d"][0].rearrange("(q p) -> p q", p=P), ssm_in)
            dma(pool, sinR.bitcast(i32), row(A["positions"][0]), rope_in)
            dma(pool, x3, A["x"][0].rearrange("(t p) d -> p t d", p=P), x_in)
            for n, d in enumerate((shm, Am, GTm)):
                dma(pool, d, row(A["ada_b"][0][n * D:(n + 1) * D]), mod_in)
            dma(pool, gpre, row(A["mix_pre_g"][0]), mod_in)
            dma(pool, gpost, row(A["mix_post_g"][0]), mod_in)

        def sp_first(sp):
            dma(sp, c_col, A["c"].rearrange("a (k p) -> p (a k)", p=P), c_in)
            dma(sp, CON[:, :], A["k_main"], con_in)
            stream(sp, 0, 2)
            sp.wait_ge(ssm_in, 16 * 5)
            sp.wait_ge(rope_in, 16)
            stream(sp, 2, FIRST)

        def act_s0(act, o):
            act.wait_ge(c_in, 16)
            o(act.activation(cond, c_col, ACT.Silu), cond_silu)
            act.wait_ge(par_in, 16 * 4)
            o(act.activation(dt_c, dt_c, ACT.Exp), par_exp)
            act.wait_ge(par_red, 1)
            o(act.activation(mag, mag, ACT.Exp), par_exp)
            act.wait_ge(par_red, 2)
            o(act.activation(lbi, frq, ACT.Sin, scale=TWO_PI))
            o(act.activation(lbr, tc, ACT.Sin, scale=TWO_PI), par_trig)
            act.wait_ge(rope_red, 1)
            o(act.activation(cosR, cosR, ACT.Sin))
            o(act.activation(sinR, sinR, ACT.Sin), rope_tab)
            act.wait_ge(x_in, 16)
            act_rms(act, o, [x3[:, t, :] for t in range(TT)], hT[:, 0:4, :].rearrange("p k m -> p (k m)"), 1)
            for n in range(4):
                act.wait_ge(bc_ps, n + 1)
                o(act.copy(BC[n], bank(6 + n % 2).rearrange("p (q m) -> p q m", q=SQ)), bc_ev)

        def act_tables(act, o, h):
            act.wait_ge(ph_ready, h + 1)
            for x in (sinS, cosS):
                o(act.activation(x[:, 4 * h:4 * h + 4, :], x[:, 4 * h:4 * h + 4, :], ACT.Sin, scale=TWO_PI), tab_ready)

        def turn(dve, o, x, n_int, n_f):
            o(dve.tensor_copy(n_int, x))
            o(dve.tensor_copy(n_f, n_int))
            return dve.tensor_tensor(x, x, n_f, ALU.subtract)

        def quarter_on(dve, o, outp, x, tmp):
            o(dve.tensor_scalar(tmp, x, 0.25, None, ALU.is_gt))
            return dve.scalar_tensor_tensor(outp, x, 0.25, tmp, ALU.add, ALU.subtract)

        def dve_s0(dve, o):
            dve.wait_ge(cond_silu, 1)
            o(dve.tensor_copy(condrep, cols_bc(cond, P)))
            o(dve.tensor_copy(cond32, cols_bc(cond, 32)), cond_ready)
            dve.wait_ge(rope_in, 16)
            dve.wait_ge(con_in, 16)
            o(dve.tensor_copy(cosR, sinR.bitcast(i32)))
            o(dve.tensor_scalar(sinR, cosR, con("inv_freq"), None, ALU.mult))
            turns, whole = ar(8192, SEQ), ar(8448, SEQ)
            o(dve.tensor_scalar(turns, sinR, float(1 / (2 * np.pi)), None, ALU.mult))
            o(dve.tensor_copy(whole.bitcast(i32), turns))
            o(dve.tensor_copy(turns, whole.bitcast(i32)))
            o(dve.scalar_tensor_tensor(sinR, turns, -6.28125, sinR, ALU.mult, ALU.add))
            o(dve.scalar_tensor_tensor(sinR, turns, float(-(2 * np.pi - 6.28125)), sinR, ALU.mult, ALU.add))
            o(dve.tensor_scalar(whole, sinR, float(np.pi / 2), float(-2 * np.pi), ALU.is_gt, ALU.mult))
            o(dve.scalar_tensor_tensor(cosR, sinR, float(np.pi / 2), whole, ALU.add, ALU.add))
            for r in (sinR, cosR):
                last = dve.tensor_scalar(r, r, 3.1415925, -3.1415925, ALU.min, ALU.max)
                o(last, rope_red if r is cosR else None)
            dve.wait_ge(par_exp, 1)
            o(dve.tensor_tensor(mag, lam_re, dt_c, ALU.mult), par_red)
            o(dve.tensor_tensor(th, lam_im, dt_c, ALU.mult))
            o(dve.tensor_scalar(frq, th, float(1 / (2 * np.pi)), None, ALU.mult))
            o(turn(dve, o, frq, intc.bitcast(i32), tc2))
            o(quarter_on(dve, o, tc, frq, tc2), par_red)
            o(dve.tensor_scalar(tc2, frq, 4096.0, None, ALU.mult))
            o(dve.tensor_copy(intc.bitcast(i32), tc2))
            o(dve.tensor_copy(tc2, intc.bitcast(i32)))
            o(dve.tensor_scalar(fhi, tc2, 1.0 / 4096, None, ALU.mult))
            o(dve.tensor_tensor(flo, frq, fhi, ALU.subtract))
            dve.wait_ge(par_exp, 2)
            dve.wait_ge(par_trig, 1)
            o(dve.tensor_tensor(lbr, lbr, mag, ALU.mult))
            o(dve.tensor_tensor(lbi, lbi, mag, ALU.mult))
            o(dve.tensor_scalar(lbr, lbr, -1.0, None, ALU.add))
            o(dve.tensor_tensor(den, lam_re, lam_re, ALU.mult))
            o(dve.tensor_tensor(tc2, lam_im, lam_im, ALU.mult))
            o(dve.tensor_tensor(den, den, tc2, ALU.add))
            o(dve.reciprocal(den, den))
            o(dve.tensor_tensor(cr, lbr, lam_re, ALU.mult))
            o(dve.tensor_tensor(tc2, lbi, lam_im, ALU.mult))
            o(dve.tensor_tensor(cr, cr, tc2, ALU.add))
            o(dve.tensor_tensor(cr, cr, den, ALU.mult))
            o(dve.tensor_tensor(ci, lbi, lam_re, ALU.mult))
            o(dve.tensor_tensor(tc2, lbr, lam_im, ALU.mult))
            o(dve.tensor_tensor(ci, ci, tc2, ALU.subtract))
            o(dve.tensor_tensor(ci, ci, den, ALU.mult))
            dve.wait_ge(ssm_in, 16 * 5)
            crb, cib = cols_bc(cr, SSM_C), cols_bc(ci, SSM_C)
            o(dve.tensor_tensor(bbar[0], braw[0], crb, ALU.mult))
            o(dve.tensor_tensor(btmp, braw[1], cib, ALU.mult))
            o(dve.tensor_tensor(bbar[0], bbar[0], btmp, ALU.subtract))
            o(dve.tensor_tensor(bbar[1], braw[1], crb, ALU.mult))
            o(dve.tensor_tensor(btmp, braw[0], cib, ALU.mult))
            o(dve.tensor_tensor(bbar[1], bbar[1], btmp, ALU.add))
            mb = spread(con("mask_b"), [0, SJ], [SSM_C, 2], [1, SSM_C])
            mc = spread(con("mask_c"), [0, SQ], [SSM_P, 2], [1, SSM_P])
            for n in range(2):
                o(dve.tensor_tensor(Bd[n].rearrange("p (j g c) -> p j g c", g=2, c=SSM_C),
                                    spread(bbar[n], [SSM_C, SJ], [0, 2], [1, SSM_C]), mb, ALU.mult), bc_ready)
            for n in range(2):
                o(dve.tensor_tensor(Cd[n].rearrange("p (q g s) -> p q g s", g=2, s=SSM_P),
                                    spread(craw[n], [SSM_P, SQ], [0, 2], [1, SSM_P]), mc, ALU.mult), bc_ready)
            dve_rms(dve, o, 1)
            dve.wait_ge(mod_in, 16 * 5)
            dve.wait_ge(ada_ps, 6)
            o(dve.tensor_tensor(shm, shm, bank(0, 2), ALU.add))
            o(dve.scalar_tensor_tensor(Am, bank(2, 2), 1.0, Am, ALU.add, ALU.add))
            o(dve.tensor_tensor(Am, Am, gpre, ALU.mult))
            o(dve.tensor_tensor(GTm, GTm, bank(4, 2), ALU.add))
            o(dve.tensor_tensor(GTm, GTm, gpost, ALU.mult))

        def dve_tables(dve, o):
            dve.wait_ge(bc_ps, 4)
            steps = spread(con("steps"), [0, 4], [1, SEQ])
            for h in range(4):
                f3, t3 = sinS[:, 4 * h:4 * h + 4, :], cosS[:, 4 * h:4 * h + 4, :]
                f, t = (x.rearrange("p j s -> p (j s)") for x in (f3, t3))
                o(dve.tensor_tensor(f3, steps, cols_bc(fhi[:, 4 * h:4 * h + 4], SEQ), ALU.mult))
                o(turn(dve, o, f, ph_n.bitcast(i32), t))
                o(dve.tensor_tensor(t3, steps, cols_bc(flo[:, 4 * h:4 * h + 4], SEQ), ALU.mult))
                o(dve.tensor_tensor(f, f, t, ALU.add))
                o(turn(dve, o, f, ph_n.bitcast(i32), t))
                o(quarter_on(dve, o, t, f, ph_n), ph_ready)

        def pe_ada(pe, pcs, base):
            for n, pc in enumerate(pcs):
                w = arrived(pe, pc)
                for k in range(KD):
                    m = pe.matmul(bank(base + n), condrep[:, k, :], w[:, k, :], start=(k == 0), stop=(k == KD - 1))
                m.then_inc(ada_ps, 1)

        def pe_s0(pe):
            pe.wait_ge(cond_ready, 1)
            pe_ada(pe, pc_ada, 0)
            for n in range(4):
                pe.wait_ge(bc_ready, n + 1)
                if n >= 2:
                    pe.wait_ge(bc_ev, n - 1)
                src = (Bd + Cd)[n]
                for q in range(SQ):
                    m = pe.transpose(bank(6 + n % 2)[:, q * P:(q + 1) * P], src[:, q * P:(q + 1) * P], ident)
                m.then_inc(bc_ps, 1)

        norms = [0]

        def act_rms(act, o, srcs, junk, n):
            for t in range(TT):
                o(act.activation(junk, srcs[t], ACT.Square, accum_out=ssq[:, t:t + 1]), sq_done if t == TT - 1 else None)
            act.wait_ge(ms_done, n)
            o(act.activation(rms, rms, ACT.Sqrt), rt_done)

        def dve_rms(dve, o, n, width=D):
            dve.wait_ge(sq_done, n)
            o(dve.tensor_scalar(rms, ssq, 1.0 / width, EPS, ALU.mult, ALU.add), ms_done)
            dve.wait_ge(rt_done, n)
            o(dve.reciprocal(rms, rms))

        TURNS = ("mixer", "merged", "experts", "memory0", "attention", "ffn0", "memory1", "delta", "ffn1")
        NT, QT, OT = 9, 6, 3

        def turn_base(which):
            return 4 * TURNS.index(which) + (NT + QT + OT if which == "ffn1" else 0)

        D_BASE = 4 * (TURNS.index("delta") + 1)

        def pe_turn(pe, src3, which):
            for t in range(TT):
                pe.wait_ge(nat_ready, TT * TURNS.index(which) + t + 1)
                for b in range(2):
                    for k in range(4):
                        kk = 4 * b + k
                        m = pe.transpose(bank(2 * t + b)[:, k * P:(k + 1) * P], src3[:, t, kk * P:(kk + 1) * P], ident)
                    m.then_inc(turn_ps, 1)

        def act_turned(act, o, dst3, which):
            for t in range(TT):
                for b in range(2):
                    act.wait_ge(turn_ps, turn_base(which) + 2 * t + b + 1)
                    o(act.copy(dst3[:, 4 * b:4 * b + 4, t * P:(t + 1) * P],
                               bank(2 * t + b).rearrange("p (k m) -> p k m", k=4)), turned)

        def pe_after_turn(pe, which):
            pe.wait_ge(turned, turn_base(which) + 4)

        def act_s1(act, o):
            act_turned(act, o, hT, "mixer")

        def dve_s1(dve, o):
            for t in range(TT):
                o(dve.scalar_tensor_tensor(h_nat[:, t, :], x3[:, t, :], rms[:, t:t + 1], Am, ALU.mult, ALU.mult))
                o(dve.tensor_tensor(h_nat[:, t, :], h_nat[:, t, :], shm, ALU.add), nat_ready)

        def pe_s1(pe):
            pe_turn(pe, h_nat, "mixer")

        def pe_cols(pe, w, b0, src3, kn, done):
            for c in range(4):
                for k in range(kn):
                    m = pe.matmul(bank(b0 + c // 2)[:, (c % 2) * SEQ:(c % 2 + 1) * SEQ], w[:, k, c * P:(c + 1) * P],
                                  src3[:, k, :], start=(k == 0), stop=(k == kn - 1))
            m.then_inc(done, 1)

        def pe_rows(pe, w, banks, src3, kn, done):
            for t in range(TT):
                for k in range(kn):
                    m = pe.matmul(bank(banks[t]), src3[:, k, t * P:(t + 1) * P], w[:, k, :], start=(k == 0), stop=(k == kn - 1))
            m.then_inc(done, 1)

        def pe_s2(pe):
            pe_after_turn(pe, "mixer")
            pe.wait_ge(bc_ev, 4)
            pe_cols(pe, arrived(pe, pc_in[0]), 4, hT, KD, proj_ps)
            pe_cols(pe, arrived(pe, pc_in[1]), 6, hT, KD, proj_ps)
            pe_cols(pe, arrived(pe, pc_in[2]), 0, hT, KD, proj_ps)
            pe_rows(pe, arrived(pe, pc_in[3]), (2, 3), hT, KD, proj_ps)
            for n, raw in enumerate((qraw, kraw)):
                pe.wait_ge(proj_ev, n + 2)
                for b in range(2):
                    m = pe.matmul(bank(4 + 2 * n + b), con("rot"), raw[:, b * 512:(b + 1) * 512], start=True, stop=True)
                m.then_inc(rot_ps, 1)
            for n in range(2):
                ws = [arrived(pe, pc) for pc in pc_ada2[4 * n:4 * n + 4]]
                for k in range(KD):
                    for j, w in enumerate(ws):
                        m = pe.matmul(bank(n)[32 * j:32 * j + 32, :], cond32[:, k, :], w[:, k, :], start=(k == 0), stop=(k == KD - 1),
                                      tile_position=(0, 32 * j))
                m.then_inc(ada_ps, 1)

        def act_s2(act, o):
            act_tables(act, o, 0)
            act.wait_ge(proj_ps, 1)
            o(act.copy(uT.rearrange("p c s -> p (c s)"), bank(4, 2)), proj_ev)
            for n, raw in enumerate((qraw, kraw)):
                act_tables(act, o, 1 + n)
                act.wait_ge(proj_ps, 2 + n)
                o(act.copy(raw, bank(6 if n == 0 else 0, 2)), proj_ev)
            act_tables(act, o, 3)
            act.wait_ge(proj_ps, 4)
            o(act.copy(vN.rearrange("p t n -> p (t n)"), bank(2, 2)), proj_ev)
            act.wait_ge(ada_ps, 8)
            o(act.copy(adaS[:, 0:512], bank(0)), rows_ready)
            o(act.copy(adaS[0:64, 512:1024], bank(1)[0:64, :]), rows_ready)

        def dve_s2(dve, o):
            dve.wait_ge(rope_tab, 1)
            for n, (raw, dst) in enumerate(((qraw, qT), (kraw, kT))):
                dve.wait_ge(rot_ps, n + 1)
                o(dve.tensor_tensor(dst, raw.rearrange("p (c s) -> p c s", c=4), rows_bc(cosR, 4), ALU.mult))
                o(dve.tensor_tensor(rtmp, bank(4 + 2 * n, 2).rearrange("p (c s) -> p c s", c=4), rows_bc(sinR, 4), ALU.mult))
                o(dve.tensor_tensor(dst, dst, rtmp, ALU.add), rope_done)

        def at(i):
            return (i % 2) * 2 + i // 2

        def probs_of(n):
            return prob3[(n - 4) % 3] if 4 <= n < 10 else prob[n % 2]

        def pe_scores(pe, u, q_of, k_of, bias=None):
            if bias is not None:
                for a in range(2):
                    pe.matmul(bank(2 * (u % 2) + a), con("flip"), bias[:, 2 * a:2 * a + 2, :], start=True, stop=False, skip_group_check=True)
            for i in range(HPG):
                m = pe.matmul(bank(2 * (u % 2) + i % 2)[:, (i // 2) * SEQ:(i // 2 + 1) * SEQ], q_of(i), k_of(i), start=bias is None, stop=True,
                              skip_group_check=bias is not None)
            m.then_inc(sc_ps, 1)

        def pe_probs(pe, u, n, v_of):
            pe.wait_ge(pr_ready, n + 1)
            if n:
                pe.wait_ge(prT_ready, n)
            for kb in range(2):
                for i in range(HPG):
                    m = pe.transpose(bank(4 + kb)[:, i * P:(i + 1) * P], probs_of(n)[:, at(i) * SEQ + kb * P:at(i) * SEQ + (kb + 1) * P], ident)
            m.then_inc(prT_ps, 1)
            pe.wait_ge(prT_ready, n + 1)
            if n >= 2:
                pe.wait_ge(pv_ev, n - 1)
            for i in range(HPG):
                for kb in range(2):
                    r = HD * (i % 2)
                    m = pe.matmul(bank(6 + n % 2)[r:r + HD, (i // 2) * P:(i // 2 + 1) * P], v_of(kb, i),
                                  prT[n % 2][:, kb * 512 + i * P:kb * 512 + (i + 1) * P], start=(kb == 0), stop=(kb == 1))
            m.then_inc(pv_ps, 1)

        def dve_softmax(dve, o, u, n, scale, bias, weigh=None):
            S = probs_of(n)
            s3 = S.rearrange("p (h k) -> p h k", h=HPG)
            dve.wait_ge(sc_ps, n + 1)
            if n >= 2:
                dve.wait_ge(prT_ps, n - 1)
            if bias is None:
                o(dve.tensor_scalar(S, bank(2 * (n % 2), 2), scale, None, ALU.mult), sc_read)
            else:
                o(dve.scalar_tensor_tensor(s3, bank(2 * (n % 2), 2).rearrange("p (h k) -> p h k", h=HPG), scale, bias,
                                           ALU.mult, ALU.add), sc_read)
            o(dve.tensor_reduce(amax, s3, AX.X, ALU.max))
            o(dve.tensor_tensor(s3, s3, cols_bc(amax, SEQ), ALU.subtract), sc_sub)
            dve.wait_ge(sc_exp, n + 1)
            o(dve.tensor_reduce(aden, s3, AX.X, ALU.add))
            o(dve.reciprocal(aden, aden))
            if weigh is not None:
                weigh()
            o(dve.tensor_tensor(s3, s3, cols_bc(aden, SEQ), ALU.mult), pr_ready)

        def dve_pv(dve, o, u, n, dst):
            dve.wait_ge(pv_ps, n + 1)
            o(dve.tensor_copy(dst, bank(6 + n % 2)[:, 0:SEQ].rearrange("p (c m) -> p c m", c=2)), pv_ev)

        def act_probs(act, o, u, n):
            act.wait_ge(sc_sub, n + 1)
            o(act.activation(probs_of(n), probs_of(n), ACT.Exp), sc_exp)
            act_probsT(act, o, n)

        def act_probsT(act, o, n):
            act.wait_ge(prT_ps, n + 1)
            if n >= 2:
                act.wait_ge(pv_ps, n - 1)
            o(act.copy(prT[n % 2], bank(4, 2)), prT_ready)

        U1 = [(g, t) for g in range(HEADS // HPG) for t in range(TT)]

        def pe_s4(pe):
            def scores(u):
                g, t = U1[u]
                pe.wait_ge(rope_done, 2)
                pe.wait_ge(rows_ready, 2)
                if u == 1:
                    pe.wait_ge(proj_ev, 4)
                if u >= 2:
                    pe.wait_ge(sc_read, u - 1)
                def half(x, i):
                    return x[HD * (i % 2):HD * (i % 2) + HD, 2 * g + i // 2, :]
                pe_scores(pe, u, lambda i: half(qT, i)[:, t * P:(t + 1) * P], lambda i: half(kT, i))
            scores(0)
            for u, (g, t) in enumerate(U1):
                if u + 1 < len(U1):
                    scores(u + 1)
                pe_probs(pe, u, u, lambda kb, i: vN[:, kb, (HPG * g + i) * HD:(HPG * g + i + 1) * HD])

        def act_s4(act, o):
            for u in range(len(U1)):
                act_probs(act, o, u, u)

        def dve_s4(dve, o):
            for u, (g, t) in enumerate(U1):
                causal = spread(con("causal")[:, t * SEQ:(t + 1) * SEQ], [0, HPG], [1, SEQ])
                dve_softmax(dve, o, u, u, HD ** -0.5, causal)
                if u:
                    g0, t0 = U1[u - 1]
                    dve_pv(dve, o, u - 1, u - 1, yaT[:, 2 * g0:2 * g0 + 2, t0 * P:(t0 + 1) * P])
            dve_pv(dve, o, u, u, yaT[:, 2 * g:2 * g + 2, t * P:(t + 1) * P])

        def pe_s3(pe):
            def drive(q):
                if q:
                    pe.wait_ge(bu_read, q)
                for n, m_ in enumerate((BTr, BTi)):
                    for j in range(4):
                        m = pe.matmul(bank(j)[:, n * SEQ:(n + 1) * SEQ], m_[32 * j:32 * j + 32, q, :],
                                      uT[32 * j:32 * j + 32, q, :], start=True, stop=True, tile_position=(32 * j, 0))
                m.then_inc(bu_ps, 1)
            pe.wait_ge(sc_read, len(U1))
            pe.wait_ge(pv_ev, len(U1))
            def gate(i):
                n, t = i // TT, i % TT
                if i >= 2:
                    pe.wait_ge(gate_ready, i - 1)
                w = arrived(pe, pc_gate[n])
                for k in range(KD):
                    m = pe.matmul(bank(4 + t), hT[:, k, t * P:(t + 1) * P], w[:, k, :], start=(k == 0), stop=(k == KD - 1))
                m.then_inc(gate_ps, 1)

            def y_of(q):
                pe.wait_ge(st_ready, q + 1)
                if q >= 2:
                    pe.wait_ge(y_ready, q - 1)
                for j in range(4):
                    for n, (c_, x_) in enumerate(((CTr, sT), (CTi, sU))):
                        m = pe.matmul(bank(6 + q % 2)[32 * j:32 * j + 32, 0:SEQ], c_[:, q, 32 * j:32 * j + 32], x_[:, j, :],
                                      start=(n == 0), stop=(n == 1), tile_position=(0, 32 * j))
                m.then_inc(y_ps, 1)
            drive(0)
            gate(0)
            gate(1)
            for q in range(SQ - 1):
                drive(q + 1)
                gate(2 + 2 * q)
                y_of(q)
                gate(3 + 2 * q)
            y_of(SQ - 1)
            pe.wait_ge(bu_read, SQ)
            pe_branch(pe, pc_wa, yaT, 0)
            pe.wait_ge(gate_ready, 8)
            pe.wait_ge(gel_ready, 1)
            pe_cols(pe, arrived(pe, pc_glu), 4, gel, SQ, out_ps)

        def pe_branch(pe, pc, src, b0):
            w = arrived(pe, pc)
            for t in range(TT):
                for c in range(2):
                    for k in range(4):
                        m = pe.matmul(bank(b0 + 2 * t + c), src[:, k, t * P:(t + 1) * P], w[:, k, c * 512:(c + 1) * 512],
                                      start=(k == 0), stop=(k == 3))
            m.then_inc(out_ps, 1)

        def act_s3(act, o):
            for i in range(4 * TT):
                n, t = i // TT, i % TT
                act.wait_ge(gate_ps, i + 1)
                dst = (sgs if n < 2 else sga)[:, t, (n % 2) * 512:(n % 2 + 1) * 512]
                o(act.activation(dst, bank(4 + t), ACT.Sigmoid), gate_ready)
            act.wait_ge(y_ready, SQ)
            o(act.activation(gel.rearrange("p q s -> p (q s)"), yT.rearrange("p q s -> p (q s)"), ACT.Gelu_apprx_tanh), gel_ready)
            act.wait_ge(out_ps, 2)
            o(act.activation(sglu.rearrange("p q s -> p (q s)"), bank(4, 2), ACT.Sigmoid), gel_ready)

        def dve_s3(dve, o):
            dve.wait_ge(tab_ready, 8)

            def y_out(q):
                dve.wait_ge(y_ps, q + 1)
                o(dve.scalar_tensor_tensor(yT[:, q, :], uT[:, q, :], dcol[:, q:q + 1], bank(6 + q % 2)[:, 0:SEQ],
                                           ALU.mult, ALU.add), y_ready)
            for q in range(SQ):
                cq, sq = cosS[:, 4 * q:4 * q + 4, :], sinS[:, 4 * q:4 * q + 4, :]
                re, im = (bank(0, 4).rearrange("p (j c s) -> p j c s", j=4, c=2)[:, :, n, :] for n in range(2))
                dve.wait_ge(bu_ps, q + 1)
                if q:
                    y_out(q - 1)
                o(dve.tensor_tensor(sA, re, cq, ALU.mult))
                o(dve.tensor_tensor(sT, im, sq, ALU.mult))
                o(dve.tensor_tensor(sA, sA, sT, ALU.add))
                o(dve.tensor_tensor(sB, im, cq, ALU.mult))
                o(dve.tensor_tensor(sT, re, sq, ALU.mult), bu_read)
                o(dve.tensor_tensor(sB, sB, sT, ALU.subtract))
                for x_ in (sA, sB):
                    for j in range(4):
                        o(dve.tensor_tensor_scan(x_[:, j, :], cols_bc(mag[:, 4 * q + j], SEQ), x_[:, j, :], 0.0, ALU.mult, ALU.add))
                o(dve.tensor_tensor(sT, sA, cq, ALU.mult))
                o(dve.tensor_tensor(sU, sB, sq, ALU.mult))
                o(dve.tensor_tensor(sT, sT, sU, ALU.subtract))
                o(dve.tensor_tensor(sU, sA, sq, ALU.mult))
                o(dve.tensor_tensor(sB, sB, cq, ALU.mult))
                o(dve.scalar_tensor_tensor(sU, sU, -1.0, sB, ALU.mult, ALU.subtract), st_ready)
            y_out(SQ - 1)
            dve.wait_ge(out_ps, 1)
            dve.wait_ge(gate_ready, 8)
            for t in range(TT):
                o(dve.tensor_tensor(mgd[:, t, :], sga[:, t, :], bank(2 * t, 2), ALU.mult))
            dve.wait_ge(gel_ready, 2)
            o(dve.tensor_tensor(ysT, gel, sglu, ALU.mult), ys_ready)

        def pe_s5(pe):
            pe.wait_ge(ys_ready, 1)
            pe_branch(pe, pc_ws, ysT, 4)
            pe_turn(pe, mgd, "merged")
            pe_after_turn(pe, "merged")

            def mod_rows(blocks):
                for n in blocks:
                    j = 32 * (n % 4)
                    one = CON[j:j + 1, names["ones"][0]:names["ones"][0] + P]
                    m = pe.matmul(bank(n % 4), one, adaS[j:j + 1, n // 4 * 512:(n // 4 + 1) * 512], start=True, stop=True, tile_position=(j, 0))
                m.then_inc(mod_ps, 1)
            pe_rows(pe, arrived(pe, pc_out[0]), (4, 6), mgT, KD, out_ps)
            mod_rows(range(4))
            pe_rows(pe, arrived(pe, pc_out[1]), (5, 7), mgT, KD, out_ps)
            pe.wait_ge(mod_read, 1)
            mod_rows(range(4, 6))

        def dve_s5(dve, o):
            dve.wait_ge(out_ps, 3)
            for t in range(TT):
                o(dve.tensor_tensor(mtmp, sgs[:, t, :], bank(4 + 2 * t, 2), ALU.mult))
                o(dve.tensor_tensor(mgd[:, t, :], mgd[:, t, :], mtmp, ALU.add), nat_ready)
            dve.wait_ge(rout_in, 16 * 7)
            dve.wait_ge(mod_ps, 1)
            o(dve.tensor_tensor(Bf, Bf, bank(0, 2), ALU.add))
            o(dve.scalar_tensor_tensor(Af, bank(2, 2), 1.0, Af, ALU.add, ALU.add), mod_read)
            o(dve.tensor_tensor(Af, Af, gpre2, ALU.mult))
            dve.wait_ge(mod_ps, 2)
            o(dve.tensor_tensor(GTf, GTf, bank(0, 2), ALU.add))
            o(dve.tensor_tensor(GTf, GTf, gpost2, ALU.mult))
            dve_rms(dve, o, 2)
            for t in range(TT):
                o(dve.scalar_tensor_tensor(mtmp, bank(4 + 2 * t, 2), rms[:, t:t + 1], GTm, ALU.mult, ALU.mult))
                o(dve.tensor_tensor(x3[:, t, :], x3[:, t, :], mtmp, ALU.add), x1_ready)

        def act_s5(act, o):
            act_turned(act, o, mgT, "merged")
            act.wait_ge(out_ps, 5)
            act_rms(act, o, [bank(4 + 2 * t, 2) for t in range(TT)], ar(10240, D), 2)
        FIRST = len(pieces)
        E_SLOT = [(FIRST + i) % SLOTS for i in range(SLOTS)]
        E_USED = [filled[s] for s in E_SLOT]
        assert SLOTS == 6
        rout_in = sem("rout_in")
        (mk_ready, pos_ready, wT_ready, bias_in) = (sem(n) for n in (
            "mk_ready", "pos_ready", "wT_ready", "bias_in"))
        ff_ps, x2_ready = sem("ff_ps"), sem("x2_ready")

        class Steps:

            def __init__(self, kind):
                self.p_ready = sem(kind + "_p_ready")
                self.pw_ready = sem(kind + "_pw_ready")
                self.x_ps = sem(kind + "_x_ps")
                self.x_ready = sem(kind + "_x_ready")
                self.pwT_ps = sem(kind + "_pwT_ps")
                self.pwT_ready = sem(kind + "_pwT_ready")
                self.g_ps = sem(kind + "_g_ps")
                self.u_ps = sem(kind + "_u_ps")
                self.gm_ready = sem(kind + "_gm_ready")
                self.sg_ready = sem(kind + "_sg_ready")
                self.a_ready = sem(kind + "_a_ready")
                self.aT_ps = sem(kind + "_aT_ps")
                self.aT_ready = sem(kind + "_aT_ready")
                self.d_ps = sem(kind + "_d_ps")
                self.y_out = sem(kind + "_y_out")
                self.s_ps = sem(kind + "_s_ps")

        main, extra = Steps("first"), Steps("further")

        Bf, Af, GTf = ar(0, D), ar(D, D), ar(3072, D)
        gpre2, gpost2 = ar(11264, D), ar(12288, D)
        h2 = ar3(6144, 2048, TT)
        h2T = ar3(8192, 2048, KD)
        rw, rb = ar3(13312, 256, KD), ar(13568, E)
        lg, top8, idx8, idxf = ar3(13600, 64, TT), ar3(13664, 16, TT), ar3(13680, 16, TT), ar3(13696, 16, TT)
        ew, esum, eqt = ar3(13712, 8, TT), ar(13720, TT), ar(13728, E)
        mk, wt, posm = ar3(13792, 64, TT), ar3(13856, 64, TT), ar3(13920, 64, TT)
        cnt = ar(14016, E).bitcast(i32)
        wT = ar(14048, SEQ, E)
        bgs, bus, bds = ar(14336, FF, E), ar(15360, FF, E), ar(16384, D, E)
        Psel, Pw = ar3(17408, 256, TT), ar3(17664, 256, TT)
        PwT, Ee = ar(17920, SEQ), ar(18176, CAP, E)
        XT = ar3(18432, 1024, KD)
        gm, um, sg, act_, actT, Yb = (ar(19456 + 512 * n, 512) for n in range(6))

        def pool_s6(pool):
            pool.wait_ge(out_ps, 3)
            for n, d in enumerate((Bf, Af, GTf)):
                dma(pool, d, row(A["ada_b"][0][(3 + n) * D:(4 + n) * D]), rout_in)
            dma(pool, gpre2, row(A["ffn_pre_g"][0]), rout_in)
            dma(pool, gpost2, row(A["ffn_post_g"][0]), rout_in)
            dma(pool, rw, A["router_w"][0].rearrange("(k p) e -> p k e", p=P), rout_in)
            dma(pool, rb, row(A["router_b"][0]), rout_in)
            pool.wait_ge(x1_ready, 1)
            for d, a in ((bgs, "b_gate"), (bus, "b_up"), (bds, "b_down")):
                dma(pool, d, A[a][0], bias_in)

        def pe_s6(pe):
            pe_turn(pe, h2, "experts")
            pe_after_turn(pe, "experts")
            pe.wait_ge(rout_in, 16 * 7)
            for t in range(TT):
                for k in range(KD):
                    m = pe.matmul(bank(6)[:, t * E:(t + 1) * E], h2T[:, k, t * P:(t + 1) * P], rw[:, k, :],
                                  start=(k == 0), stop=(k == KD - 1))
            m.then_inc(router_ps, 1)
            pe.wait_ge(mk_ready, 1)
            pe.matmul(bank(7)[:, 0:E], con("before"), mk[:, 0, :], start=True, stop=True)
            pe.matmul(bank(7)[:, E:2 * E], con("before"), mk[:, 1, :], start=True, stop=False)
            pe.matmul(bank(7)[:, E:2 * E], con("ones"), mk[:, 0, :], start=False, stop=True)
            for t in range(TT):
                m = pe.matmul(bank(7)[:, 2 * E:3 * E], con("ones"), mk[:, t, :], start=(t == 0), stop=(t == 1))
            m.then_inc(router_ps, 1)
            for t in range(TT):
                m = pe.transpose(bank(0, 1, E)[:, t * P:(t + 1) * P], wt[:, t, :], ident)
            m.then_inc(router_ps, 1)
            pe.wait_ge(wT_ready, 1)
            pe.wait_ge(pos_ready, 1)
            pe.wait_ge(bias_in, 48)
            for t in range(TT):
                for d in range(2):
                    m = pe.matmul(bank(4 + 2 * t + d), wT[:, t * P:(t + 1) * P], bds[:, d * 512:(d + 1) * 512],
                                  start=True, stop=False, skip_group_check=True)
            m.then_inc(extra.s_ps, 1)

        def act_s6(act, o):
            act.wait_ge(x1_ready, 2)
            act_rms(act, o, [x3[:, t, :] for t in range(TT)], ar(10240, D), 3)
            act_turned(act, o, h2T, "experts")
            act.wait_ge(fn_asked, 1)
            o(act.activation(ew, ew, ACT.Exp), fn_done)
            act.wait_ge(router_ps, 3)
            o(act.copy(wT, bank(0, 1, E)[:, 0:SEQ]), wT_ready)

        def dve_s6(dve, o):
            dve_rms(dve, o, 3)
            for t in range(TT):
                o(dve.scalar_tensor_tensor(h2[:, t, :], x3[:, t, :], rms[:, t:t + 1], Af, ALU.mult, ALU.mult))
                o(dve.tensor_tensor(h2[:, t, :], h2[:, t, :], Bf, ALU.add), nat_ready)
            dve.wait_ge(router_ps, 1)
            o(dve.tensor_tensor(lg, bank(6)[:, 0:2 * E].rearrange("p (t e) -> p t e", t=TT), rows_bc(rb, TT), ALU.add))
            for t in range(TT):
                o(dve.max(top8[:, t, :], lg[:, t, :]))
                o(dve.max_index(idx8[:, t, :].bitcast(u32), top8[:, t, :], lg[:, t, :]))
            o(dve.tensor_copy(idxf, idx8.bitcast(u32)))
            for t in range(TT):
                o(dve.tensor_scalar(ew[:, t, :], top8[:, t, 0:TOPK], top8[:, t, 0:1], None, ALU.subtract),
                  fn_asked if t == TT - 1 else None)
            for t in range(TT):
                o(dve.tensor_scalar(mk[:, t, :], con("experts"), idxf[:, t, 0:1], None, ALU.is_equal))
                for k in range(1, TOPK):
                    o(dve.scalar_tensor_tensor(mk[:, t, :], con("experts"), idxf[:, t, k:k + 1], mk[:, t, :], ALU.is_equal, ALU.add))
            dve.wait_ge(fn_done, 1)
            o(dve.tensor_reduce(esum, ew, AX.X, ALU.add))
            o(dve.reciprocal(esum, esum))
            o(dve.tensor_tensor(ew, ew, cols_bc(esum, TOPK), ALU.mult))
            for t in range(TT):
                o(dve.tensor_scalar(wt[:, t, :], con("experts"), idxf[:, t, 0:1], ew[:, t, 0:1], ALU.is_equal, ALU.mult))
                for k in range(1, TOPK):
                    o(dve.tensor_scalar(eqt, con("experts"), idxf[:, t, k:k + 1], ew[:, t, k:k + 1], ALU.is_equal, ALU.mult))
                    last = dve.tensor_tensor(wt[:, t, :], wt[:, t, :], eqt, ALU.add)
                    o(last, mk_ready if (t, k) == (TT - 1, TOPK - 1) else None)
            dve.wait_ge(router_ps, 2)
            o(dve.scalar_tensor_tensor(posm, bank(7)[:, 0:2 * E].rearrange("p (t e) -> p t e", t=TT), 1.0, mk, ALU.add, ALU.mult))
            o(dve.tensor_scalar(posm, posm, -1.0, None, ALU.add))
            o(dve.tensor_copy(cnt, bank(7)[:, 2 * E:3 * E]), pos_ready)

        W7 = [RING[:, i * SLOT_W:(i + 1) * SLOT_W] for i in E_SLOT]
        gate_w = [W7[h].rearrange("p (k n) -> p k n", k=KD) for h in range(2)]
        up_w = [W7[2 + h].rearrange("p (k n) -> p k n", k=KD) for h in range(2)]
        down_w = [W7[4 + h].rearrange("p (k n) -> p k n", k=4) for h in range(2)]

        def slot_iota(r, n):
            a = names["slots"][0] + r * 2 * CAP
            return CON[:, a:a + n]

        def dve_round(dve, s, n, e, r):
            for t in range(TT):
                dve.tensor_scalar(Psel[:, t, :], slot_iota(r, 2 * CAP), posm[:, t, bass.ds(e, 1)], None, ALU.is_equal)
            dve.drain()
            dve.tensor_copy(Ee, ident[0:E, bass.ds(e, 1)].to_broadcast([E, CAP])).then_inc(s.p_ready, 1)
            for t in range(TT):
                m = dve.tensor_scalar(Pw[:, t, :], slot_iota(r, 2 * CAP), posm[:, t, bass.ds(e, 1)], wt[:, t, bass.ds(e, 1)],
                                      ALU.is_equal, ALU.mult)
                if t == 0:
                    dve.drain()
            m.then_inc(s.pw_ready, 1)
            dve.wait_ge(s.g_ps, n)
            dve.tensor_scalar(gm, bank(0), LIMIT, None, ALU.min).then_inc(s.gm_ready, 1)
            dve.wait_ge(s.u_ps, n)
            dve.tensor_scalar(um, bank(1), LIMIT, -LIMIT, ALU.min, ALU.max)
            dve.drain()
            dve.scalar_tensor_tensor(um, um, 1.0, gm, ALU.add, ALU.mult)
            dve.drain()
            dve.wait_ge(s.sg_ready, n)
            dve.tensor_tensor(act_, um, sg, ALU.mult).then_inc(s.a_ready, 1)

        def act_round(act, s, n):
            act.wait_ge(s.x_ps, n)
            act.copy(XT.rearrange("p k m -> p (k m)"), bank(2, 2)).then_inc(s.x_ready, 1)
            act.wait_ge(s.pwT_ps, n)
            act.copy(PwT, bank(3)[:, 0:SEQ]).then_inc(s.pwT_ready, 1)
            act.wait_ge(s.gm_ready, n)
            act.activation(sg, gm, ACT.Sigmoid, scale=ALPHA).then_inc(s.sg_ready, 1)
            act.wait_ge(s.aT_ps, n)
            act.copy(actT, bank(3)).then_inc(s.aT_ready, 1)
            act.wait_ge(s.d_ps, n)
            act.copy(Yb, bank(2)).then_inc(s.y_out, 1)

        def pe_round(pe, s, n, weights):
            pe.wait_ge(s.p_ready, n)
            for k in range(KD):
                for t in range(TT):
                    m = pe.matmul(bank(2 + k // 4)[:, (k % 4) * P:(k % 4 + 1) * P], h2[:, t, k * P:(k + 1) * P], Psel[:, t, :],
                                  start=(t == 0), stop=(t == 1))
            m.then_inc(s.x_ps, 1)
            pe.wait_ge(s.pw_ready, n)
            pe.wait_ge(s.x_ready, n)
            for t in range(TT):
                m = pe.transpose(bank(3)[:, t * P:(t + 1) * P], Pw[:, t, :], ident)
            m.then_inc(s.pwT_ps, 1)
            for i, (w, b_, done) in enumerate(((gate_w, bgs, s.g_ps), (up_w, bus, s.u_ps))):
                weights(i)
                for k in range(KD):
                    for h in range(2):
                        pe.matmul(bank(i)[h * CAP:(h + 1) * CAP, :], XT[:, k, 0:CAP], w[h][:, k, :], start=(k == 0), stop=False)
                for h in range(2):
                    m = pe.matmul(bank(i)[h * CAP:(h + 1) * CAP, :], Ee, b_[:, h * 512:(h + 1) * 512], start=False, stop=True)
                m.then_inc(done, 1)
            pe.wait_ge(s.a_ready, n)
            pe.wait_ge(s.pwT_ready, n)
            for j in range(4):
                m = pe.transpose(bank(3)[:, j * P:(j + 1) * P], act_[:, j * P:(j + 1) * P], ident)
            m.then_inc(s.aT_ps, 1)
            weights(2)
            pe.wait_ge(s.aT_ready, n)
            for h in range(2):
                for j in range(4):
                    for d in range(2):
                        m = pe.matmul(bank(2)[d * CAP:(d + 1) * CAP, :], actT[:, j * P + h * CAP:j * P + (h + 1) * CAP],
                                      down_w[h][:, j, d * 512:(d + 1) * 512], start=(h + j == 0), stop=(h + j == 4))
            m.then_inc(s.d_ps, 1)
            pe.wait_ge(s.y_out, n)
            for t in range(TT):
                for d in range(2):
                    m = pe.matmul(bank(4 + 2 * t + d), PwT[d * CAP:(d + 1) * CAP, t * P:(t + 1) * P], Yb[d * CAP:(d + 1) * CAP, :],
                                  start=False, stop=False, skip_group_check=True)
            m.then_inc(s.s_ps, 1)

        def further(eng, e, rounds_of, body=None):
            n_e = eng.value_load(cnt[0:1, bass.ds(e, 1)], min_val=0, max_val=SEQ)

            def deeper(r):
                with eng.If(n_e > r * CAP):
                    eng.reg_add(rounds_of, rounds_of, 1)
                    if body is not None:
                        body(r, eng.snap(rounds_of))
                    if r + 1 < ROUNDS:
                        deeper(r + 1)
            deeper(1)

        def expert_rounds(eng, first_round, extra_round):
            eng.wait_ge(pos_ready, 1)
            taken = eng.alloc_register(f"further_{eng.engine.name}")
            eng.reg_mov(taken, 0)
            with eng.Fori(0, E) as e:
                first_round(e)
                further(eng, e, taken, lambda r, n: extra_round(e, r, n))

        def pe_s7(pe):
            def first(e):
                def weights(i):
                    for h in range(2):
                        n = 2 * i + h
                        pe.wait_ge(slot_ready[E_SLOT[n]], e * 16 + 16 * (E_USED[n] + 1))
                pe_round(pe, main, e + 1, weights)
            expert_rounds(pe, first, lambda e, r, n: pe_round(pe, extra, n, lambda i: None))
            pe.wait_ge(main.y_out, E)

        def dve_s7(dve):
            expert_rounds(dve, lambda e: dve_round(dve, main, e + 1, e, 0), lambda e, r, n: dve_round(dve, extra, n, e, r))

        def act_s7(act):
            expert_rounds(act, lambda e: act_round(act, main, e + 1), lambda e, r, n: act_round(act, extra, n))

        def load_expert(sp, e, free):
            for i, name in enumerate(("w_gate", "w_up")):
                free(i)
                for h in range(2):
                    w = A[name][0][e, :, h * 512:(h + 1) * 512] if isinstance(e, int) else A[name][0][bass.ds(e, 1), :, h * 512:(h + 1) * 512]
                    w = w.rearrange("(k p) n -> p k n", p=P) if isinstance(e, int) else w.rearrange("a (k p) n -> p (a k) n", p=P)
                    sp.dma_start((gate_w, up_w)[i][h], w).then_inc(slot_ready[E_SLOT[2 * i + h]], 16)
            free(2)
            for h in range(2):
                w = A["w_down"][0][e, h * 512:(h + 1) * 512, :] if isinstance(e, int) else A["w_down"][0][bass.ds(e, 1), h * 512:(h + 1) * 512, :]
                w = w.rearrange("(k p) n -> p k n", p=P) if isinstance(e, int) else w.rearrange("a (k p) n -> p (a k) n", p=P)
                sp.dma_start(down_w[h], w).then_inc(slot_ready[E_SLOT[4 + h]], 16)

        def sp_s7(sp):
            def free_first(i):
                for h in range(2):
                    used = pieces[FIRST - SLOTS + 2 * i + h]
                    sp.wait_ge(used[1], used[2])
            load_expert(sp, 0, free_first)
            sp.wait_ge(pos_ready, 1)
            taken = sp.alloc_register("further_SP")
            sp.reg_mov(taken, 1)
            with sp.Fori(1, E) as e:
                further(sp, e - 1, taken)

                def free(i):
                    sp.wait_ge((main.g_ps, main.u_ps, main.d_ps)[i], e)
                    if i == 0:
                        sp.wait_ge(extra.s_ps, taken)
                load_expert(sp, e, free)

        def post(dve, o, n, b0, gain, tells, tmp):
            dve_rms(dve, o, n)
            for t in range(TT):
                o(dve.scalar_tensor_tensor(tmp, bank(b0 + 2 * t, 2), rms[:, t:t + 1], gain, ALU.mult, ALU.mult))
                o(dve.tensor_tensor(x3[:, t, :], x3[:, t, :], tmp, ALU.add), tells)

        def act_s8(act, o):
            act.wait_ge(ff_ps, 1)
            act.wait_ge(bv_stored, 16)
            act_rms(act, o, [bank(4 + 2 * t, 2) for t in range(TT)], ar(10240, D), 4)

        def dve_s8(dve, o):
            post(dve, o, 4, 4, GTf, x2_ready, ar(4096, D))

        def pe_s8(pe):
            for t in range(TT):
                for d in range(2):
                    m = pe.matmul(bank(4 + 2 * t + d), con("zero_rows", E), bds[:, d * 512:(d + 1) * 512],
                                  start=False, stop=True, skip_group_check=True)
            m.then_inc(ff_ps, 1)
        (mem_in, mkv_ps, mkv_ready, gain_in) = (sem(n) for n in (
            "mem_in", "mkv_ps", "mkv_ready", "gain_in"))
        (post_done, gu_ps, gu_silu, gu_done, dn_ps, ffn_done) = (sem(n) for n in (
            "post_done", "gu_ps", "gu_silu", "gu_done", "dn_ps", "ffn_done"))
        (hot_in, bv_ready, bv_stored, bm_in) = (sem(n) for n in (
            "hot_in", "bv_ready", "bv_stored", "bm_in"))
        out_stored, neg_ready = sem("out_stored"), sem("neg_ready")
        pc_at_ffn = []
        pc_mem, pc_ao, pc_gu, pc_dn = [], [], [], []
        MOE_PIECES = SLOTS
        LAST = FIRST + MOE_PIECES

        def moe_last():
            for i in range(SLOTS):
                pieces.append((None, (main.g_ps, main.u_ps, main.d_ps)[i // 2], E))
                filled[i] += E
        moe_last()
        def layer_pieces(i):
            pc_mem.append(piece(by_k(A["mem_w_kv_2"][i], 0, 2 * MW), mkv_ps, i + 1))
            if i == 0:
                w = A["att_w_in_2"][0]
                pc_at.extend(piece(by_k(w, n * 512, n * 512 + 512), proj_ps, 4 + n + 1) for n in range(5))
                w = A["att_w_out_2"][0]
            else:
                w = A["dn_w_in_2"][0]
                pc_dw.extend(piece(by_k(w, n * 512, min(n * 512 + 512, w.shape[1])), proj_ps, 10 + i_) for i_, n in enumerate((6, 0, 1, 2, 3, 4, 5)))
                w = A["dn_w_out_2"][0]
            pc_ao.append([piece(by_k(w, n * 512, n * 512 + 512), out_ps, 5 + 2 * i + n + 1) for n in range(2)])
            w = A["ffn_w_gate_up_2"][i]
            pc_gu.append([piece(by_k(w, n * 512, n * 512 + 512), gu_ps, 11 * i + n + 1) for n in range(11)])
            w = A["ffn_w_down_2"][i].rearrange("(k p) n -> p k n", p=P)
            pc_dn.append([piece(w[:, n * 4:min(n * 4 + 4, FC2), :], dn_ps, 6 * i + n + 1) for n in range(6)])
        pc_at, pc_dw = [], []
        layer_pieces(0)
        layer_pieces(1)

        gA, gB = ar(2048, D), ar(3072, D)
        hn = ar3(6144, 2048, TT)
        yA = ar3(6144, 2048, KD)
        hT2 = ar3(8192, 2048, KD)
        mem_nat, mem_n, mem_T, mem_g = ar3(15360, 2048, TT), ar3(17408, 2048, TT), ar3(19456, 2048, KD), ar(4096, D)
        kmT, vm = ar3(21504, 512, 2), ar3(22016, 512, TT)
        prob3 = [ar(4096, 1024), ar(5120, 1024), ar(8192, 1024)]
        qkA = ar3(10240, 3072, 12)
        vA = ar3(13312, 1536, TT)
        qmA = ar3(14848, 512, 2)
        BM = [[ar3(15360 + 1024 * (3 * t + g), 1024, HPG) for g in range(3)] for t in range(TT)]
        hotS, relS, bvS = ar(8192, 3 * 2 * SEQ, BUCKETS + 1), ar(9728, ATT_HEADS, BUCKETS + 1), ar3(10240, 1536, 3)[0:HPG]
        mx3, dn3, em3, mxx = ar3(9216, 12, 3), ar3(9228, 12, 3), ar3(9240, 12, 3), ar(9252, HPG)
        actF = ar3(10240, FC2 * SEQ, FC2)
        sil = [ar(16384, 512), ar(16896, 512)]
        tmpP = ar(4096, D)
        tmpJ = ar(5120, D)

        PRE = ("attention", "ffn0", "delta", "ffn1")

        def act_pre(act, o, n_rms, k):
            act_rms(act, o, [x3[:, t, :] for t in range(TT)], tmpJ, n_rms)
            act_turned(act, o, hT2, PRE[k])

        def dve_pre(dve, o, n_rms, k, gains):
            dve_rms(dve, o, n_rms)
            dve.wait_ge(gain_in, 16 * gains)
            for t in range(TT):
                o(dve.scalar_tensor_tensor(hn[:, t, :], x3[:, t, :], rms[:, t:t + 1], gA, ALU.mult, ALU.mult), nat_ready)

        def pe_pre(pe, k):
            pe_turn(pe, hn, PRE[k])
            pe_after_turn(pe, PRE[k])

        def pool_gains(pool, i, names2):
            for d, a in zip((gA, gB), names2):
                dma(pool, d, row(A[a][i]), gain_in)

        def pool_mem(pool, i):
            dma(pool, mem_nat, A["mem_2"][0].rearrange("(t p) d -> p t d", p=P), mem_in)
            dma(pool, mem_g, row(A["mem_norm_2"][i]), mem_in)

        def act_mem(act, o, i, n_rms):
            act.wait_ge(mem_in, 32 * (i + 1))
            act_rms(act, o, [mem_nat[:, t, :] for t in range(TT)], tmpJ, n_rms)
            act_turned(act, o, mem_T, f"memory{i}")
            act.wait_ge(mkv_ps, i + 1)
            o(act.copy(kmT.rearrange("p c s -> p (c s)"), bank(4)))
            o(act.copy(vm.rearrange("p t n -> p (t n)"), bank(5)), mkv_ready)

        def dve_mem(dve, o, i, n_rms):
            dve.wait_ge(mem_in, 32 * (i + 1))
            dve_rms(dve, o, n_rms)
            for t in range(TT):
                o(dve.scalar_tensor_tensor(mem_n[:, t, :], mem_nat[:, t, :], rms[:, t:t + 1], mem_g, ALU.mult, ALU.mult), nat_ready)

        def pe_mem(pe, i):
            pe_turn(pe, mem_n, f"memory{i}")
            pe_after_turn(pe, f"memory{i}")
            w = arrived(pe, pc_mem[i])
            for c in range(2):
                for k in range(KD):
                    pe.matmul(bank(4)[:, c * SEQ:(c + 1) * SEQ], w[:, k, c * P:(c + 1) * P], mem_T[:, k, :], start=(k == 0), stop=(k == KD - 1))
            for t in range(TT):
                for k in range(KD):
                    m = pe.matmul(bank(5)[:, t * MW:(t + 1) * MW], mem_T[:, k, t * P:(t + 1) * P], w[:, k, MW:2 * MW],
                                  start=(k == 0), stop=(k == KD - 1))
            m.then_inc(mkv_ps, 1)

        def half_head(x, c0, i):
            return x[HD * (i % 2):HD * (i % 2) + HD, c0 + i // 2, :]

        def pe_mem_scores(pe, i, qm):
            for t in range(TT):
                n = 10 + 2 * i + t
                pe.wait_ge(sc_read, n - 1)
                pe_scores(pe, n, lambda i_: half_head(qm, 0, i_)[:, t * P:(t + 1) * P], lambda i_: half_head(kmT, 0, i_))

        def pe_mem_probs(pe, i):
            for t in range(TT):
                pe_probs(pe, 10 + 2 * i + t, 10 + 2 * i + t, lambda kb, i_: vm[:, kb, i_ * HD:(i_ + 1) * HD])

        def act_mem_attention(act, o, i):
            for t in range(TT):
                act_probs(act, o, 10 + 2 * i + t, 10 + 2 * i + t)

        def dve_mem_attention(dve, o, i):
            for t in range(TT):
                dve_softmax(dve, o, t, 10 + 2 * i + t, HD ** -0.5, None)
            for t in range(TT):
                dve_pv(dve, o, t, 10 + 2 * i + t, yA[:, 6:8, t * P:(t + 1) * P])

        def pe_out(pe, i):
            for n, pc in enumerate(pc_ao[i]):
                pe_rows(pe, arrived(pe, pc), (4 + n, 6 + n), yA, KD, out_ps)

        def pe_ffn(pe, i):
            pe_pre(pe, 2 * i + 1)
            pe.wait_ge(post_done, 2 * (i + 1))
            for n, pc in enumerate(pc_gu[i]):
                w = arrived(pe, pc)
                if n >= 2:
                    pe.wait_ge(gu_done, 11 * i + n - 1)
                b0 = 4 + 2 * (n % 2)
                for g in range(2):
                    for c in range(2):
                        for k in range(KD):
                            m = pe.matmul(bank(b0 + g)[:, c * SEQ:(c + 1) * SEQ], w[:, k, (2 * g + c) * P:(2 * g + c + 1) * P], hT2[:, k, :],
                                          start=(k == 0), stop=(k == KD - 1))
                m.then_inc(gu_ps, 1)
            for n, pc in enumerate(pc_dn[i]):
                w = arrived(pe, pc)
                if n in (0, 5):
                    pe.wait_ge(gu_done, 11 * i + (10 if n == 0 else 11))
                for j in range(w.shape[1]):
                    f = 4 * n + j
                    for t in range(TT):
                        for d in range(2):
                            m = pe.matmul(bank(2 * t + d), actF[:, f, t * P:(t + 1) * P], w[:, j, d * 512:(d + 1) * 512],
                                          start=(f == 0), stop=(f == FC2 - 1))
                m.then_inc(dn_ps, 1)

        def act_ffn(act, o, i, n_rms):
            act.wait_ge(post_done, 2 * (i + 1))
            act_pre(act, o, n_rms, 2 * i + 1)
            for n in range(11):
                act.wait_ge(gu_ps, 11 * i + n + 1)
                if n >= 2:
                    act.wait_ge(gu_done, 11 * i + n - 1)
                o(act.activation(sil[n % 2], bank(4 + 2 * (n % 2)), ACT.Silu), gu_silu)
            act.wait_ge(dn_ps, 6 * (i + 1))
            act_rms(act, o, [bank(2 * t, 2) for t in range(TT)], tmpJ, n_rms + 1)

        def dve_ffn(dve, o, i, n_rms):
            dve_pre(dve, o, n_rms, 2 * i + 1, 4 * (i + 1))
            for n in range(11):
                dve.wait_ge(gu_silu, 11 * i + n + 1)
                o(dve.tensor_tensor(actF[:, 2 * n:2 * n + 2, :].rearrange("p c s -> p (c s)"), sil[n % 2], bank(5 + 2 * (n % 2)), ALU.mult), gu_done)
            post(dve, o, n_rms + 1, 0, gB, ffn_done, tmpP)

        def pool_ffn(pool, i):
            pool.wait_ge(post_done, 2 * (i + 1))
            pool_gains(pool, i, ("norm_ffn_pre_2", "norm_ffn_post_2"))

        bv_dram = nc.dram_tensor("band_bias", [ATT_HEADS, 2 * SEQ], f32, kind="Internal").ap()

        def pool_bias(pool):
            pool.wait_ge(pos_ready, 1)
            pool.wait_ge(neg_ready, 1)
            dma(pool, hotS, A["k_hot"], hot_in)
            dma(pool, relS[0:BUCKETS, :], A["rel_bias_2"], hot_in)
            pool.wait_ge(bv_ready, 1)
            dma(pool, bv_dram.rearrange("(g h) r -> h g r", g=3), bvS, bv_stored)
            pool.wait_ge(bv_stored, 16)

        def pool_s9(pool):
            pool.wait_ge(x2_ready, 2)
            pool_gains(pool, 0, ("norm_mix_pre_2", "norm_mix_post_2"))
            pool_mem(pool, 0)
            pool.wait_ge(mkv_ready, 1)
            for t in range(TT):
                for g in range(3):
                    for a in range(2):
                        src = bass.AP(bv_dram.tensor, bv_dram.offset + (HPG * g + a) * 2 * SEQ + SEQ - (t + 1) * P,
                                      [[1, P], [2 * 2 * SEQ, 2], [1, SEQ]])
                        dma(pool, BM[t][g][:, 2 * a:2 * a + 2, :], src, bm_in)

        def dve_bias(dve, o):
            o(dve.memset(relS, NEG), neg_ready)

        def pe_bias(pe):
            pe.wait_ge(hot_in, 32)
            for g in range(3):
                m = pe.matmul(bank(g, 1, HPG), relS[:, HPG * g:HPG * g + HPG], hotS[:, g * 2 * SEQ:(g + 1) * 2 * SEQ], start=True, stop=True)
            m.then_inc(router_ps, 1)
            pe.wait_ge(bv_ready, 1)

        def act_bias(act, o):
            act.wait_ge(router_ps, 4)
            o(act.copy(bvS.rearrange("h g r -> h (g r)"), bank(0, 3, HPG)), bv_ready)

        def pe_s9(pe):
            pe.wait_ge(x2_ready, 2)
            pe_mem(pe, 0)
            pe_pre(pe, 0)
            pe.wait_ge(mkv_ready, 1)
            pe_cols(pe, arrived(pe, pc_at[0]), 4, hT2, KD, proj_ps)
            pe_cols(pe, arrived(pe, pc_at[1]), 6, hT2, KD, proj_ps)
            pe_cols(pe, arrived(pe, pc_at[2]), 0, hT2, KD, proj_ps)
            pe_rows(pe, arrived(pe, pc_at[3]), (2, 3), hT2, KD, proj_ps)
            w = arrived(pe, pc_at[4])
            pe.wait_ge(proj_ev, 4 + 1)
            for t in range(TT):
                for k in range(KD):
                    pe.matmul(bank(4)[:, t * SEQ:(t + 1) * SEQ], hT2[:, k, t * P:(t + 1) * P], w[:, k, 0:256], start=(k == 0), stop=(k == KD - 1))
            for c in range(2):
                for k in range(KD):
                    m = pe.matmul(bank(5)[:, c * SEQ:(c + 1) * SEQ], w[:, k, 256 + c * P:256 + (c + 1) * P], hT2[:, k, :], start=(k == 0), stop=(k == KD - 1))
            m.then_inc(proj_ps, 1)
            pe.wait_ge(proj_ev, 4 + 6)
            pe.wait_ge(bm_in, 16 * 12)
            for t in range(TT):
                for g in range(3):
                    n = 4 + 3 * t + g
                    pe.wait_ge(sc_read, n - 1)
                    pe_scores(pe, n, lambda i: half_head(qkA, 2 * g, i)[:, t * P:(t + 1) * P], lambda i: half_head(qkA, 6 + 2 * g, i), BM[t][g])
                for g in range(3):
                    pe_probs(pe, 4 + 3 * t + g, 4 + 3 * t + g, lambda kb, i: vA[:, kb, (HPG * g + i) * HD:(HPG * g + i + 1) * HD])
            pe_mem_scores(pe, 0, qmA)
            pe_mem_probs(pe, 0)
            pe.wait_ge(pv_ev, 12)
            pe_out(pe, 0)

        def act_s9(act, o):
            act_mem(act, o, 0, 5)
            act_pre(act, o, 6, 0)
            for n in range(3):
                act.wait_ge(proj_ps, 4 + n + 1)
                o(act.copy(qkA[:, 4 * n:4 * n + 4, :].rearrange("p c s -> p (c s)"), bank((4, 6, 0)[n], 2)), proj_ev)
            act.wait_ge(proj_ps, 4 + 4)
            o(act.copy(vA[:, :, 0:512], bank(2, 2).rearrange("p (t n) -> p t n", t=TT)), proj_ev)
            act.wait_ge(proj_ps, 4 + 5)
            o(act.copy(vA[:, :, 512:768], bank(4).rearrange("p (t n) -> p t n", t=TT)), proj_ev)
            o(act.copy(qmA.rearrange("p c s -> p (c s)"), bank(5)), proj_ev)
            for t in range(TT):
                for g in range(3):
                    act.wait_ge(sc_sub, 4 + 3 * t + g + 1)
                    b = probs_of(4 + 3 * t + g)
                    o(act.activation(b, b, ACT.Exp), sc_exp)
                act.wait_ge(fn_asked, t + 2)
                o(act.activation(em3, em3, ACT.Exp), fn_done)
                for g in range(3):
                    act_probsT(act, o, 4 + 3 * t + g)
            act_mem_attention(act, o, 0)
            act.wait_ge(out_ps, 7)
            act_rms(act, o, [bank(4 + 2 * t, 2) for t in range(TT)], tmpJ, 7)

        def dve_s9(dve, o):
            dve_mem(dve, o, 0, 5)
            dve_pre(dve, o, 6, 0, 2)
            for t in range(TT):
                for g in range(3):
                    n = 4 + 3 * t + g
                    s3 = probs_of(n).rearrange("p (h k) -> p h k", h=HPG)
                    dve.wait_ge(sc_ps, n + 1)
                    if g == 0:
                        dve.wait_ge(prT_ps, n)
                    o(dve.tensor_scalar(probs_of(n), bank(2 * (n % 2), 2), HD ** -0.5, None, ALU.mult), sc_read)
                    o(dve.tensor_reduce(mx3[:, g, :], s3, AX.X, ALU.max))
                    o(dve.tensor_tensor(s3, s3, cols_bc(mx3[:, g, :], SEQ), ALU.subtract), sc_sub)
                o(dve.tensor_tensor(mxx, mx3[:, 0, :], mx3[:, 1, :], ALU.max))
                o(dve.tensor_tensor(mxx, mxx, mx3[:, 2, :], ALU.max))
                o(dve.tensor_tensor(em3, mx3, rows_bc(mxx, 3), ALU.subtract), fn_asked)
                for g in range(3):
                    n = 4 + 3 * t + g
                    dve.wait_ge(sc_exp, n + 1)
                    o(dve.tensor_reduce(dn3[:, g, :], probs_of(n).rearrange("p (h k) -> p h k", h=HPG), AX.X, ALU.add))
                dve.wait_ge(fn_done, t + 2)
                o(dve.tensor_tensor(dn3, dn3, em3, ALU.mult))
                o(dve.tensor_tensor(mxx, dn3[:, 0, :], dn3[:, 1, :], ALU.add))
                o(dve.tensor_tensor(mxx, mxx, dn3[:, 2, :], ALU.add))
                o(dve.reciprocal(mxx, mxx))
                o(dve.tensor_tensor(em3, em3, rows_bc(mxx, 3), ALU.mult))
                for g in range(3):
                    s3 = probs_of(4 + 3 * t + g).rearrange("p (h k) -> p h k", h=HPG)
                    o(dve.tensor_tensor(s3, s3, cols_bc(em3[:, g, :], SEQ), ALU.mult), pr_ready)
                for g in range(3):
                    dve_pv(dve, o, None, 4 + 3 * t + g, yA[:, 2 * g:2 * g + 2, t * P:(t + 1) * P])
            dve_mem_attention(dve, o, 0)
            post(dve, o, 7, 4, gB, post_done, tmpP)

        (dl_in, cv_ready, cs_ready, qk_ready) = (sem(n) for n in (
            "dl_in", "cv_ready", "cs_ready", "qk_ready"))
        (g_done, gc_ps, gr_in, gr_ps, df_ready, df_exp, kk_ps, kq_ps, kq_read) = (sem(n) for n in (
            "g_done", "gc_ps", "gr_in", "gr_ps", "df_ready", "df_exp", "kk_ps", "kq_ps", "kq_read"))
        (lm_ready, la_ps, la_ready, lx_ps, rhs_ready, uw_ps, uw_ready, kl_ready, st_ps, s_out, vn_ps, un_ready, o_ps, o_read) = (sem(n) for n in (
            "lm_ready", "la_ps", "la_ready", "lx_ps", "rhs_ready", "uw_ps", "uw_ready", "kl_ready", "st_ps", "s_out", "vn_ps", "un_ready", "o_ps", "o_read"))
        (onorm_in, on_ready, lev_in, L_ready, t_first, t_ready) = (sem(n) for n in (
            "onorm_in", "on_ready", "lev_in", "L_ready", "t_first", "t_ready"))
        NM = TT * DH
        CH = 3 * DH
        PADW = SEQ + TAPS - 1
        rawP = ar3(10240, CH * PADW, CH)
        conv = ar3(14920, CH * SEQ, CH)
        nat = ar3(10240, TT * CH * DD, TT * CH)
        qkT = ar3(14848, 2 * DH * SEQ, 2 * DH)
        zN = ar3(19528, TT * TW, TT)
        oN = ar3(21064, NM * DD, NM)
        qmD = ar3(6144, 512, 2)
        Lm = ar3(0, NM * P, NM)
        Tm, TTm = ar3(4096, NM * P, NM), ar3(8192, NM * P, NM)
        intra = ar3(17920, NM * P, NM)
        scr = ar3(1536, NM * P, NM)
        Ab = [ar(6144 + 512 * n, 512) for n in range(3)]
        uD, wTD = ar3(0, NM * P, NM), ar3(4096, DH * P, DH)
        rhsD = ar3(1536, NM * P, DH)
        klD, stD = ar3(1536, DH * P, DH), ar3(2304, DH * P, DH)
        LEVELS = 7
        lev_at = names["before"][0]
        levC = CON[:, lev_at:lev_at + LEVELS * 2 * P]

        def level(n, d):
            return levC[:, (2 * n + d) * P:(2 * n + d + 1) * P]

        taps = sm(900, CH * TAPS).rearrange("p (c k) -> p c k", c=CH)
        gin = sm(990, TT * 4 * DH).rearrange("p (t d b h) -> p t d b h", t=TT, d=2, b=2)
        alog, dtb = sm(1038, 12), sm(1050, 12)
        gdl, gab, beta = (sm(1062 + 24 * n, 24).rearrange("p (t d h) -> p t d h", t=TT, d=2) for n in range(3))
        gcs, egc, ekl = (sm(1134 + 24 * n, 24).rearrange("p (t d h) -> p t d h", t=TT, d=2) for n in range(3))
        ssn = sm(1206, 24).rearrange("p (t h) -> p t h", t=TT)
        sso = sm(1230, 12)
        onr = ar(9728, DD)

        def merge4(x):
            return x.rearrange("p a b -> p (a b)")

        def pool_delta_loads(pool):
            for c in range(CH):
                dma(pool, taps[:, c, :], A["dn_conv_2"][0][:, c * P:(c + 1) * P].rearrange("k p -> p k"), dl_in)
            dma(pool, alog, row(A["dn_a_log_2"][0].rearrange("d h -> (d h)")), dl_in)
            dma(pool, dtb, row(A["dn_dt_bias_2"][0].rearrange("d h -> (d h)")), dl_in)
            dma(pool, levC, A["k_levels"], lev_in)

        def pool_s11(pool):
            pool.wait_ge(ffn_done, 2)
            pool_gains(pool, 1, ("norm_mix_pre_2", "norm_mix_post_2"))
            pool_mem(pool, 1)
            for d in range(2):
                pool.wait_ge(L_ready, d + 1)
                for n in range(1, LEVELS):
                    masked = 3 * ((LEVELS - 1) * d + n - 1)
                    for b in range(3):
                        if n > 1:
                            pool.wait_ge(la_ps, masked - 3 + b + 1)
                        pool.tensor_tensor(scr[:, 4 * b:4 * b + 4, :], Lm[:, 4 * b:4 * b + 4, :], rows_bc(level(n, d), 4),
                                           ALU.mult).then_inc(lm_ready, 1)
            pool.wait_ge(o_read, 2)
            dma(pool, onr, row(A["dn_out_norm_2"][0]), onorm_in)
        DL_IN = 16 * (CH + 2)

        def pe_s11(pe):
            pe.wait_ge(ffn_done, 2)
            pe_mem(pe, 1)
            pe_pre(pe, 2)
            pe.wait_ge(mkv_ready, 2)
            w = arrived(pe, pc_dw[0])
            for t in range(TT):
                for k in range(KD):
                    pe.matmul(bank(0)[:, t * 24:(t + 1) * 24], hT2[:, k, t * P:(t + 1) * P], w[:, k, 0:24], start=(k == 0), stop=(k == KD - 1))
            for c in range(2):
                for k in range(KD):
                    m = pe.matmul(bank(1)[:, c * SEQ:(c + 1) * SEQ], w[:, k, 24 + c * P:24 + (c + 1) * P], hT2[:, k, :], start=(k == 0), stop=(k == KD - 1))
            m.then_inc(proj_ps, 1)
            pe.wait_ge(proj_ev, 12)
            pe_mem_scores(pe, 1, qmD)
            pe_cols(pe, arrived(pe, pc_dw[1]), 4, hT2, KD, proj_ps)
            pe.wait_ge(sc_read, 13)
            pe_cols(pe, arrived(pe, pc_dw[2]), 0, hT2, KD, proj_ps)
            pe.wait_ge(proj_ev, 13)
            pe_mem_probs(pe, 1)
            pe.wait_ge(sc_read, 14)
            pe_cols(pe, arrived(pe, pc_dw[3]), 2, hT2, KD, proj_ps)
            pe.wait_ge(prT_ready, 14)
            pe_cols(pe, arrived(pe, pc_dw[4]), 4, hT2, KD, proj_ps)
            w = arrived(pe, pc_dw[5])
            pe.wait_ge(pv_ev, 14)
            for c in range(2):
                for k in range(KD):
                    pe.matmul(bank(6)[:, c * SEQ:(c + 1) * SEQ], w[:, k, c * P:(c + 1) * P], hT2[:, k, :], start=(k == 0), stop=(k == KD - 1))
            for t in range(TT):
                for k in range(KD):
                    m = pe.matmul(bank(7)[:, t * SEQ:(t + 1) * SEQ], hT2[:, k, t * P:(t + 1) * P], w[:, k, 256:512], start=(k == 0), stop=(k == KD - 1))
            m.then_inc(proj_ps, 1)
            pe.wait_ge(proj_ev, 14)
            pe_rows(pe, arrived(pe, pc_dw[6]), (0, 1), hT2, KD, proj_ps)
            pe.wait_ge(proj_ev, 19)
            pe.wait_ge(cs_ready, 3)
            for b in range(NT):
                if b >= 8:
                    pe.wait_ge(turned, D_BASE + b - 7)
                for j in range(4):
                    n = 4 * b + j
                    t, c = n // CH, n % CH
                    m = pe.transpose(bank(b % 8)[:, j * P:(j + 1) * P], conv[:, c, t * P:(t + 1) * P], ident)
                m.then_inc(turn_ps, 1)
            pe.wait_ge(g_done, 1)
            pe.wait_ge(turned, D_BASE + NT)
            for t in range(TT):
                pe.matmul(bank(7)[:, t * 12:t * 12 + 6], con("upto"), gdl[:, t, 0, :], start=True, stop=True)
                pe.matmul(bank(7)[:, t * 12 + 6:t * 12 + 12], con("from"), gdl[:, t, 1, :], start=True, stop=True)
            m = pe.matmul(bank(7)[:, 24:48], con("ones"), gdl.rearrange("p t d h -> p (t d h)"), start=True, stop=True)
            m.then_inc(gc_ps, 1)
            pe.wait_ge(qk_ready, 1)
            for b in range(6):
                for j in range(4):
                    n = 4 * b + j
                    t, c = n // (2 * DH), n % (2 * DH)
                    m = pe.transpose(bank(b)[:, j * P:(j + 1) * P], nat[:, t * CH + c, :], ident)
                m.then_inc(turn_ps, 1)
            pe.wait_ge(turned, D_BASE + NT + QT)
            pe.wait_ge(fn_asked, 5)
            for d in range(2):
                pe_delta(pe, d)
            pe.wait_ge(on_ready, 1)
            for b in range(3):
                for j in range(4):
                    t, h = (4 * b + j) // DH, (4 * b + j) % DH
                    m = pe.transpose(bank(b)[:, j * P:(j + 1) * P], oN[:, t * DH + h, :], ident)
                m.then_inc(turn_ps, 1)
            pe.wait_ge(turned, D_BASE + NT + QT + OT)
            pe_out(pe, 1)

        def mh(m):
            return m // DH, m % DH

        def pe_delta(pe, d):
            first, second = (0, 1) if d == 0 else (1, 0)
            pe.wait_ge(gr_in, d + 1)
            for b in range(3):
                m = pe.matmul(bank(b), con("ones"), merge4(scr[:, 4 * b:4 * b + 4, :]), start=True, stop=True)
            m.then_inc(gr_ps, 1)
            for b in range(3):
                for j in range(4):
                    t, h = mh(4 * b + j)
                    m = pe.matmul(bank(3 + b)[:, j * P:(j + 1) * P], qkT[:, DH + h, t * P:(t + 1) * P], qkT[:, h, t * P:(t + 1) * P], start=True, stop=True)
            m.then_inc(kq_ps, 1)
            pe.wait_ge(df_ready, 2 * d + 2)
            for b in range(3):
                for j in range(4):
                    t, h = mh(4 * b + j)
                    m = pe.matmul(bank(b)[:, j * P:(j + 1) * P], qkT[:, DH + h, t * P:(t + 1) * P], qkT[:, DH + h, t * P:(t + 1) * P], start=True, stop=True)
            m.then_inc(kk_ps, 1)
            pe.wait_ge(kq_read, d + 1)
            for b in range(3):
                pe.wait_ge(t_first, 3 * d + b + 1)
                for j in range(4):
                    m = pe.transpose(bank(3 + b)[:, j * P:(j + 1) * P], Tm[:, 4 * b + j, :], ident)
                m.then_inc(lx_ps, 1)
            for n in range(1, LEVELS):
                done = 3 * (LEVELS * d + n)
                masked = 3 * ((LEVELS - 1) * d + n - 1)
                for b in range(3):
                    pe.wait_ge(lm_ready, masked + b + 1)
                    pe.wait_ge(t_ready, done - 3 + b + 1)
                    for j in range(4):
                        m_ = 4 * b + j
                        m = pe.matmul(bank(b)[:, j * P:(j + 1) * P], scr[:, m_, :], TTm[:, m_, :], start=True, stop=True)
                    m.then_inc(la_ps, 1)
                for b in range(3):
                    pe.wait_ge(la_ready, masked + b + 1)
                    for j in range(4):
                        m_ = 4 * b + j
                        m = pe.matmul(bank(3 + b)[:, j * P:(j + 1) * P], Tm[:, m_, :], Ab[b][:, j * P:(j + 1) * P], start=True, stop=True)
                    for j in range(4):
                        m_ = 4 * b + j
                        if n < LEVELS - 1:
                            m = pe.matmul(bank(b)[:, j * P:(j + 1) * P], Ab[b][:, j * P:(j + 1) * P], Tm[:, m_, :], start=True, stop=True)
                    m.then_inc(lx_ps, 1)
            pe.wait_ge(t_ready, 3 * LEVELS * (d + 1))
            for t in range(TT):
                pe.wait_ge(rhs_ready, 2 * d + t + 1)
                for h in range(DH):
                    m_ = t * DH + h
                    m = pe.matmul(bank(m_ // 4)[:, (m_ % 4) * P:(m_ % 4 + 1) * P], TTm[:, m_, :], rhsD[:, h, 0:P], start=True, stop=True)
                if t == second:
                    for h in range(DH):
                        m = pe.matmul(bank(3 + h // 4)[:, (h % 4) * P:(h % 4 + 1) * P], rhsD[:, h, P:2 * P], TTm[:, t * DH + h, :], start=True, stop=True)
                m.then_inc(uw_ps, 1)
            pe.wait_ge(uw_ready, d + 1)
            pe.wait_ge(kl_ready, d + 1)
            for h in range(DH):
                m = pe.matmul(bank(5 + h // 4)[:, (h % 4) * P:(h % 4 + 1) * P], klD[:, h, :], uD[:, first * DH + h, :], start=True, stop=True)
            m.then_inc(st_ps, 1)
            pe.wait_ge(s_out, d + 1)
            for h in range(DH):
                m = pe.matmul(bank(3 + h // 4)[:, (h % 4) * P:(h % 4 + 1) * P], wTD[:, h, :], stD[:, h, :], start=True, stop=True)
            for h in range(DH):
                m = pe.matmul(bank(h // 4)[:, (h % 4) * P:(h % 4 + 1) * P], qkT[:, h, second * P:(second + 1) * P], stD[:, h, :], start=True, stop=True)
            m.then_inc(vn_ps, 1)
            pe.wait_ge(un_ready, d + 1)
            for i, t in enumerate((first, second)):
                for h in range(DH):
                    m = pe.matmul(bank(4 + 2 * i + h // 4)[:, (h % 4) * P:(h % 4 + 1) * P], intra[:, t * DH + h, :], uD[:, t * DH + h, :], start=True, stop=True)
            m.then_inc(o_ps, 1)
            pe.wait_ge(o_read, d + 1)

        def act_s11(act, o):
            act.wait_ge(ffn_done, 2)
            act_mem(act, o, 1, 10)
            act_pre(act, o, 11, 2)
            def raw(n):
                act.wait_ge(proj_ps, 10 + n + 1)
                o(act.copy(rawP[:, 4 * n:4 * n + 4, 2:2 + SEQ], bank((4, 0, 2, 4)[n], 2).rearrange("p (c s) -> p c s", c=4)), proj_ev)

            def silu(n):
                act.wait_ge(cv_ready, DH * (n + 1))
                c = conv[:, DH * n:DH * (n + 1), :]
                o(act.activation(c, c, ACT.Silu), cs_ready)
            act.wait_ge(proj_ps, 10)
            o(act.copy(gin.rearrange("p t d b h -> p (t d b h)"), bank(0)[:, 0:48]), proj_ev)
            o(act.copy(qmD.rearrange("p c s -> p (c s)"), bank(1)), proj_ev)
            for n in (12, 13):
                act.wait_ge(sc_sub, n + 1)
                o(act.activation(probs_of(n), probs_of(n), ACT.Exp), sc_exp)
            raw(0)
            raw(1)
            act_probsT(act, o, 12)
            act_probsT(act, o, 13)
            act.wait_ge(fn_asked, 4)
            o(act.activation(beta, gin[:, :, :, 1, :], ACT.Sigmoid))
            o(act.activation(alog, alog, ACT.Exp))
            o(act.activation(gab, gab, ACT.Exp, scale=-1.0))
            o(act.activation(gab, gab, ACT.Ln, bias=1.0), fn_done)
            raw(2)
            silu(0)
            raw(3)
            silu(1)
            act.wait_ge(proj_ps, 15)
            o(act.copy(rawP[:, 16:18, 2:2 + SEQ], bank(6).rearrange("p (c s) -> p c s", c=2)), proj_ev)
            o(act.copy(zN[:, :, 0:256], bank(7).rearrange("p (t n) -> p t n", t=TT)), proj_ev)
            silu(2)
            act.wait_ge(proj_ps, 16)
            o(act.copy(zN[:, :, 256:768], bank(0, 2).rearrange("p (t n) -> p t n", t=TT)), proj_ev)
            for b in range(NT):
                act.wait_ge(turn_ps, D_BASE + b + 1)
                o(act.copy(merge4(nat[:, 4 * b:4 * b + 4, :]), bank(b % 8)), turned)
            act.wait_ge(fn_asked, 5)
            o(act.activation(egc, gcs, ACT.Exp))
            o(act.activation(ekl, ekl, ACT.Exp), fn_done)
            act.wait_ge(fn_asked, 6)
            o(act.activation(ssn, ssn, ACT.Sqrt), fn_done)
            for b in range(6):
                act.wait_ge(turn_ps, D_BASE + NT + b + 1)
                n = 4 * b
                t, c = n // (2 * DH), n % (2 * DH)
                o(act.copy(qkT[:, c:c + 4, t * P:(t + 1) * P], bank(b).rearrange("p (c s) -> p c s", c=4)), turned)
            for d in range(2):
                act_delta(act, o, d)
            act.wait_ge(fn_asked, 7)
            o(act.activation(sso, sso, ACT.Sqrt), fn_done)
            o(act.activation(zN, zN, ACT.Silu), fn_done)
            for b in range(3):
                act.wait_ge(turn_ps, D_BASE + NT + QT + b + 1)
                for j in range(4):
                    t, h = (4 * b + j) // DH, (4 * b + j) % DH
                    o(act.copy(yA[:, h, t * P:(t + 1) * P], bank(b)[:, j * P:(j + 1) * P]), turned if j == 3 else None)
            act.wait_ge(out_ps, 9)
            act_rms(act, o, [bank(4 + 2 * t, 2) for t in range(TT)], tmpJ, 12)

        def act_delta(act, o, d):
            second = 1 - d
            act.wait_ge(df_ready, 2 * d + 1)
            o(act.activation(intra, intra, ACT.Exp), df_exp)
            act.wait_ge(df_ready, 2 * d + 2)
            o(act.activation(Lm, Lm, ACT.Exp, scale=-1.0), df_exp)
            for n in range(1, LEVELS):
                masked = 3 * ((LEVELS - 1) * d + n - 1)
                for b in range(3):
                    act.wait_ge(la_ps, masked + b + 1)
                    if n > 1:
                        act.wait_ge(lx_ps, 3 * (LEVELS * d + n - 1) + b + 1)
                    o(act.copy(Ab[b], bank(b)), la_ready)
            act.wait_ge(uw_ps, 2 * d + 2)
            o(act.copy(merge4(uD), bank(0, 3)))
            o(act.copy(merge4(wTD), bank(3, 2)[:, 0:DH * P]), uw_ready)
            act.wait_ge(st_ps, d + 1)
            o(act.copy(merge4(stD), bank(5, 2)[:, 0:DH * P]), s_out)

        def dve_s11(dve, o):
            dve_mem(dve, o, 1, 10)
            dve.wait_ge(dl_in, DL_IN)
            dve_pre(dve, o, 11, 2, 6)
            o(dve.memset(spread(rawP[:, 0, 0:1], [PADW, CH], [1, TAPS // 2]), 0.0))
            o(dve.memset(spread(rawP[:, 0, SEQ + TAPS // 2:SEQ + TAPS // 2 + 1], [PADW, CH], [1, TAPS // 2]), 0.0))
            for t in range(TT):
                dve_softmax(dve, o, t, 12 + t, HD ** -0.5, None)
            o(dve.tensor_tensor(gdl, gin[:, :, :, 0, :], rows_bc(dtb.rearrange("p (d h) -> p d h", d=2), TT), ALU.add))
            o(dve.tensor_scalar(gab, gdl, -1.0, None, ALU.mult))
            o(dve.tensor_tensor(gab, gab, gdl, ALU.max), fn_asked)
            o(dve.tensor_scalar(gdl, gdl, 0.0, None, ALU.max))

            def convolve(first, last):
                for c in range(first, last):
                    dve.wait_ge(proj_ev, 12 + c // 4 + 1)
                    o(dve.tensor_scalar(conv[:, c, :], rawP[:, c, 0:SEQ], taps[:, c, 0:1], None, ALU.mult))
                    for k in range(1, TAPS):
                        o(dve.scalar_tensor_tensor(conv[:, c, :], rawP[:, c, k:k + SEQ], taps[:, c, k:k + 1], conv[:, c, :], ALU.mult, ALU.add),
                          cv_ready if k == TAPS - 1 else None)
            convolve(0, 4)
            for t in range(TT):
                dve_pv(dve, o, t, 12 + t, yA[:, 6:8, t * P:(t + 1) * P])
            dve.wait_ge(fn_done, 4)
            o(dve.tensor_tensor(gdl, gdl, gab, ALU.add))
            o(dve.tensor_tensor(gdl, gdl, rows_bc(alog.rearrange("p (d h) -> p d h", d=2), TT), ALU.mult))
            o(dve.tensor_scalar(gdl, gdl, -1.0, None, ALU.mult), g_done)
            convolve(4, CH)
            dve.wait_ge(gc_ps, 1)
            o(dve.tensor_copy(gcs.rearrange("p t d h -> p (t d h)"), bank(7)[:, 0:24]))
            o(dve.tensor_tensor(ekl.rearrange("p t d h -> p (t d h)"), bank(7)[:, 24:48], gcs.rearrange("p t d h -> p (t d h)"), ALU.subtract), fn_asked)
            sq = Tm
            for t in range(TT):
                x = nat[:, t * CH:t * CH + 2 * DH, :]
                o(dve.tensor_tensor(sq, x, x, ALU.mult))
                o(dve.tensor_reduce(ssn[:, t, :], sq, AX.X, ALU.add))
            o(dve.tensor_scalar(ssn, ssn, EPS, None, ALU.add), fn_asked)
            dve.wait_ge(fn_done, 6)
            o(dve.reciprocal(ssn, ssn))
            o(dve.tensor_scalar(ssn[:, :, 0:DH], ssn[:, :, 0:DH], DD ** -0.5, None, ALU.mult))
            for t in range(TT):
                x = nat[:, t * CH:t * CH + 2 * DH, :]
                o(dve.tensor_tensor(x, x, cols_bc(ssn[:, t, :], DD), ALU.mult), qk_ready if t == TT - 1 else None)
            o(dve.memset(oN, 0.0))
            dve.wait_ge(fn_done, 5)
            dve.wait_ge(turned, D_BASE + NT + QT)
            for d in range(2):
                dve_delta(dve, o, d)
            sq = Lm
            o(dve.tensor_tensor(sq, oN, oN, ALU.mult))
            o(dve.tensor_reduce(sso, sq, AX.X, ALU.add))
            o(dve.tensor_scalar(sso, sso, 1.0 / DD, EPS, ALU.mult, ALU.add), fn_asked)
            dve.wait_ge(fn_done, 7)
            o(dve.reciprocal(sso, sso))
            o(dve.tensor_tensor(oN, oN, cols_bc(sso, DD), ALU.mult))
            dve.wait_ge(onorm_in, 16)
            o(dve.tensor_tensor(oN, oN, rows_bc(onr, NM), ALU.mult))
            dve.wait_ge(fn_done, 8)
            o(dve.tensor_tensor(merge4(oN), merge4(oN), merge4(zN), ALU.mult), on_ready)
            post(dve, o, 12, 4, gB, post_done, tmpP)

        def dve_delta(dve, o, d):
            first, second = (0, 1) if d == 0 else (1, 0)
            def per(x):
                return bass.AP(x.tensor, x.offset + d * DH, [list(x.ap[0]), [2 * DH, TT], [1, DH]])
            def wide(x):
                y = per(x)
                return bass.AP(y.tensor, y.offset, [list(v) for v in y.ap] + [[0, P]])
            def four(x):
                return x.rearrange("p (t h) n -> p t h n", t=TT)
            tri = con("upto") if d == 0 else con("from")
            tri4 = bass.AP(tri.tensor, tri.offset, [list(tri.ap[0]), [0, TT], [0, DH], [1, P]])
            o(dve.tensor_tensor(four(scr), tri4, wide(gdl), ALU.mult), gr_in)
            dve.wait_ge(gr_ps, d + 1)
            o(dve.tensor_tensor(four(Tm), bank(0, 3).rearrange("p (t h n) -> p t h n", t=TT, h=DH), wide(gcs), ALU.subtract))
            o(dve.tensor_scalar(intra, Tm, 0.0, None, ALU.min), df_ready)
            o(dve.tensor_scalar(Lm, Tm, 0.0, None, ALU.max), df_ready)
            dve.wait_ge(df_exp, 2 * d + 1)
            o(dve.tensor_tensor(intra, intra, rows_bc(tri, NM), ALU.mult))
            dve.wait_ge(kq_ps, d + 1)
            o(dve.tensor_tensor(merge4(intra), merge4(intra), bank(3, 3), ALU.mult), kq_read)
            dve.wait_ge(df_exp, 2 * d + 2)
            o(dve.tensor_tensor(four(Lm), four(Lm), wide(beta), ALU.mult))
            dve.wait_ge(kk_ps, d + 1)
            o(dve.tensor_tensor(merge4(Lm), merge4(Lm), bank(0, 3), ALU.mult))
            dve.wait_ge(lev_in, 16)
            def group(x, b):
                return x[:, 4 * b:4 * b + 4, :]
            for b in range(3):
                o(dve.tensor_tensor(group(Tm, b), group(Lm, b), rows_bc(level(0, d), 4), ALU.mult), L_ready if b == 0 else None)
                o(dve.tensor_tensor(group(Tm, b), rows_bc(ident, 4), group(Tm, b), ALU.subtract), t_first)
            for n in range(LEVELS):
                for b in range(3):
                    dve.wait_ge(lx_ps, 3 * (LEVELS * d + n) + b + 1)
                    tt, tm = merge4(group(TTm, b)), merge4(group(Tm, b))
                    if n == 0:
                        o(dve.tensor_copy(tt, bank(3 + b)), t_ready)
                    elif n < LEVELS - 1:
                        o(dve.tensor_tensor(tt, tt, bank(3 + b), ALU.subtract))
                        o(dve.tensor_tensor(tm, tm, bank(b), ALU.subtract), t_ready)
                    else:
                        o(dve.tensor_tensor(tt, tt, bank(3 + b), ALU.subtract), t_ready)
            for t in range(TT):
                if t:
                    dve.wait_ge(uw_ps, 2 * d + t)
                b3 = beta[:, t, d, :]
                o(dve.tensor_tensor(rhsD[:, :, 0:P], nat[:, t * CH + 2 * DH:(t + 1) * CH, :], cols_bc(b3, P), ALU.mult))
                o(dve.tensor_tensor(sso[:, 0:DH], b3, egc[:, t, d, :], ALU.mult))
                o(dve.tensor_tensor(rhsD[:, :, P:2 * P], nat[:, t * CH + DH:t * CH + 2 * DH, :], cols_bc(sso[:, 0:DH], P), ALU.mult), rhs_ready)
            dve.wait_ge(uw_ps, 2 * d + 2)
            o(dve.tensor_tensor(klD, nat[:, first * CH + DH:first * CH + 2 * DH, :], cols_bc(ekl[:, first, d, :], P), ALU.mult), kl_ready)
            dve.wait_ge(vn_ps, d + 1)
            u2 = merge4(uD[:, second * DH:(second + 1) * DH, :])
            o(dve.tensor_tensor(u2, u2, bank(3, 2)[:, 0:DH * P], ALU.subtract), un_ready)
            inter = klD
            o(dve.tensor_tensor(inter, bank(0, 2)[:, 0:DH * P].rearrange("p (h n) -> p h n", h=DH), cols_bc(egc[:, second, d, :], P), ALU.mult))
            def o_of(t):
                return oN[:, t * DH:(t + 1) * DH, :]
            o(dve.tensor_tensor(o_of(second), o_of(second), inter, ALU.add))
            dve.wait_ge(o_ps, d + 1)
            o(dve.tensor_tensor(merge4(o_of(first)), merge4(o_of(first)), bank(4, 2)[:, 0:DH * P], ALU.add))
            o(dve.tensor_tensor(merge4(o_of(second)), merge4(o_of(second)), bank(6, 2)[:, 0:DH * P], ALU.add), o_read)

        def store_out(sp):
            for t in range(TT):
                sp.wait_ge(ffn_done, 2 + t + 1)
                sp.dma_start(out[0, t * P:(t + 1) * P, :], x3[:, t, :]).then_inc(out_stored, 16)
            sp.wait_ge(out_stored, 16 * TT)

        block = ctx.enter_context(nc.Block())

        @block.sync
        def _(sp):
            sp_first(sp)
            sp_s7(sp)
            sp.wait_ge(ff_ps, 1)
            stream(sp, LAST, len(pieces))
            store_out(sp)

        @block.gpsimd
        def _(pool):
            pool_s0(pool)
            pool_s6(pool)
            pool_bias(pool)
            pool_s9(pool)
            pool_ffn(pool, 0)
            pool_delta_loads(pool)
            pool_s11(pool)
            pool_ffn(pool, 1)


        @block.scalar
        def _(act):
            o = Ordered(act, act_order)
            act_s0(act, o)
            act_s1(act, o)
            act_s2(act, o)
            act_s4(act, o)
            act_s3(act, o)
            act_s5(act, o)
            act_s6(act, o)
            act_bias(act, o)
            act_s7(act)
            act_s8(act, o)
            act_s9(act, o)
            act_ffn(act, o, 0, 8)
            act_s11(act, o)
            act_ffn(act, o, 1, 13)


        @block.vector
        def _(dve):
            o = Ordered(dve, dve_order)
            dve_s0(dve, o)
            dve_s1(dve, o)
            dve_tables(dve, o)
            dve_s2(dve, o)
            dve_s4(dve, o)
            dve_s3(dve, o)
            dve_s5(dve, o)
            dve_s6(dve, o)
            dve_bias(dve, o)
            dve_s7(dve)
            dve_s8(dve, o)
            dve_s9(dve, o)
            dve_ffn(dve, o, 0, 8)
            dve_s11(dve, o)
            dve_ffn(dve, o, 1, 13)


        @block.tensor
        def _(pe):
            pe_s0(pe)
            pe_s1(pe)
            pe_s2(pe)
            pe_s4(pe)
            pe_s3(pe)
            pe_s5(pe)
            pe_s6(pe)
            pe_bias(pe)
            pe_s7(pe)
            pe_s8(pe)
            pe_s9(pe)
            pe_ffn(pe, 0)
            pe_s11(pe)
            pe_ffn(pe, 1)



def kernel(**inputs):
    import concourse.bacc as bacc
    from concourse.bass_utils import run_bass_kernel_spmd

    nc = bacc.Bacc("TRN2", target_bir_lowering=False, num_devices=1)
    arrays = {name: np.ascontiguousarray(a) for name, a in inputs.items()}
    arrays["ffn_w_gate_up_2"] = paired(arrays["ffn_w_gate_up_2"])
    arrays["k_main"], names, arrays["k_levels"], arrays["k_hot"] = shape_constants()
    A, fed = {}, {}
    for name, a in arrays.items():
        fed[f"in_{name}"] = a
        A[name] = nc.dram_tensor(f"in_{name}", a.shape, mybir.dt.from_np(a.dtype), kind="ExternalInput").ap()
    out = nc.dram_tensor("out", (1, SEQ, D), mybir.dt.float32, kind="ExternalOutput").ap()
    block_kernel(nc, A, out, names)
    r = run_bass_kernel_spmd(nc, [fed], core_ids=[0])
    return r.results[0]["out"]
```

```python
from contextlib import ExitStack

import numpy as np
import concourse.bass as bass
from concourse import mybir

P = 128
D = 1024
SEQ = 256
TT = SEQ // P
KD = D // P
EPS = 1e-6
NEG = -1e30
HEADS, HD = 8, 64
SSM_G, SSM_C, SSM_P = 32, 16, 64
SW = SSM_G * SSM_C
SJ = SSM_G * SSM_P // P
SQ = SW // P
E, TOPK, CAP = 32, 4, 64
ROUNDS = SEQ // CAP
FF = 1024
ALPHA, LIMIT = 1.702, 7.0
TW, MW = 768, 256
GROUPS = ((128, 1), (512, 4), (2048, 16))
ATT_HEADS, HPG = 12, 4
BUCKETS, MAX_DIST = 32, 1024
DH = 6
DD = 128
TAPS = 5
FF2 = 2816
FC2 = FF2 // P
TWO_PI = 6.2831845
SLOTS, SLOT_W = 6, 4096


def shape_constants():
    i = np.arange(P)
    c = {}
    c["ident"] = np.eye(P)
    c["ones"] = np.ones((P, P))
    c["upto"] = (i[:, None] <= i[None, :])
    c["from"] = (i[:, None] >= i[None, :])
    c["before"] = (i[:, None] < i[None, :])
    c["slots"] = np.tile(np.arange(SEQ).reshape(ROUNDS, 1, CAP), (1, 2, 1)).reshape(1, -1).repeat(P, 0)
    c["steps"] = np.arange(SEQ)[None, :].repeat(P, 0)
    c["experts"] = np.arange(E)[None, :].repeat(P, 0)
    rot = np.zeros((P, P))
    for b in range(0, P, HD):
        for d in range(HD // 2):
            rot[b + d + HD // 2, b + d] = -1.0
            rot[b + d, b + d + HD // 2] = 1.0
    c["rot"] = rot
    c["zero_rows"] = np.zeros((P, P))
    c["flip"] = np.eye(P)[::-1] * HD ** 0.5
    half = HD // 2
    inv = (np.float32(10000.0) ** (-np.arange(half, dtype=np.float32) / np.float32(half))).astype(np.float32)
    c["inv_freq"] = inv[i % half][:, None]
    causal = np.where(np.arange(SEQ)[None, None, :] <= (i[:, None, None] + P * np.arange(TT)[None, :, None]), 0.0, NEG)
    c["causal"] = causal.reshape(P, -1)
    c["mask_b"] = ((i // SSM_P)[:, None] == (np.arange(2 * SSM_C) // SSM_C)[None, :])
    c["mask_c"] = (((i // SSM_C) % 2)[:, None] == (np.arange(P) // SSM_P)[None, :])
    names, cols, at = {}, [], 0
    for k, v in c.items():
        v = np.asarray(v, np.float32)
        names[k] = (at, v.shape[1])
        at += v.shape[1]
        cols.append(v)
    main = np.ascontiguousarray(np.concatenate(cols, 1))
    lev = []
    for n in range(7):
        b = 1 << n
        m = (i[:, None] // (2 * b) == i[None, :] // (2 * b)) & ((i[:, None] // b) % 2 == 1) & ((i[None, :] // b) % 2 == 0)
        lev.append(np.stack([m, m.T], 1))
    levels = np.stack(lev, 1).astype(np.float32).reshape(P, -1)
    rel = np.arange(SEQ - 1, -SEQ, -1) * -1
    hot = np.zeros((BUCKETS + 1, len(GROUPS), 2 * SEQ), np.float32)
    for g, (window, dil) in enumerate(GROUPS):
        h = window // (2 * dil)
        n = np.abs(rel)
        hb = BUCKETS // 2
        me = hb // 2
        large = me + (np.log(np.maximum(n, 1) / me) / np.log(MAX_DIST / me) * (hb - me)).astype(np.int64)
        bucket = (rel > 0) * hb + np.where(n < me, n, np.minimum(large, hb - 1))
        ok = (rel % dil == 0) & (np.abs(rel // dil) <= h)
        for r in range(len(rel)):
            hot[bucket[r] if ok[r] else BUCKETS, g, r] = 1.0
        hot[BUCKETS, g, len(rel)] = 1.0
    return main, names, levels, hot.reshape(BUCKETS + 1, -1)


def paired(w):
    n, d, f2 = w.shape
    return np.ascontiguousarray(w.reshape(n, d, 2, f2 // 512, 256).transpose(0, 1, 3, 2, 4)).reshape(n, d, f2)


def block_kernel(nc, A, out, names):
    f32, i32, u32 = mybir.dt.float32, mybir.dt.int32, mybir.dt.uint32
    ALU, ACT, AX = mybir.AluOpType, mybir.ActivationFunctionType, mybir.AxisListType
    ctx = ExitStack()

    def sem(name):
        return ctx.enter_context(nc.semaphore(name))

    def sb(name, cols, dt=f32, parts=P):
        return ctx.enter_context(nc.sbuf_tensor(name, [parts, cols], dt))

    def spread(ap, *dims):
        return bass.AP(ap.tensor, ap.offset, [list(ap.ap[0])] + [list(d) for d in dims])

    def cols_bc(ap, n):
        return bass.AP(ap.tensor, ap.offset, [list(d) for d in ap.ap] + [[0, n]])

    def rows_bc(ap, n):
        return bass.AP(ap.tensor, ap.offset, [list(ap.ap[0]), [0, n]] + [list(d) for d in ap.ap[1:]])

    class Ordered:

        def __init__(self, eng, own):
            self.eng, self.own, self.n, self.told, self.base = eng, own, 0, {}, None

        def __call__(self, ins, tells=None):
            if tells is None:
                self.n += 1
                ins.then_inc(self.own, 1)
                self.eng.wait_ge(self.own, self.n if self.base is None else self.base + self.n)
            else:
                self.told[tells.name] = self.told.get(tells.name, 0) + 1
                ins.then_inc(tells, 1)
                if self.base is None:
                    self.eng.wait_ge(tells, self.told[tells.name])

    with ctx:
        CON = sb("constants", A["k_main"].shape[1])
        X = sb("x_res", TT * D)
        RING = sb("ring", SLOTS * SLOT_W)
        AR = sb("arena", 22600)
        SM = sb("smalls", 1280)
        x3 = X[:, :].rearrange("p (t d) -> p t d", t=TT)
        PS = ctx.enter_context(nc.psum_tensor("ps", [P, 4096], f32))

        def con(name, rows=P):
            a, n = names[name]
            return CON[0:rows, a:a + n]

        def bank(b, n=1, rows=P):
            return PS[0:rows, b * 512:(b + n) * 512]

        def ar(at, n, rows=P):
            return AR[0:rows, at:at + n]

        def sm(at, n, rows=P):
            return SM[0:rows, at:at + n]

        ident = con("ident")

        slot_ready = [sem(f"slot_ready{i}") for i in range(SLOTS)]
        pieces = []
        filled = [0] * SLOTS

        def hold(used, count):
            pieces.append((None, used, count))
            return RING[:, (len(pieces) - 1) % SLOTS * SLOT_W:((len(pieces) - 1) % SLOTS + 1) * SLOT_W]

        def piece(src, used, count):
            pieces.append((src, used, count))
            n = len(pieces) - 1
            filled[n % SLOTS] += 1
            shape = [s for s in src.shape][1:]
            w = int(np.prod(shape))
            v = RING[:, (n % SLOTS) * SLOT_W:(n % SLOTS) * SLOT_W + w]
            if len(shape) > 1:
                v = v.rearrange("p (k n) -> p k n", k=shape[0])
            return n, v, filled[n % SLOTS]

        def arrived(pe, pc):
            n, place, loads = pc
            pe.wait_ge(slot_ready[n % SLOTS], 16 * loads)
            return place

        def by_k(w, c0, c1):
            return w[:, c0:c1].rearrange("(k p) n -> p k n", p=P)

        ada_w = A["ada_w"][0]
        w_in = A["w_in"][0]

        (act_order, dve_order) = (sem(n) for n in (
            "act_order", "dve_order"))
        x_in, con_in, mod_in, ssm_in, rope_in = (sem(n) for n in ("x_in", "con_in", "mod_in", "ssm_in", "rope_in"))
        cond_silu, cond_ready, ada_ps = sem("cond_silu"), sem("cond_ready"), sem("ada_ps")
        bc_ready, bc_ps, bc_ev = sem("bc_ready"), sem("bc_ps"), sem("bc_ev")
        par_in, par_exp, par_red, par_trig = sem("par_in"), sem("par_exp"), sem("par_red"), sem("par_trig")
        ph_ready, tab_ready, rope_red, rope_tab = sem("ph_ready"), sem("tab_ready"), sem("rope_red"), sem("rope_tab")
        sq_done, ms_done, rt_done = sem("sq_done"), sem("ms_done"), sem("rt_done")
        (proj_ps, rot_ps, rope_done) = (sem(n) for n in (
            "proj_ps", "rot_ps", "rope_done"))
        sc_ps, sc_sub, sc_exp, pr_ready, prT_ps, prT_ready, pv_ps, pv_ev = (sem(n) for n in (
            "sc_ps", "sc_sub", "sc_exp", "pr_ready", "prT_ps", "prT_ready", "pv_ps", "pv_ev"))
        bu_ps, bu_read, st_ready, y_ps, y_ready, gel_ready = (
            sem(n) for n in ("bu_ps", "bu_read", "st_ready", "y_ps", "y_ready", "gel_ready"))
        ys_ready = sem("ys_ready")
        (gate_ready, x1_ready) = (sem(n) for n in (
            "gate_ready", "x1_ready"))
        (hot_in, neg_ready, bv_ready, bv_stored, mem_in, mkv_ps, mem_ready, mkv_ready) = (sem(n) for n in (
            "hot_in", "neg_ready", "bv_ready", "bv_stored", "mem_in", "mkv_ps", "mem_ready", "mkv_ready"))
        (gate_ps, mod_ps, mod_read, rows_ready, c_in) = (sem(n) for n in ("gate_ps", "mod_ps", "mod_read", "rows_ready", "c_in"))

        (turn_ps, turned, nat_ready, fn_asked, fn_done, proj_ev, out_ps, router_ps) = (sem(n) for n in (
            "turn_ps", "turned", "nat_ready", "fn_asked", "fn_done", "proj_ev", "out_ps", "router_ps"))
        pc_ada = [piece(by_k(ada_w, n * 512, n * 512 + 512), ada_ps, n + 1) for n in range(6)]
        pc_in = [piece(by_k(w_in, n * 512, n * 512 + 512), proj_ps, n + 1) for n in range(4)]
        pc_ada2 = [piece(by_k(ada_w, n * 512, n * 512 + 512), ada_ps, 6 + 1 + (n - 6) // 4) for n in range(6, 12)]
        pc_gate = [piece(by_k(w_in, (4 + n) * 512, (5 + n) * 512), gate_ps, TT * (n + 1)) for n in range(4)]
        HELD = hold(mod_ps, 2)
        pc_wa = piece(by_k(A["w_attn_branch"][0], 0, D), out_ps, 1)
        pc_glu = piece(by_k(A["ssm_w_glu"][0], 0, SW), out_ps, 2)
        pc_ws = piece(by_k(A["w_ssm_branch"][0], 0, D), out_ps, 3)
        pc_out = [piece(by_k(A["w_out"][0], n * 512, n * 512 + 512), out_ps, 3 + n + 1) for n in range(2)]
        hold(mod_ps, 2)
        pc_mem = [piece(by_k(A["mem_w_kv_2"][i], 0, 2 * MW), mkv_ps, i + 1) for i in range(2)]

        def ar3(at, n, k):
            return ar(at, n).rearrange("p (k m) -> p k m", k=k)

        shm, Am, GTm = ar(0, D), ar(D, D), ar(2 * D, D)
        condrep = ar3(3072, 1024, KD)
        gpre, gpost = ar(4096, D), ar(5120, D)
        h_nat = ar3(4096, 2048, TT)
        hT = ar3(6144, 2048, KD)
        uT, qT, kT = ar3(8192, 1024, 4), ar3(9216, 1024, 4), ar3(20480, 1024, 4)
        vN = ar3(21504, 1024, TT)
        cosS, sinS = ar3(10240, 4096, SJ), ar3(14336, 4096, SJ)
        BTr, BTi, CTr, CTi = (ar3(18432 + 512 * n, 512, SQ) for n in range(4))
        braw = [ar3(10240 + 256 * n, 256, SJ) for n in range(2)]
        bbar = [ar3(10752 + 256 * n, 256, SJ) for n in range(2)]
        craw = [ar3(11264 + 256 * n, 256, SQ) for n in range(2)]
        btmp = ar3(11776, 256, SJ)
        Bd = [ar(12288 + 512 * n, 512) for n in range(2)]
        Cd = [ar(13312 + 512 * n, 512) for n in range(2)]
        BC = [BTr, BTi, CTr, CTi]
        ph_n = ar(3072, 1024)
        qraw, kraw = ar(0, 1024), ar(1024, 1024)
        rtmp = ar3(4096, 1024, 4)
        prob = [ar(4096, 1024), ar(5120, 1024)]
        prT = [ar(0, 1024), ar(1024, 1024)]
        yaT = ar3(3072, 1024, 4)
        sA, sB, sT, sU = ar3(0, 1024, 4), ar3(1024, 1024, 4), ar3(4096, 1024, 4), ar3(5120, 1024, 4)
        yT = ar3(9216, 1024, SQ)
        sgs, sga = ar3(20480, 2048, TT), HELD[:, 0:2048].rearrange("p (t d) -> p t d", t=TT)
        adaS = HELD[:, 2048:3072]
        gel, sglu, ysT = ar3(10240, 1024, SQ), ar3(11264, 1024, SQ), ar3(12288, 1024, SQ)
        mgd, mtmp = ar3(16384, 2048, TT), ar(18432, 1024)
        mgT = ar3(6144, 2048, KD)

        hotS, relS = ar(18432, 3 * 2 * SEQ, BUCKETS + 1), ar(19968, ATT_HEADS, BUCKETS + 1)
        bvS = ar(20480, 2 * SEQ)
        mem_nat = ar3(20480, 2048, TT)
        mem_T = [ar3(8192, 2048, KD), ar3(14336, 2048, KD)]
        kvNow = ar(21504, 1024)
        kvKept = CON[:, names["before"][0]:names["before"][0] + 1024]

        def kv_of(x):
            return x[:, 0:512].rearrange("p (c s) -> p c s", c=2), x[:, 512:1024].rearrange("p (t n) -> p t n", t=TT)
        kvM = [ar(4096 + 1024 * i, 1024) for i in range(2)]
        mem_g = sm(1136, 2 * KD).rearrange("p (i k) -> p i k", i=2)

        c_col, cond = sm(0, KD), sm(8, KD)
        (lam_re, lam_im, dt_c, mag, th, frq, tc, lbr, lbi, cr, ci, den, fhi, flo) = (sm(16 + 16 * n, SJ) for n in range(14))
        dcol, ssq, rms = sm(256, SQ), sm(260, TT), sm(262, TT)
        cosR, sinR = sm(320, SEQ), sm(576, SEQ)
        tc2, intc = sm(832, SJ), sm(848, SJ)
        cond32 = sm(880, 32 * KD).rearrange("p (k m) -> p k m", k=KD)
        amax, aden = sm(864, HPG), sm(868, HPG)

        def dma(eng, dst, src, s):
            eng.dma_start(dst, src, allow_slow_non_contiguous=True).then_inc(s, 16)

        def row(ap1):
            return bass.AP(ap1.tensor, ap1.offset, [[0, P]] + [list(d) for d in ap1.ap])

        def stream(sp, first, last):
            for n in range(first, last):
                src = pieces[n][0]
                if src is None:
                    continue
                if n >= SLOTS:
                    sp.wait_ge(pieces[n - SLOTS][1], pieces[n - SLOTS][2])
                shape = list(src.shape)[1:]
                v = RING[:, (n % SLOTS) * SLOT_W:(n % SLOTS) * SLOT_W + int(np.prod(shape))]
                if len(shape) > 1:
                    v = v.rearrange("p (k n) -> p k n", k=shape[0])
                sp.dma_start(v, src).then_inc(slot_ready[n % SLOTS], 16)

        bv_dram = nc.dram_tensor("band_bias", [ATT_HEADS, 2 * SEQ], f32, kind="Internal").ap()

        def pool_bias_loads(pool):
            pool.wait_ge(neg_ready, 1)
            dma(pool, hotS, A["k_hot"], hot_in)
            dma(pool, relS[0:BUCKETS, :], A["rel_bias_2"], hot_in)

        def pool_bias_store(pool):
            pool.wait_ge(bv_ready, 3)
            for g in range(3):
                dma(pool, bv_dram[HPG * g:HPG * (g + 1), :], bvS[32 * g:32 * g + HPG, :], bv_stored)
            pool.wait_ge(bv_stored, 16 * 3)

        def dve_bias(dve, o):
            o(dve.memset(relS, NEG), neg_ready)

        def pe_bias(pe):
            pe.wait_ge(hot_in, 32)
            for g in range(3):
                m = pe.matmul(bank(7)[32 * g:32 * g + HPG, :], relS[:, HPG * g:HPG * g + HPG], hotS[:, g * 2 * SEQ:(g + 1) * 2 * SEQ],
                              start=True, stop=True, tile_position=(0, 32 * g))
            m.then_inc(router_ps, 1)
            pe.wait_ge(bv_ready, 3)

        def act_bias(act, o):
            act.wait_ge(router_ps, 1)
            for g in range(3):
                o(act.copy(bvS[32 * g:32 * g + HPG, :], bank(7)[32 * g:32 * g + HPG, :]), bv_ready)

        def pool_s0(pool):
            for s, a in ((lam_re, "ssm_lam_re"), (lam_im, "ssm_lam_im")):
                dma(pool, s, A[a][0].rearrange("(j g) s -> (g s) j", g=2), par_in)
            for g in range(2):
                src = A["ssm_log_dt"][0]
                dma(pool, dt_c[g * SSM_P:(g + 1) * SSM_P, :],
                    bass.AP(src.tensor, src.offset + g, [[0, SSM_P], [2, SJ]]), par_in)
            for n, a in enumerate(("ssm_b_re", "ssm_b_im")):
                dma(pool, braw[n], A[a][0].rearrange("(j g) s c -> (g s) j c", g=2), ssm_in)
            for n, a in enumerate(("ssm_c_re", "ssm_c_im")):
                dma(pool, craw[n], A[a][0].rearrange("(q r) c s -> (r c) q s", q=SQ), ssm_in)
            dma(pool, dcol, A["ssm_d"][0].rearrange("(q p) -> p q", p=P), ssm_in)
            dma(pool, sinR.bitcast(i32), row(A["positions"][0]), rope_in)
            pool_bias_loads(pool)
            dma(pool, mem_g, A["mem_norm_2"].rearrange("i (k p) -> p i k", p=P), mem_in)
            dma(pool, x3, A["x"][0].rearrange("(t p) d -> p t d", p=P), x_in)
            for n, d in enumerate((shm, Am, GTm)):
                dma(pool, d, row(A["ada_b"][0][n * D:(n + 1) * D]), mod_in)
            dma(pool, gpre, row(A["mix_pre_g"][0]), mod_in)
            dma(pool, gpost, row(A["mix_post_g"][0]), mod_in)

        def sp_first(sp):
            dma(sp, c_col, A["c"].rearrange("a (k p) -> p (a k)", p=P), c_in)
            dma(sp, CON[:, :], A["k_main"], con_in)
            stream(sp, 0, SLOTS)
            sp.wait_ge(ssm_in, 16 * 5)
            sp.wait_ge(rope_in, 16)
            stream(sp, SLOTS, FIRST)

        def act_s0(act, o):
            act.wait_ge(c_in, 16)
            o(act.activation(cond, c_col, ACT.Silu), cond_silu)
            act.wait_ge(par_in, 16 * 4)
            o(act.activation(dt_c, dt_c, ACT.Exp), par_exp)
            act.wait_ge(par_red, 1)
            o(act.activation(mag, mag, ACT.Exp), par_exp)
            act.wait_ge(par_red, 2)
            o(act.activation(lbi, frq, ACT.Sin, scale=TWO_PI))
            o(act.activation(lbr, tc, ACT.Sin, scale=TWO_PI), par_trig)
            act.wait_ge(rope_red, 1)
            o(act.activation(cosR, cosR, ACT.Sin))
            o(act.activation(sinR, sinR, ACT.Sin), rope_tab)
            act.wait_ge(x_in, 16)
            act_rms(act, o, [x3[:, t, :] for t in range(TT)], hT[:, 0:4, :].rearrange("p k m -> p (k m)"), 1)
            act_bias(act, o)
            for n in range(4):
                act.wait_ge(bc_ps, n + 1)
                o(act.copy(BC[n], bank(6 + n % 2).rearrange("p (q m) -> p q m", q=SQ)), bc_ev)

        def act_tables(act, o, h):
            act.wait_ge(ph_ready, h + 1)
            for x in (sinS, cosS):
                o(act.activation(x[:, 4 * h:4 * h + 4, :], x[:, 4 * h:4 * h + 4, :], ACT.Sin, scale=TWO_PI), tab_ready)

        def turn(dve, o, x, n_int, n_f):
            o(dve.tensor_copy(n_int, x))
            o(dve.tensor_copy(n_f, n_int))
            return dve.tensor_tensor(x, x, n_f, ALU.subtract)

        def quarter_on(dve, o, outp, x, tmp):
            o(dve.tensor_scalar(tmp, x, 0.25, None, ALU.is_gt))
            return dve.scalar_tensor_tensor(outp, x, 0.25, tmp, ALU.add, ALU.subtract)

        def dve_s0(dve, o):
            dve_bias(dve, o)
            dve.wait_ge(cond_silu, 1)
            o(dve.tensor_copy(condrep, cols_bc(cond, P)))
            o(dve.tensor_copy(cond32, cols_bc(cond, 32)), cond_ready)
            dve.wait_ge(rope_in, 16)
            dve.wait_ge(con_in, 16)
            o(dve.tensor_copy(cosR, sinR.bitcast(i32)))
            o(dve.tensor_scalar(sinR, cosR, con("inv_freq"), None, ALU.mult))
            turns, whole = ar(8192, SEQ), ar(8448, SEQ)
            o(dve.tensor_scalar(turns, sinR, float(1 / (2 * np.pi)), None, ALU.mult))
            o(dve.tensor_copy(whole.bitcast(i32), turns))
            o(dve.tensor_copy(turns, whole.bitcast(i32)))
            o(dve.scalar_tensor_tensor(sinR, turns, -6.28125, sinR, ALU.mult, ALU.add))
            o(dve.scalar_tensor_tensor(sinR, turns, float(-(2 * np.pi - 6.28125)), sinR, ALU.mult, ALU.add))
            o(dve.tensor_scalar(whole, sinR, float(np.pi / 2), float(-2 * np.pi), ALU.is_gt, ALU.mult))
            o(dve.scalar_tensor_tensor(cosR, sinR, float(np.pi / 2), whole, ALU.add, ALU.add))
            for r in (sinR, cosR):
                last = dve.tensor_scalar(r, r, 3.1415925, -3.1415925, ALU.min, ALU.max)
                o(last, rope_red if r is cosR else None)
            dve.wait_ge(par_exp, 1)
            o(dve.tensor_tensor(mag, lam_re, dt_c, ALU.mult), par_red)
            o(dve.tensor_tensor(th, lam_im, dt_c, ALU.mult))
            o(dve.tensor_scalar(frq, th, float(1 / (2 * np.pi)), None, ALU.mult))
            o(turn(dve, o, frq, intc.bitcast(i32), tc2))
            o(quarter_on(dve, o, tc, frq, tc2), par_red)
            o(dve.tensor_scalar(tc2, frq, 4096.0, None, ALU.mult))
            o(dve.tensor_copy(intc.bitcast(i32), tc2))
            o(dve.tensor_copy(tc2, intc.bitcast(i32)))
            o(dve.tensor_scalar(fhi, tc2, 1.0 / 4096, None, ALU.mult))
            o(dve.tensor_tensor(flo, frq, fhi, ALU.subtract))
            dve.wait_ge(par_exp, 2)
            dve.wait_ge(par_trig, 1)
            o(dve.tensor_tensor(lbr, lbr, mag, ALU.mult))
            o(dve.tensor_tensor(lbi, lbi, mag, ALU.mult))
            o(dve.tensor_scalar(lbr, lbr, -1.0, None, ALU.add))
            o(dve.tensor_tensor(den, lam_re, lam_re, ALU.mult))
            o(dve.tensor_tensor(tc2, lam_im, lam_im, ALU.mult))
            o(dve.tensor_tensor(den, den, tc2, ALU.add))
            o(dve.reciprocal(den, den))
            o(dve.tensor_tensor(cr, lbr, lam_re, ALU.mult))
            o(dve.tensor_tensor(tc2, lbi, lam_im, ALU.mult))
            o(dve.tensor_tensor(cr, cr, tc2, ALU.add))
            o(dve.tensor_tensor(cr, cr, den, ALU.mult))
            o(dve.tensor_tensor(ci, lbi, lam_re, ALU.mult))
            o(dve.tensor_tensor(tc2, lbr, lam_im, ALU.mult))
            o(dve.tensor_tensor(ci, ci, tc2, ALU.subtract))
            o(dve.tensor_tensor(ci, ci, den, ALU.mult))
            dve.wait_ge(ssm_in, 16 * 5)
            crb, cib = cols_bc(cr, SSM_C), cols_bc(ci, SSM_C)
            o(dve.tensor_tensor(bbar[0], braw[0], crb, ALU.mult))
            o(dve.tensor_tensor(btmp, braw[1], cib, ALU.mult))
            o(dve.tensor_tensor(bbar[0], bbar[0], btmp, ALU.subtract))
            o(dve.tensor_tensor(bbar[1], braw[1], crb, ALU.mult))
            o(dve.tensor_tensor(btmp, braw[0], cib, ALU.mult))
            o(dve.tensor_tensor(bbar[1], bbar[1], btmp, ALU.add))
            mb = spread(con("mask_b"), [0, SJ], [SSM_C, 2], [1, SSM_C])
            mc = spread(con("mask_c"), [0, SQ], [SSM_P, 2], [1, SSM_P])
            for n in range(2):
                o(dve.tensor_tensor(Bd[n].rearrange("p (j g c) -> p j g c", g=2, c=SSM_C),
                                    spread(bbar[n], [SSM_C, SJ], [0, 2], [1, SSM_C]), mb, ALU.mult), bc_ready)
            for n in range(2):
                o(dve.tensor_tensor(Cd[n].rearrange("p (q g s) -> p q g s", g=2, s=SSM_P),
                                    spread(craw[n], [SSM_P, SQ], [0, 2], [1, SSM_P]), mc, ALU.mult), bc_ready)
            dve_rms(dve, o, 1)
            dve.wait_ge(mod_in, 16 * 5)
            dve.wait_ge(ada_ps, 6)
            o(dve.tensor_tensor(shm, shm, bank(0, 2), ALU.add))
            o(dve.scalar_tensor_tensor(Am, bank(2, 2), 1.0, Am, ALU.add, ALU.add))
            o(dve.tensor_tensor(Am, Am, gpre, ALU.mult))
            o(dve.tensor_tensor(GTm, GTm, bank(4, 2), ALU.add))
            o(dve.tensor_tensor(GTm, GTm, gpost, ALU.mult))

        def dve_tables(dve, o):
            dve.wait_ge(bc_ps, 4)
            steps = spread(con("steps"), [0, 4], [1, SEQ])
            for h in range(4):
                f3, t3 = sinS[:, 4 * h:4 * h + 4, :], cosS[:, 4 * h:4 * h + 4, :]
                f, t = (x.rearrange("p j s -> p (j s)") for x in (f3, t3))
                o(dve.tensor_tensor(f3, steps, cols_bc(fhi[:, 4 * h:4 * h + 4], SEQ), ALU.mult))
                o(turn(dve, o, f, ph_n.bitcast(i32), t))
                o(dve.tensor_tensor(t3, steps, cols_bc(flo[:, 4 * h:4 * h + 4], SEQ), ALU.mult))
                o(dve.tensor_tensor(f, f, t, ALU.add))
                o(turn(dve, o, f, ph_n.bitcast(i32), t))
                o(quarter_on(dve, o, t, f, ph_n), ph_ready)

        def pe_ada(pe, pcs, base):
            for n, pc in enumerate(pcs):
                w = arrived(pe, pc)
                for k in range(KD):
                    m = pe.matmul(bank(base + n), condrep[:, k, :], w[:, k, :], start=(k == 0), stop=(k == KD - 1))
                m.then_inc(ada_ps, 1)

        def pe_s0(pe):
            pe.wait_ge(cond_ready, 1)
            pe_ada(pe, pc_ada, 0)
            pe_bias(pe)
            for n in range(4):
                pe.wait_ge(bc_ready, n + 1)
                if n >= 2:
                    pe.wait_ge(bc_ev, n - 1)
                src = (Bd + Cd)[n]
                for q in range(SQ):
                    m = pe.transpose(bank(6 + n % 2)[:, q * P:(q + 1) * P], src[:, q * P:(q + 1) * P], ident)
                m.then_inc(bc_ps, 1)

        def act_rms(act, o, srcs, junk, n):
            for t in range(TT):
                o(act.activation(junk, srcs[t], ACT.Square, accum_out=ssq[:, t:t + 1]), sq_done if t == TT - 1 else None)
            act.wait_ge(ms_done, n)
            o(act.activation(rms, rms, ACT.Sqrt), rt_done)

        def dve_rms(dve, o, n, width=D):
            dve.wait_ge(sq_done, n)
            o(dve.tensor_scalar(rms, ssq, 1.0 / width, EPS, ALU.mult, ALU.add), ms_done)
            dve.wait_ge(rt_done, n)
            o(dve.reciprocal(rms, rms))

        TURNS = ("mixer", "merged", "memory", "experts", "attention", "ffn0", "delta", "ffn1")
        NT, QT, OT = 9, 6, 3

        def turn_base(which):
            return 4 * TURNS.index(which) + (NT + QT + OT if which == "ffn1" else 0)

        D_BASE = 4 * (TURNS.index("delta") + 1)

        def pe_turn(pe, src3, which):
            for t in range(TT):
                pe.wait_ge(nat_ready, TT * TURNS.index(which) + t + 1)
                for b in range(2):
                    for k in range(4):
                        kk = 4 * b + k
                        m = pe.transpose(bank(2 * t + b)[:, k * P:(k + 1) * P], src3[:, t, kk * P:(kk + 1) * P], ident)
                    m.then_inc(turn_ps, 1)

        def act_turned(act, o, dst3, which):
            for t in range(TT):
                for b in range(2):
                    act.wait_ge(turn_ps, turn_base(which) + 2 * t + b + 1)
                    o(act.copy(dst3[:, 4 * b:4 * b + 4, t * P:(t + 1) * P],
                               bank(2 * t + b).rearrange("p (k m) -> p k m", k=4)), turned)

        def pe_after_turn(pe, which):
            pe.wait_ge(turned, turn_base(which) + 4)

        def act_s1(act, o):
            act_turned(act, o, hT, "mixer")

        def dve_s1(dve, o):
            for t in range(TT):
                o(dve.scalar_tensor_tensor(h_nat[:, t, :], x3[:, t, :], rms[:, t:t + 1], Am, ALU.mult, ALU.mult))
                o(dve.tensor_tensor(h_nat[:, t, :], h_nat[:, t, :], shm, ALU.add), nat_ready)

        def pe_s1(pe):
            pe_turn(pe, h_nat, "mixer")

        def pe_cols(pe, w, b0, src3, kn, done):
            for c in range(4):
                for k in range(kn):
                    m = pe.matmul(bank(b0 + c // 2)[:, (c % 2) * SEQ:(c % 2 + 1) * SEQ], w[:, k, c * P:(c + 1) * P],
                                  src3[:, k, :], start=(k == 0), stop=(k == kn - 1))
            m.then_inc(done, 1)

        def pe_rows(pe, w, banks, src3, kn, done):
            for t in range(TT):
                for k in range(kn):
                    m = pe.matmul(bank(banks[t]), src3[:, k, t * P:(t + 1) * P], w[:, k, :], start=(k == 0), stop=(k == kn - 1))
            m.then_inc(done, 1)

        def pe_s2(pe):
            pe_after_turn(pe, "mixer")
            pe.wait_ge(bc_ev, 4)
            pe_cols(pe, arrived(pe, pc_in[0]), 4, hT, KD, proj_ps)
            pe_cols(pe, arrived(pe, pc_in[1]), 6, hT, KD, proj_ps)
            pe_cols(pe, arrived(pe, pc_in[2]), 0, hT, KD, proj_ps)
            pe_rows(pe, arrived(pe, pc_in[3]), (2, 3), hT, KD, proj_ps)
            for n, raw in enumerate((qraw, kraw)):
                pe.wait_ge(proj_ev, n + 2)
                for b in range(2):
                    m = pe.matmul(bank(4 + 2 * n + b), con("rot"), raw[:, b * 512:(b + 1) * 512], start=True, stop=True)
                m.then_inc(rot_ps, 1)
            for n in range(2):
                ws = [arrived(pe, pc) for pc in pc_ada2[4 * n:4 * n + 4]]
                for k in range(KD):
                    for j, w in enumerate(ws):
                        m = pe.matmul(bank(n)[32 * j:32 * j + 32, :], cond32[:, k, :], w[:, k, :], start=(k == 0), stop=(k == KD - 1),
                                      tile_position=(0, 32 * j))
                m.then_inc(ada_ps, 1)

        def act_s2(act, o):
            act_tables(act, o, 0)
            act.wait_ge(proj_ps, 1)
            o(act.copy(uT.rearrange("p c s -> p (c s)"), bank(4, 2)), proj_ev)
            for n, raw in enumerate((qraw, kraw)):
                act_tables(act, o, 1 + n)
                act.wait_ge(proj_ps, 2 + n)
                o(act.copy(raw, bank(6 if n == 0 else 0, 2)), proj_ev)
            act_tables(act, o, 3)
            act.wait_ge(proj_ps, 4)
            o(act.copy(vN.rearrange("p t n -> p (t n)"), bank(2, 2)), proj_ev)
            act.wait_ge(ada_ps, 8)
            o(act.copy(adaS[:, 0:512], bank(0)), rows_ready)
            o(act.copy(adaS[0:64, 512:1024], bank(1)[0:64, :]), rows_ready)

        def dve_s2(dve, o):
            dve.wait_ge(rope_tab, 1)
            dve.wait_ge(bv_stored, 16 * 3)
            for n, (raw, dst) in enumerate(((qraw, qT), (kraw, kT))):
                dve.wait_ge(rot_ps, n + 1)
                o(dve.tensor_tensor(dst, raw.rearrange("p (c s) -> p c s", c=4), rows_bc(cosR, 4), ALU.mult))
                o(dve.tensor_tensor(rtmp, bank(4 + 2 * n, 2).rearrange("p (c s) -> p c s", c=4), rows_bc(sinR, 4), ALU.mult))
                o(dve.tensor_tensor(dst, dst, rtmp, ALU.add), rope_done)

        def at(i):
            return (i % 2) * 2 + i // 2

        def probs_of(n):
            return prob6[n - 6] if 6 <= n < 12 else prob[n % 2]

        def pe_scores(pe, u, q_of, k_of, bias=None):
            if bias is not None:
                for a in range(2):
                    pe.matmul(bank(2 * (u % 2) + a), con("flip"), bias[:, 2 * a:2 * a + 2, :], start=True, stop=False, skip_group_check=True)
            for i in range(HPG):
                m = pe.matmul(bank(2 * (u % 2) + i % 2)[:, (i // 2) * SEQ:(i // 2 + 1) * SEQ], q_of(i), k_of(i), start=bias is None, stop=True,
                              skip_group_check=bias is not None)
            m.then_inc(sc_ps, 1)

        def pe_probs(pe, u, n, v_of):
            pe.wait_ge(pr_ready, n + 1)
            if n:
                pe.wait_ge(prT_ready, n)
            for kb in range(2):
                for i in range(HPG):
                    m = pe.transpose(bank(4 + kb)[:, i * P:(i + 1) * P], probs_of(n)[:, at(i) * SEQ + kb * P:at(i) * SEQ + (kb + 1) * P], ident)
            m.then_inc(prT_ps, 1)
            pe.wait_ge(prT_ready, n + 1)
            if n >= 2:
                pe.wait_ge(pv_ev, n - 1)
            for i in range(HPG):
                for kb in range(2):
                    r = HD * (i % 2)
                    m = pe.matmul(bank(6 + n % 2)[r:r + HD, (i // 2) * P:(i // 2 + 1) * P], v_of(kb, i),
                                  prT[n % 2][:, kb * 512 + i * P:kb * 512 + (i + 1) * P], start=(kb == 0), stop=(kb == 1))
            m.then_inc(pv_ps, 1)

        def dve_less_max(dve, o, s3, raw, top, scale):
            o(dve.tensor_reduce(top, raw, AX.X, ALU.max))
            o(dve.tensor_scalar(top, top, scale, None, ALU.mult))
            o(dve.scalar_tensor_tensor(s3, raw, scale, cols_bc(top, SEQ), ALU.mult, ALU.subtract), sc_sub)

        def dve_softmax(dve, o, u, n, scale, bias, weigh=None):
            S = probs_of(n)
            s3 = S.rearrange("p (h k) -> p h k", h=HPG)
            dve.wait_ge(sc_ps, n + 1)
            if n >= 2:
                dve.wait_ge(prT_ps, n - 1)
            raw = bank(2 * (n % 2), 2).rearrange("p (h k) -> p h k", h=HPG)
            if bias is None:
                dve_less_max(dve, o, s3, raw, amax, scale)
            else:
                o(dve.scalar_tensor_tensor(s3, raw, scale, bias, ALU.mult, ALU.add))
                o(dve.tensor_reduce(amax, s3, AX.X, ALU.max))
                o(dve.tensor_tensor(s3, s3, cols_bc(amax, SEQ), ALU.subtract), sc_sub)
            dve.wait_ge(sc_exp, n + 1)
            o(dve.tensor_reduce(aden, s3, AX.X, ALU.add))
            o(dve.reciprocal(aden, aden))
            if weigh is not None:
                weigh()
            o(dve.tensor_tensor(s3, s3, cols_bc(aden, SEQ), ALU.mult), pr_ready)

        def dve_pv(dve, o, u, n, dst):
            dve.wait_ge(pv_ps, n + 1)
            o(dve.tensor_copy(dst, bank(6 + n % 2)[:, 0:SEQ].rearrange("p (c m) -> p c m", c=2)), pv_ev)

        def act_probs(act, o, u, n):
            act.wait_ge(sc_sub, n + 1)
            o(act.activation(probs_of(n), probs_of(n), ACT.Exp), sc_exp)
            act_probsT(act, o, n)

        def act_probsT(act, o, n):
            act.wait_ge(prT_ps, n + 1)
            if n >= 2:
                act.wait_ge(pv_ps, n - 1)
            o(act.copy(prT[n % 2], bank(4, 2)), prT_ready)

        U1 = [(g, t) for g in range(HEADS // HPG) for t in range(TT)]

        def pe_s4(pe):
            def scores(u):
                g, t = U1[u]
                pe.wait_ge(rope_done, 2)
                pe.wait_ge(rows_ready, 2)
                if u == 1:
                    pe.wait_ge(proj_ev, 4)
                if u >= 2:
                    pe.wait_ge(sc_sub, u - 1)
                def half(x, i):
                    return x[HD * (i % 2):HD * (i % 2) + HD, 2 * g + i // 2, :]
                pe_scores(pe, u, lambda i: half(qT, i)[:, t * P:(t + 1) * P], lambda i: half(kT, i))
            scores(0)
            for u, (g, t) in enumerate(U1):
                if u + 1 < len(U1):
                    scores(u + 1)
                pe_probs(pe, u, u, lambda kb, i: vN[:, kb, (HPG * g + i) * HD:(HPG * g + i + 1) * HD])

        def act_s4(act, o):
            for u in range(len(U1)):
                act_probs(act, o, u, u)

        def dve_s4(dve, o):
            for u, (g, t) in enumerate(U1):
                causal = spread(con("causal")[:, t * SEQ:(t + 1) * SEQ], [0, HPG], [1, SEQ])
                dve_softmax(dve, o, u, u, HD ** -0.5, causal)
                if u:
                    g0, t0 = U1[u - 1]
                    dve_pv(dve, o, u - 1, u - 1, yaT[:, 2 * g0:2 * g0 + 2, t0 * P:(t0 + 1) * P])
            dve_pv(dve, o, u, u, yaT[:, 2 * g:2 * g + 2, t * P:(t + 1) * P])

        def pe_s3(pe):
            def drive(q):
                if q:
                    pe.wait_ge(bu_read, q)
                for n, m_ in enumerate((BTr, BTi)):
                    for j in range(4):
                        m = pe.matmul(bank(j)[:, n * SEQ:(n + 1) * SEQ], m_[32 * j:32 * j + 32, q, :],
                                      uT[32 * j:32 * j + 32, q, :], start=True, stop=True, tile_position=(32 * j, 0))
                m.then_inc(bu_ps, 1)
            pe.wait_ge(sc_sub, len(U1))
            pe.wait_ge(pv_ev, len(U1))
            def gate(i):
                n, t = i // TT, i % TT
                if i >= 2:
                    pe.wait_ge(gate_ready, i - 1)
                w = arrived(pe, pc_gate[n])
                for k in range(KD):
                    m = pe.matmul(bank(4 + t), hT[:, k, t * P:(t + 1) * P], w[:, k, :], start=(k == 0), stop=(k == KD - 1))
                m.then_inc(gate_ps, 1)

            def y_of(q):
                pe.wait_ge(st_ready, q + 1)
                if q >= 2:
                    pe.wait_ge(y_ready, q - 1)
                for j in range(4):
                    for n, (c_, x_) in enumerate(((CTr, sT), (CTi, sU))):
                        m = pe.matmul(bank(6 + q % 2)[32 * j:32 * j + 32, 0:SEQ], c_[:, q, 32 * j:32 * j + 32], x_[:, j, :],
                                      start=(n == 0), stop=(n == 1), tile_position=(0, 32 * j))
                m.then_inc(y_ps, 1)
            drive(0)
            gate(0)
            gate(1)
            for q in range(SQ - 1):
                drive(q + 1)
                gate(2 + 2 * q)
                y_of(q)
                gate(3 + 2 * q)
            y_of(SQ - 1)
            pe.wait_ge(bu_read, SQ)
            pe_branch(pe, pc_wa, yaT, 0)
            pe.wait_ge(gate_ready, 8)
            pe.wait_ge(gel_ready, 1)
            pe_cols(pe, arrived(pe, pc_glu), 4, gel, SQ, out_ps)

        def pe_branch(pe, pc, src, b0):
            w = arrived(pe, pc)
            for t in range(TT):
                for c in range(2):
                    for k in range(4):
                        m = pe.matmul(bank(b0 + 2 * t + c), src[:, k, t * P:(t + 1) * P], w[:, k, c * 512:(c + 1) * 512],
                                      start=(k == 0), stop=(k == 3))
            m.then_inc(out_ps, 1)

        def act_s3(act, o):
            for i in range(4 * TT):
                n, t = i // TT, i % TT
                act.wait_ge(gate_ps, i + 1)
                dst = (sgs if n < 2 else sga)[:, t, (n % 2) * 512:(n % 2 + 1) * 512]
                o(act.activation(dst, bank(4 + t), ACT.Sigmoid), gate_ready)
            act.wait_ge(y_ready, SQ)
            o(act.activation(gel.rearrange("p q s -> p (q s)"), yT.rearrange("p q s -> p (q s)"), ACT.Gelu_apprx_tanh), gel_ready)
            act.wait_ge(out_ps, 2)
            o(act.activation(sglu.rearrange("p q s -> p (q s)"), bank(4, 2), ACT.Sigmoid), gel_ready)

        def dve_s3(dve, o):
            dve.wait_ge(tab_ready, 8)

            def y_out(q):
                dve.wait_ge(y_ps, q + 1)
                o(dve.scalar_tensor_tensor(yT[:, q, :], uT[:, q, :], dcol[:, q:q + 1], bank(6 + q % 2)[:, 0:SEQ],
                                           ALU.mult, ALU.add), y_ready)
            for q in range(SQ):
                cq, sq = cosS[:, 4 * q:4 * q + 4, :], sinS[:, 4 * q:4 * q + 4, :]
                re, im = (bank(0, 4).rearrange("p (j c s) -> p j c s", j=4, c=2)[:, :, n, :] for n in range(2))
                dve.wait_ge(bu_ps, q + 1)
                if q:
                    y_out(q - 1)
                o(dve.tensor_tensor(sA, re, cq, ALU.mult))
                o(dve.tensor_tensor(sT, im, sq, ALU.mult))
                o(dve.tensor_tensor(sA, sA, sT, ALU.add))
                o(dve.tensor_tensor(sB, im, cq, ALU.mult))
                o(dve.tensor_tensor(sT, re, sq, ALU.mult), bu_read)
                o(dve.tensor_tensor(sB, sB, sT, ALU.subtract))
                for x_ in (sA, sB):
                    for j in range(4):
                        o(dve.tensor_tensor_scan(x_[:, j, :], cols_bc(mag[:, 4 * q + j], SEQ), x_[:, j, :], 0.0, ALU.mult, ALU.add))
                o(dve.tensor_tensor(sT, sA, cq, ALU.mult))
                o(dve.tensor_tensor(sU, sB, sq, ALU.mult))
                o(dve.tensor_tensor(sT, sT, sU, ALU.subtract))
                o(dve.tensor_tensor(sU, sA, sq, ALU.mult))
                o(dve.tensor_tensor(sB, sB, cq, ALU.mult))
                o(dve.scalar_tensor_tensor(sU, sU, -1.0, sB, ALU.mult, ALU.subtract), st_ready)
            y_out(SQ - 1)
            dve.wait_ge(out_ps, 1)
            dve.wait_ge(gate_ready, 8)
            for t in range(TT):
                o(dve.tensor_tensor(mgd[:, t, :], sga[:, t, :], bank(2 * t, 2), ALU.mult))
            dve.wait_ge(gel_ready, 2)
            o(dve.tensor_tensor(ysT, gel, sglu, ALU.mult), ys_ready)

        def pe_s5(pe):
            pe.wait_ge(ys_ready, 1)
            pe_branch(pe, pc_ws, ysT, 4)
            pe_turn(pe, mgd, "merged")
            pe_after_turn(pe, "merged")

            def mod_rows(blocks):
                for n in blocks:
                    j = 32 * (n % 4)
                    one = CON[j:j + 1, names["ones"][0]:names["ones"][0] + P]
                    m = pe.matmul(bank(n % 4), one, adaS[j:j + 1, n // 4 * 512:(n // 4 + 1) * 512], start=True, stop=True, tile_position=(j, 0))
                m.then_inc(mod_ps, 1)
            pe_rows(pe, arrived(pe, pc_out[0]), (4, 6), mgT, KD, out_ps)
            pe_turn(pe, mem_nat, "memory")
            pe_after_turn(pe, "memory")
            mod_rows(range(4))
            pe_rows(pe, arrived(pe, pc_out[1]), (5, 7), mgT, KD, out_ps)
            pe.wait_ge(mod_read, 1)
            mod_rows(range(4, 6))
            pe_kv(pe, 0)

        def pe_kv(pe, i):
            w = arrived(pe, pc_mem[i])
            pe.wait_ge(mem_ready, 2)
            for c in range(2):
                for k in range(KD):
                    pe.matmul(bank(2)[:, c * SEQ:(c + 1) * SEQ], w[:, k, c * P:(c + 1) * P], mem_T[i][:, k, :], start=(k == 0), stop=(k == KD - 1))
            for t in range(TT):
                for k in range(KD):
                    m = pe.matmul(bank(3)[:, t * MW:(t + 1) * MW], mem_T[i][:, k, t * P:(t + 1) * P], w[:, k, MW:2 * MW],
                                  start=(k == 0), stop=(k == KD - 1))
            m.then_inc(mkv_ps, 1)

        def act_kv(act, o, i):
            act.wait_ge(mkv_ps, i + 1)
            o(act.copy(kvM[i], bank(2, 2)), mkv_ready)

        def dve_s5(dve, o):
            dve.wait_ge(out_ps, 3)
            for t in range(TT):
                o(dve.tensor_tensor(mtmp, sgs[:, t, :], bank(4 + 2 * t, 2), ALU.mult))
                o(dve.tensor_tensor(mgd[:, t, :], mgd[:, t, :], mtmp, ALU.add), nat_ready)
            dve_rms(dve, o, 2)
            for t in range(TT):
                o(dve.tensor_scalar(mem_nat[:, t, :], mem_nat[:, t, :], rms[:, t:t + 1], None, ALU.mult), nat_ready)
            dve.wait_ge(rout_in, 16 * 7)
            dve.wait_ge(mod_ps, 1)
            o(dve.tensor_tensor(Bf, Bf, bank(0, 2), ALU.add))
            o(dve.scalar_tensor_tensor(Af, bank(2, 2), 1.0, Af, ALU.add, ALU.add), mod_read)
            o(dve.tensor_tensor(Af, Af, gpre2, ALU.mult))
            dve.wait_ge(mod_ps, 2)
            o(dve.tensor_tensor(GTf, GTf, bank(0, 2), ALU.add))
            o(dve.tensor_tensor(GTf, GTf, gpost2, ALU.mult))
            dve_rms(dve, o, 3)
            for t in range(TT):
                o(dve.scalar_tensor_tensor(mtmp, bank(4 + 2 * t, 2), rms[:, t:t + 1], GTm, ALU.mult, ALU.mult))
                o(dve.tensor_tensor(x3[:, t, :], x3[:, t, :], mtmp, ALU.add), x1_ready)

        def act_s5(act, o):
            act_turned(act, o, mgT, "merged")
            act.wait_ge(mem_in, 32)
            act_rms(act, o, [mem_nat[:, t, :] for t in range(TT)], ar(10240, D), 2)
            act_turned(act, o, mem_T[0], "memory")
            act.wait_ge(out_ps, 5)
            act_rms(act, o, [bank(4 + 2 * t, 2) for t in range(TT)], ar(10240, D), 3)
        FIRST = len(pieces)
        E_SLOT = [(FIRST + i) % SLOTS for i in range(SLOTS)]
        E_USED = [filled[s] for s in E_SLOT]
        assert SLOTS == 6
        rout_in = sem("rout_in")
        odd_ready = [sem(f"odd_gate_ready{h}") for h in range(2)]
        (mk_ready, pos_ready, wT_ready, bias_in) = (sem(n) for n in (
            "mk_ready", "pos_ready", "wT_ready", "bias_in"))
        ff_ps, x2_ready = sem("ff_ps"), sem("x2_ready")

        class Steps:

            def __init__(self, kind):
                self.p_ready = sem(kind + "_p_ready")
                self.pw_ready = sem(kind + "_pw_ready")
                self.x_ps = sem(kind + "_x_ps")
                self.x_ready = sem(kind + "_x_ready")
                self.pwT_ps = sem(kind + "_pwT_ps")
                self.pwT_ready = sem(kind + "_pwT_ready")
                self.g_ps = sem(kind + "_g_ps")
                self.u_ps = sem(kind + "_u_ps")
                self.gm_ready = sem(kind + "_gm_ready")
                self.sg_ready = sem(kind + "_sg_ready")
                self.a_ready = sem(kind + "_a_ready")
                self.aT_ps = sem(kind + "_aT_ps")
                self.aT_ready = sem(kind + "_aT_ready")
                self.d_ps = sem(kind + "_d_ps")
                self.y_out = sem(kind + "_y_out")

        main, extra = Steps("first"), Steps("further")

        Bf, Af, GTf = ar(0, D), ar(D, D), ar(12288, D)
        gpre2, gpost2 = ar(11264, D), ar(19456, D)
        odd_gate = [ar(0, SLOT_W), ar(8192, SLOT_W)]
        h2 = ar3(6144, 2048, TT)
        h2T = ar3(8192, 2048, KD)
        rw, rb = ar3(13312, 256, KD), ar(13568, E)
        lg, top8, idx8, idxf = ar3(13600, 64, TT), ar3(13664, 16, TT), ar3(13680, 16, TT), ar3(13696, 16, TT)
        ew, esum, eqt = ar3(13712, 8, TT), ar(13720, TT), ar(13728, E)
        mk = ar3(13792, 64, TT)
        wt, posm = ar3(13856, TT * (E + 1), TT), ar3(13924, TT * (E + 1), TT)
        cnt = ar(14016, E).bitcast(i32)
        wT = ar(14048, SEQ, E)
        bgs, bus, bds = ar(20480, FF, E), ar(21504, FF, E), ar(19456, D, E)
        Psel, Pw = ar3(17408, 256, TT), ar3(17664, 256, TT)
        PwT, Ee = [ar(17920, SEQ), ar(14048, SEQ)], [ar(18176 + CAP * n, CAP, E) for n in range(2)]
        XT = ar3(18432, 1024, KD)
        XTf, PwTf = ar3(19456, 1024, KD), ar(13312, SEQ)
        gm, um, sg, act_, actT, Yb = (ar(14336 + 512 * n, 512) for n in range(6))

        def pool_s6(pool):
            pool.wait_ge(out_ps, 3)
            for n, d in enumerate((Bf, Af, GTf)):
                dma(pool, d, row(A["ada_b"][0][(3 + n) * D:(4 + n) * D]), rout_in)
            dma(pool, gpre2, row(A["ffn_pre_g"][0]), rout_in)
            dma(pool, gpost2, row(A["ffn_post_g"][0]), rout_in)
            dma(pool, rw, A["router_w"][0].rearrange("(k p) e -> p k e", p=P), rout_in)
            dma(pool, rb, row(A["router_b"][0]), rout_in)
            pool.wait_ge(nat_ready, 2 * TT)
            dma(pool, mem_nat, A["mem_2"][0].rearrange("(t p) d -> p t d", p=P), mem_in)
            pool.wait_ge(turned, turn_base("memory") + 4)
            for i in (1, 0):
                pool.tensor_tensor(mem_T[i], mem_T[0], cols_bc(mem_g[:, i, :], SEQ), ALU.mult).then_inc(mem_ready, 1)
            pool.wait_ge(x1_ready, 1)
            for d, a in ((bds, "b_down"), (bgs, "b_gate"), (bus, "b_up")):
                dma(pool, d, A[a][0], bias_in)

        def pe_s6(pe):
            pe.wait_ge(mkv_ready, 1)
            pe_turn(pe, h2, "experts")
            pe_after_turn(pe, "experts")
            pe.wait_ge(rout_in, 16 * 7)
            for t in range(TT):
                for k in range(KD):
                    m = pe.matmul(bank(6)[:, t * E:(t + 1) * E], h2T[:, k, t * P:(t + 1) * P], rw[:, k, :],
                                  start=(k == 0), stop=(k == KD - 1))
            m.then_inc(router_ps, 1)
            pe_kv(pe, 1)
            pe.wait_ge(mk_ready, 1)
            pe.matmul(bank(7)[:, 0:E], con("before"), mk[:, 0, :], start=True, stop=True)
            pe.matmul(bank(7)[:, E:2 * E], con("before"), mk[:, 1, :], start=True, stop=False)
            pe.matmul(bank(7)[:, E:2 * E], con("ones"), mk[:, 0, :], start=False, stop=True)
            for t in range(TT):
                m = pe.matmul(bank(7)[:, 2 * E:3 * E], con("ones"), mk[:, t, :], start=(t == 0), stop=(t == 1))
            m.then_inc(router_ps, 1)
            for t in range(TT):
                m = pe.transpose(bank(0, 1, E)[:, t * P:(t + 1) * P], wt[:, t, 0:E], ident)
            m.then_inc(router_ps, 1)
            pe.wait_ge(wT_ready, 1)
            pe.wait_ge(pos_ready, 1)
            pe.wait_ge(bias_in, 48)
            for t in range(TT):
                for d in range(2):
                    m = pe.matmul(bank(4 + 2 * t + d), wT[:, t * P:(t + 1) * P], bds[:, d * 512:(d + 1) * 512],
                                  start=True, stop=False, skip_group_check=True)
                m.then_inc((extra.u_ps, extra.d_ps)[t], 1)

        def act_s6(act, o):
            act.wait_ge(x1_ready, 2)
            act_rms(act, o, [x3[:, t, :] for t in range(TT)], ar(10240, D), 4)
            act_kv(act, o, 0)
            act_turned(act, o, h2T, "experts")
            act.wait_ge(fn_asked, 1)
            o(act.activation(ew, ew, ACT.Exp), fn_done)
            act_kv(act, o, 1)
            act.wait_ge(router_ps, 4)
            o(act.copy(wT, bank(0, 1, E)[:, 0:SEQ]), wT_ready)

        def dve_s6(dve, o):
            dve_rms(dve, o, 4)
            for t in range(TT):
                o(dve.scalar_tensor_tensor(h2[:, t, :], x3[:, t, :], rms[:, t:t + 1], Af, ALU.mult, ALU.mult))
                o(dve.tensor_tensor(h2[:, t, :], h2[:, t, :], Bf, ALU.add), nat_ready)
            dve.wait_ge(router_ps, 2)
            o(dve.tensor_tensor(lg, bank(6)[:, 0:2 * E].rearrange("p (t e) -> p t e", t=TT), rows_bc(rb, TT), ALU.add))
            for t in range(TT):
                o(dve.max(top8[:, t, :], lg[:, t, :]))
                o(dve.max_index(idx8[:, t, :].bitcast(u32), top8[:, t, :], lg[:, t, :]))
            o(dve.tensor_copy(idxf, idx8.bitcast(u32)))
            for t in range(TT):
                o(dve.tensor_scalar(ew[:, t, :], top8[:, t, 0:TOPK], top8[:, t, 0:1], None, ALU.subtract),
                  fn_asked if t == TT - 1 else None)
            for t in range(TT):
                o(dve.tensor_scalar(mk[:, t, :], con("experts"), idxf[:, t, 0:1], None, ALU.is_equal))
                for k in range(1, TOPK):
                    o(dve.scalar_tensor_tensor(mk[:, t, :], con("experts"), idxf[:, t, k:k + 1], mk[:, t, :], ALU.is_equal, ALU.add))
            dve.wait_ge(fn_done, 1)
            o(dve.tensor_reduce(esum, ew, AX.X, ALU.add))
            o(dve.reciprocal(esum, esum))
            o(dve.tensor_tensor(ew, ew, cols_bc(esum, TOPK), ALU.mult))
            for t in range(TT):
                o(dve.tensor_scalar(wt[:, t, 0:E], con("experts"), idxf[:, t, 0:1], ew[:, t, 0:1], ALU.is_equal, ALU.mult))
                for k in range(1, TOPK):
                    o(dve.tensor_scalar(eqt, con("experts"), idxf[:, t, k:k + 1], ew[:, t, k:k + 1], ALU.is_equal, ALU.mult))
                    last = dve.tensor_tensor(wt[:, t, 0:E], wt[:, t, 0:E], eqt, ALU.add)
                    o(last, mk_ready if (t, k) == (TT - 1, TOPK - 1) else None)
            dve.wait_ge(router_ps, 3)
            o(dve.memset(posm, 0.0))
            o(dve.memset(wt[:, :, E:E + 1], 0.0))
            o(dve.scalar_tensor_tensor(posm[:, :, 0:E], bank(7)[:, 0:2 * E].rearrange("p (t e) -> p t e", t=TT), 1.0, mk, ALU.add, ALU.mult))
            o(dve.tensor_scalar(posm, posm, -1.0, None, ALU.add))
            o(dve.tensor_copy(cnt, bank(7)[:, 2 * E:3 * E]), pos_ready)

        W7 = [RING[:, i * SLOT_W:(i + 1) * SLOT_W] for i in E_SLOT]
        gate_w = [[x.rearrange("p (k n) -> p k n", k=KD) for x in xs] for xs in (W7[0:2], odd_gate)]
        up_w = [W7[2 + h].rearrange("p (k n) -> p k n", k=KD) for h in range(2)]
        down_w = [W7[4 + h].rearrange("p (k n) -> p k n", k=4) for h in range(2)]

        def slot_iota(r, n):
            a = names["slots"][0] + r * 2 * CAP
            return CON[:, a:a + n]

        def dve_choose(dve, s, e, r, odd):
            for t in range(TT):
                dve.tensor_scalar(Psel[:, t, :], slot_iota(r, 2 * CAP), posm[:, t, bass.ds(e, 1)], None, ALU.is_equal)
            dve.drain()
            dve.tensor_copy(Ee[odd], ident[0:E, bass.ds(e, 1)].to_broadcast([E, CAP])).then_inc(s.p_ready, 1)
            for t in range(TT):
                m = dve.tensor_scalar(Pw[:, t, :], slot_iota(r, 2 * CAP), posm[:, t, bass.ds(e, 1)], wt[:, t, bass.ds(e, 1)],
                                      ALU.is_equal, ALU.mult)
                if t == 0:
                    dve.drain()
            m.then_inc(s.pw_ready, 1)

        def dve_glu(dve, s, n, more=0):
            dve.wait_ge(s.g_ps, n)
            dve.tensor_scalar(gm, bank(0), LIMIT, None, ALU.min).then_inc(s.gm_ready, 1)
            dve.wait_ge(s.u_ps, n + more)
            dve.tensor_scalar(um, bank(1), LIMIT, -LIMIT, ALU.min, ALU.max)
            dve.drain()
            dve.scalar_tensor_tensor(um, um, 1.0, gm, ALU.add, ALU.mult)
            dve.drain()
            dve.wait_ge(s.sg_ready, n)
            dve.tensor_tensor(act_, um, sg, ALU.mult).then_inc(s.a_ready, 1)

        def act_gathered(act, s, n, xT, before=None):
            for b in range(2):
                act.wait_ge(s.x_ps, n * 2 if before is None else before + 1 + b)
                act.copy(xT[:, 4 * b:4 * b + 4, :].rearrange("p k m -> p (k m)"), bank(2 + b)).then_inc(s.x_ready, 1)

        def act_weights(act, s, n, pwT):
            act.wait_ge(s.pwT_ps, n)
            act.copy(pwT, bank(3)[:, 0:SEQ]).then_inc(s.pwT_ready, 1)

        def act_sigmoid(act, s, n):
            act.wait_ge(s.gm_ready, n)
            act.activation(sg, gm, ACT.Sigmoid, scale=ALPHA).then_inc(s.sg_ready, 1)

        def act_hidden(act, s, n):
            act.wait_ge(s.aT_ps, n)
            act.copy(actT, bank(2)).then_inc(s.aT_ready, 1)

        def act_out(act, s, n, more=0):
            act.wait_ge(s.d_ps, n + more)
            act.copy(Yb, bank(1)).then_inc(s.y_out, 1)

        def pe_gather(pe, s, n):
            pe.wait_ge(s.p_ready, n)
            for k in range(KD):
                for t in range(TT):
                    m = pe.matmul(bank(2 + k // 4)[:, (k % 4) * P:(k % 4 + 1) * P], h2[:, t, k * P:(k + 1) * P], Psel[:, t, :],
                                  start=(t == 0), stop=(t == 1))
                if k % 4 == 3:
                    m.then_inc(s.x_ps, 1)

        def pe_weights(pe, s, n):
            pe.wait_ge(s.pw_ready, n)
            pe.wait_ge(s.x_ready, n * 2)
            for t in range(TT):
                m = pe.transpose(bank(3)[:, t * P:(t + 1) * P], Pw[:, t, :], ident)
            m.then_inc(s.pwT_ps, 1)

        def pe_gate_up(pe, s, n, odd, xT, weights):
            pe.wait_ge(s.x_ready, n * 2)
            for i, (w, b_, done) in enumerate(((gate_w[odd], bgs, s.g_ps), (up_w, bus, s.u_ps))):
                weights(i)
                for k in range(KD):
                    for h in range(2):
                        pe.matmul(bank(i)[h * CAP:(h + 1) * CAP, :], xT[:, k, 0:CAP], w[h][:, k, :], start=(k == 0), stop=False)
                for h in range(2):
                    m = pe.matmul(bank(i)[h * CAP:(h + 1) * CAP, :], Ee[odd], b_[:, h * 512:(h + 1) * 512], start=False, stop=True)
                m.then_inc(done, 1)

        def pe_hidden(pe, s, n):
            pe.wait_ge(s.a_ready, n)
            for j in range(4):
                m = pe.transpose(bank(2)[:, j * P:(j + 1) * P], act_[:, j * P:(j + 1) * P], ident)
            m.then_inc(s.aT_ps, 1)

        def pe_down(pe, s, n, weights, pwT):
            weights(2)
            pe.wait_ge(s.aT_ready, n)
            for h in range(2):
                for j in range(4):
                    for d in range(2):
                        m = pe.matmul(bank(1)[d * CAP:(d + 1) * CAP, :], actT[:, j * P + h * CAP:j * P + (h + 1) * CAP],
                                      down_w[h][:, j, d * 512:(d + 1) * 512], start=(h + j == 0), stop=(h + j == 4))
            m.then_inc(s.d_ps, 1)
            pe.wait_ge(s.y_out, n)
            for t in range(TT):
                for d in range(2):
                    m = pe.matmul(bank(4 + 2 * t + d), pwT[d * CAP:(d + 1) * CAP, t * P:(t + 1) * P], Yb[d * CAP:(d + 1) * CAP, :],
                                  start=False, stop=False, skip_group_check=True)

        def pe_main(pe, e, odd, weights):
            n = e + 1
            pe_gate_up(pe, main, n, odd, XT, weights)
            pe.wait_ge(main.pwT_ready, n)
            pe_gather(pe, main, n + 1)
            pe.wait_ge(main.x_ready, n * 2 + 1)
            pe_hidden(pe, main, n)
            pe_weights(pe, main, n + 1)
            pe_down(pe, main, n, weights, PwT[odd])

        def act_main(act, e, odd):
            n = e + 1
            act_sigmoid(act, main, n)
            act_gathered(act, main, n + 1, XT, n * 2)
            act_hidden(act, main, n)
            act_weights(act, main, n + 1, PwT[1 - odd])
            act_out(act, main, n)

        def dve_main(dve, e, odd):
            n = e + 1
            dve.wait_ge(main.pwT_ps, n)
            dve_choose(dve, main, e + 1, 0, 1 - odd)
            dve_glu(dve, main, n)

        def pe_further(pe, e, odd, n):
            pe.wait_ge(main.pwT_ready, e + 2)
            pe_gather(pe, extra, n)
            pe_weights(pe, extra, n)
            pe_gate_up(pe, extra, n, odd, XTf, lambda i: None)
            pe.wait_ge(extra.x_ready, n * 2)
            pe_hidden(pe, extra, n)
            pe.wait_ge(extra.pwT_ready, n)
            pe_down(pe, extra, n, lambda i: None, PwTf)

        def act_further(act, n):
            act_gathered(act, extra, n, XTf)
            act_weights(act, extra, n, PwTf)
            act_sigmoid(act, extra, n)
            act_hidden(act, extra, n)
            act_out(act, extra, n, 1)

        def dve_further(dve, e, odd, r, n):
            dve.wait_ge(main.pwT_ps, e + 2)
            dve_choose(dve, extra, e, r, odd)
            dve_glu(dve, extra, n, 1)

        def further(eng, e, rounds_of, body=None):
            n_e = eng.value_load(cnt[0:1, bass.ds(e, 1)], min_val=0, max_val=SEQ)

            def deeper(r):
                with eng.If(n_e > r * CAP):
                    eng.reg_add(rounds_of, rounds_of, 1)
                    if body is not None:
                        body(r, eng.snap(rounds_of))
                    if r + 1 < ROUNDS:
                        deeper(r + 1)
            deeper(1)

        def expert_rounds(eng, first_round, extra_round):
            eng.wait_ge(pos_ready, 1)
            taken = eng.alloc_register(f"further_{eng.engine.name}")
            eng.reg_mov(taken, 0)
            with eng.Fori(0, E // 2) as i:
                for odd in range(2):
                    e = i * 2 + odd
                    first_round(i, e, odd)
                    further(eng, e, taken, lambda r, n: extra_round(e, odd, r, n))

        def pe_s7(pe):
            def first(i, e, odd):
                def weights(n):
                    for h in range(2):
                        if n == 0:
                            there, before = (odd_ready[h], 0) if odd else (slot_ready[E_SLOT[h]], E_USED[h])
                            pe.wait_ge(there, i * 16 + 16 * (before + 1))
                        else:
                            pe.wait_ge(slot_ready[E_SLOT[2 * n + h]], e * 16 + 16 * (E_USED[2 * n + h] + 1))
                pe_main(pe, e, odd, weights)
            pe_gather(pe, main, 1)
            pe_weights(pe, main, 1)
            expert_rounds(pe, first, lambda e, odd, r, n: pe_further(pe, e, odd, n))
            pe.wait_ge(main.y_out, E)

        def dve_s7(dve):
            dve_choose(dve, main, 0, 0, 0)
            expert_rounds(dve, lambda i, e, odd: dve_main(dve, e, odd), lambda e, odd, r, n: dve_further(dve, e, odd, r, n))

        def act_s7(act):
            act_gathered(act, main, 1, XT)
            act_weights(act, main, 1, PwT[0])
            expert_rounds(act, lambda i, e, odd: act_main(act, e, odd), lambda e, odd, r, n: act_further(act, n))

        def load_in(sp, name, e, odd=0):
            i = ("w_gate", "w_up", "w_down").index(name)
            w = A[name][0][e:e + 1] if isinstance(e, int) else A[name][0][bass.ds(e, 1)]
            for h in range(2):
                if i < 2:
                    src, dst = w[:, :, h * 512:(h + 1) * 512], (gate_w[odd], up_w)[i][h]
                else:
                    src, dst = w[:, h * 512:(h + 1) * 512, :], down_w[h]
                there = odd_ready[h] if i == 0 and odd else slot_ready[E_SLOT[2 * i + h]]
                sp.dma_start(dst, src.rearrange("a (k p) n -> p (a k) n", p=P)).then_inc(there, 16)

        def sp_s7(sp):
            for i, name in enumerate(("w_gate", "w_up", "w_down")):
                if name == "w_down":
                    sp.wait_ge(router_ps, 2)
                    load_in(sp, "w_gate", 1, 1)
                for h in range(2):
                    used = pieces[FIRST - SLOTS + 2 * i + h]
                    sp.wait_ge(used[1], used[2])
                load_in(sp, name, 0)
            sp.wait_ge(pos_ready, 1)
            taken = sp.alloc_register("further_SP")
            sp.reg_mov(taken, 1)

            def behind(e, i, odd):
                further(sp, e, taken)
                sp.wait_ge(main.u_ps, e + 1)
                sp.wait_ge(extra.u_ps, taken)
                load_in(sp, "w_up", e + 1)
                sp.wait_ge(main.d_ps, e + 1)
                sp.wait_ge(extra.d_ps, taken)
                load_in(sp, "w_down", e + 1)
                if i is not None:
                    load_in(sp, "w_gate", e + 2, odd)
            with sp.Fori(0, E // 2 - 1) as i:
                for odd in range(2):
                    behind(i * 2 + odd, i, odd)
            behind(E - 2, None, 0)

        def post(dve, o, n, b0, gain, tells, tmp):
            dve_rms(dve, o, n)
            for t in range(TT):
                o(dve.scalar_tensor_tensor(tmp, bank(b0 + 2 * t, 2), rms[:, t:t + 1], gain, ALU.mult, ALU.mult))
                o(dve.tensor_tensor(x3[:, t, :], x3[:, t, :], tmp, ALU.add), tells)

        def act_s8(act, o):
            act.wait_ge(ff_ps, 1)
            o(act.copy(kvNow, kvM[0]), mkv_ready)
            o(act.copy(kvKept, kvM[1]))
            act_rms(act, o, [bank(4 + 2 * t, 2) for t in range(TT)], ar(10240, D), 5)

        def dve_s8(dve, o):
            post(dve, o, 5, 4, GTf, x2_ready, ar(0, D))

        def pe_s8(pe):
            for t in range(TT):
                for d in range(2):
                    m = pe.matmul(bank(4 + 2 * t + d), con("zero_rows", E), bgs[:, d * 512:(d + 1) * 512],
                                  start=False, stop=True, skip_group_check=True)
            m.then_inc(ff_ps, 1)
        gain_in = sem("gain_in")
        (post_done, gu_ps, gu_silu, gu_done, dn_ps, ffn_done) = (sem(n) for n in (
            "post_done", "gu_ps", "gu_silu", "gu_done", "dn_ps", "ffn_done"))
        bm_in, out_stored = sem("bm_in"), sem("out_stored")
        pc_ao, pc_gu, pc_dn = [], [], []
        MOE_PIECES = SLOTS
        LAST = FIRST + MOE_PIECES

        for i in range(SLOTS):
            pieces.append((None, (main.g_ps, main.u_ps, main.d_ps)[i // 2], E - 1 if i < 2 else E))
            filled[E_SLOT[i]] += E // 2 if i < 2 else E
        def layer_pieces(i):
            if i == 0:
                w = A["att_w_in_2"][0]
                pc_at.extend(piece(by_k(w, n * 512, n * 512 + 512), proj_ps, 5 + i_) for i_, n in enumerate((4, 0, 1, 2, 3)))
                w = A["att_w_out_2"][0]
            else:
                w = A["dn_w_in_2"][0]
                pc_dw.extend(piece(by_k(w, n * 512, min(n * 512 + 512, w.shape[1])), proj_ps, 10 + i_) for i_, n in enumerate((6, 0, 1, 2, 3, 4, 5)))
                w = A["dn_w_out_2"][0]
            pc_ao.append([piece(by_k(w, n * 512, n * 512 + 512), out_ps, 5 + 2 * i + n + 1) for n in range(2)])
            w = A["ffn_w_gate_up_2"][i]
            pc_gu.append([piece(by_k(w, n * 512, n * 512 + 512), gu_ps, 11 * i + n + 1) for n in range(11)])
            w = A["ffn_w_down_2"][i].rearrange("(k p) n -> p k n", p=P)
            pc_dn.append([piece(w[:, n * 4:min(n * 4 + 4, FC2), :], dn_ps, 6 * i + n + 1) for n in range(6)])
        pc_at, pc_dw = [], []
        layer_pieces(0)
        layer_pieces(1)

        gA, gB = ar(2048, D), ar(3072, D)
        hn = ar3(6144, 2048, TT)
        yA = ar3(6144, 2048, KD)
        hT2 = ar3(8192, 2048, KD)
        kmT, vm = kv_of(kvNow)
        prob6 = [ar(4096, 1024), ar(5120, 1024), ar(8192, 1024)] + [ar(15360 + 1024 * n, 1024) for n in range(3)]
        qkA = ar3(10240, 3072, 12)
        vA = ar3(13312, 1536, TT)
        qmA = ar3(14848, 512, 2)
        BM = [[ar3(15360 + 1024 * (3 * t + g), 1024, HPG) for g in range(3)] for t in range(TT)]
        mx3, dn3, em3 = ([ar3(9216 + 40 * t + 12 * n, 12, 3) for t in range(TT)] for n in range(3))
        mxx = [ar(9216 + 40 * t + 36, HPG) for t in range(TT)]
        actF = ar3(10240, FC2 * SEQ, FC2)
        sil = [ar(16384, 512), ar(16896, 512)]
        tmpP = ar(4096, D)
        tmpJ = ar(5120, D)

        PRE = ("attention", "ffn0", "delta", "ffn1")

        def act_pre(act, o, n_rms, k):
            act_rms(act, o, [x3[:, t, :] for t in range(TT)], tmpJ, n_rms)
            act_turned(act, o, hT2, PRE[k])

        def dve_pre(dve, o, n_rms, k, gains):
            dve_rms(dve, o, n_rms)
            dve.wait_ge(gain_in, 16 * gains)
            for t in range(TT):
                o(dve.scalar_tensor_tensor(hn[:, t, :], x3[:, t, :], rms[:, t:t + 1], gA, ALU.mult, ALU.mult), nat_ready)

        def pe_pre(pe, k):
            pe_turn(pe, hn, PRE[k])
            pe_after_turn(pe, PRE[k])

        def pool_gains(pool, i, names2):
            for d, a in zip((gA, gB), names2):
                dma(pool, d, row(A[a][i]), gain_in)

        def half_head(x, c0, i):
            return x[HD * (i % 2):HD * (i % 2) + HD, c0 + i // 2, :]

        MU = (4, 12)

        def pe_mem_scores(pe, i, qm):
            for t in range(TT):
                n = MU[i] + t
                pe.wait_ge(sc_sub, n - 1)
                pe_scores(pe, n, lambda i_: half_head(qm, 0, i_)[:, t * P:(t + 1) * P], lambda i_: half_head(kmT, 0, i_))

        def pe_mem_probs(pe, i):
            for t in range(TT):
                pe_probs(pe, MU[i] + t, MU[i] + t, lambda kb, i_: vm[:, kb, i_ * HD:(i_ + 1) * HD])

        def pe_out(pe, i):
            for n, pc in enumerate(pc_ao[i]):
                pe_rows(pe, arrived(pe, pc), (4 + n, 6 + n), yA, KD, out_ps)

        def pe_ffn(pe, i):
            pe_pre(pe, 2 * i + 1)
            pe.wait_ge(post_done, 2 * (i + 1))
            for n, pc in enumerate(pc_gu[i]):
                w = arrived(pe, pc)
                if n >= 2:
                    pe.wait_ge(gu_done, 11 * i + n - 1)
                b0 = 4 + 2 * (n % 2)
                for g in range(2):
                    for c in range(2):
                        for k in range(KD):
                            m = pe.matmul(bank(b0 + g)[:, c * SEQ:(c + 1) * SEQ], w[:, k, (2 * g + c) * P:(2 * g + c + 1) * P], hT2[:, k, :],
                                          start=(k == 0), stop=(k == KD - 1))
                m.then_inc(gu_ps, 1)
            for n, pc in enumerate(pc_dn[i]):
                w = arrived(pe, pc)
                if n in (0, 5):
                    pe.wait_ge(gu_done, 11 * i + (10 if n == 0 else 11))
                for j in range(w.shape[1]):
                    f = 4 * n + j
                    for t in range(TT):
                        for d in range(2):
                            m = pe.matmul(bank(2 * t + d), actF[:, f, t * P:(t + 1) * P], w[:, j, d * 512:(d + 1) * 512],
                                          start=(f == 0), stop=(f == FC2 - 1))
                m.then_inc(dn_ps, 1)

        def act_ffn(act, o, i, n_rms):
            act.wait_ge(post_done, 2 * (i + 1))
            act_pre(act, o, n_rms, 2 * i + 1)
            for n in range(11):
                act.wait_ge(gu_ps, 11 * i + n + 1)
                if n >= 2:
                    act.wait_ge(gu_done, 11 * i + n - 1)
                o(act.activation(sil[n % 2], bank(4 + 2 * (n % 2)), ACT.Silu), gu_silu)
            act.wait_ge(dn_ps, 6 * (i + 1))
            act_rms(act, o, [bank(2 * t, 2) for t in range(TT)], tmpJ, n_rms + 1)

        def dve_ffn(dve, o, i, n_rms):
            dve_pre(dve, o, n_rms, 2 * i + 1, 4 * (i + 1))
            for n in range(11):
                dve.wait_ge(gu_silu, 11 * i + n + 1)
                o(dve.tensor_tensor(actF[:, 2 * n:2 * n + 2, :].rearrange("p c s -> p (c s)"), sil[n % 2], bank(5 + 2 * (n % 2)), ALU.mult), gu_done)
            post(dve, o, n_rms + 1, 0, gB, ffn_done, tmpP)

        def pool_ffn(pool, i):
            pool.wait_ge(post_done, 2 * (i + 1))
            pool_gains(pool, i, ("norm_ffn_pre_2", "norm_ffn_post_2"))


        def pool_s9(pool):
            pool.wait_ge(ff_ps, 1)
            pool_gains(pool, 0, ("norm_mix_pre_2", "norm_mix_post_2"))
            for t in range(TT):
                for g in range(3):
                    for a in range(2):
                        src = bass.AP(bv_dram.tensor, bv_dram.offset + (HPG * g + a) * 2 * SEQ + SEQ - (t + 1) * P,
                                      [[1, P], [2 * 2 * SEQ, 2], [1, SEQ]])
                        dma(pool, BM[t][g][:, 2 * a:2 * a + 2, :], src, bm_in)

        def pe_s9(pe):
            pe.wait_ge(x2_ready, 2)
            pe_pre(pe, 0)
            pe.wait_ge(mkv_ready, 3)
            w = arrived(pe, pc_at[0])
            for t in range(TT):
                for k in range(KD):
                    pe.matmul(bank(4)[:, t * SEQ:(t + 1) * SEQ], hT2[:, k, t * P:(t + 1) * P], w[:, k, 0:256], start=(k == 0), stop=(k == KD - 1))
            for c in range(2):
                for k in range(KD):
                    m = pe.matmul(bank(5)[:, c * SEQ:(c + 1) * SEQ], w[:, k, 256 + c * P:256 + (c + 1) * P], hT2[:, k, :], start=(k == 0), stop=(k == KD - 1))
            m.then_inc(proj_ps, 1)
            pe.wait_ge(proj_ev, 6)
            pe_mem_scores(pe, 0, qmA)
            pe_cols(pe, arrived(pe, pc_at[1]), 6, hT2, KD, proj_ps)
            pe.wait_ge(sc_sub, 5)
            pe_cols(pe, arrived(pe, pc_at[2]), 0, hT2, KD, proj_ps)
            pe.wait_ge(proj_ev, 7)
            pe_mem_probs(pe, 0)
            pe.wait_ge(sc_sub, 6)
            pe_cols(pe, arrived(pe, pc_at[3]), 2, hT2, KD, proj_ps)
            pe.wait_ge(proj_ev, 8)
            pe_rows(pe, arrived(pe, pc_at[4]), (0, 1), hT2, KD, proj_ps)
            pe.wait_ge(proj_ev, 10)
            pe.wait_ge(bm_in, 16 * 12)
            for t in range(TT):
                for g in range(3):
                    n = 6 + 3 * t + g
                    pe.wait_ge(sc_sub, n - 1)
                    pe_scores(pe, n, lambda i: half_head(qkA, 2 * g, i)[:, t * P:(t + 1) * P], lambda i: half_head(qkA, 6 + 2 * g, i), BM[t][g])
            for t in range(TT):
                for g in range(3):
                    n = 6 + 3 * t + g
                    pe_probs(pe, n, n, lambda kb, i: vA[:, kb, (HPG * g + i) * HD:(HPG * g + i + 1) * HD])
            pe.wait_ge(pv_ev, 12)
            pe_out(pe, 0)

        def act_s9(act, o):
            act.wait_ge(x2_ready, 2)
            act_pre(act, o, 6, 0)
            act.wait_ge(proj_ps, 5)
            o(act.copy(vA[:, :, 512:768], bank(4).rearrange("p (t n) -> p t n", t=TT)), proj_ev)
            o(act.copy(qmA.rearrange("p c s -> p (c s)"), bank(5)), proj_ev)

            def qk(n):
                act.wait_ge(proj_ps, 6 + n)
                o(act.copy(qkA[:, 4 * n:4 * n + 4, :].rearrange("p c s -> p (c s)"), bank((6, 0, 2)[n], 2)), proj_ev)

            def exps(units):
                for n in units:
                    act.wait_ge(sc_sub, n + 1)
                    o(act.activation(probs_of(n), probs_of(n), ACT.Exp), sc_exp)
            exps((4, 5))
            qk(0)
            qk(1)
            act_probsT(act, o, 4)
            act_probsT(act, o, 5)
            qk(2)
            act.wait_ge(proj_ps, 9)
            o(act.copy(vA[:, :, 0:512], bank(0, 2).rearrange("p (t n) -> p t n", t=TT)), proj_ev)
            for t in range(TT):
                exps(range(6 + 3 * t, 9 + 3 * t))
                act.wait_ge(fn_asked, t + 2)
                o(act.activation(em3[t], em3[t], ACT.Exp), fn_done)
            for n in range(6, 12):
                act_probsT(act, o, n)
            act.wait_ge(out_ps, 7)
            act_rms(act, o, [bank(4 + 2 * t, 2) for t in range(TT)], tmpJ, 7)

        def dve_s9(dve, o):
            dve_pre(dve, o, 6, 0, 2)
            for t in range(TT):
                dve_softmax(dve, o, t, 4 + t, HD ** -0.5, None)
            for t in range(TT):
                dve_pv(dve, o, t, 4 + t, yA[:, 6:8, t * P:(t + 1) * P])

            def heads(n):
                return probs_of(n).rearrange("p (h k) -> p h k", h=HPG)

            def weigh(t):
                for g in range(3):
                    n = 6 + 3 * t + g
                    dve.wait_ge(sc_exp, n + 1)
                    o(dve.tensor_reduce(dn3[t][:, g, :], heads(n), AX.X, ALU.add))
                dve.wait_ge(fn_done, t + 2)
                o(dve.tensor_tensor(dn3[t], dn3[t], em3[t], ALU.mult))
                o(dve.tensor_tensor(mxx[t], dn3[t][:, 0, :], dn3[t][:, 1, :], ALU.add))
                o(dve.tensor_tensor(mxx[t], mxx[t], dn3[t][:, 2, :], ALU.add))
                o(dve.reciprocal(mxx[t], mxx[t]))
                o(dve.tensor_tensor(em3[t], em3[t], rows_bc(mxx[t], 3), ALU.mult))
                for g in range(3):
                    n = 6 + 3 * t + g
                    o(dve.tensor_tensor(heads(n), heads(n), cols_bc(em3[t][:, g, :], SEQ), ALU.mult), pr_ready)

            def outs(t):
                for g in range(3):
                    dve_pv(dve, o, None, 6 + 3 * t + g, yA[:, 2 * g:2 * g + 2, t * P:(t + 1) * P])
            dve.wait_ge(prT_ps, 6)
            for t in range(TT):
                for g in range(3):
                    n = 6 + 3 * t + g
                    dve.wait_ge(sc_ps, n + 1)
                    dve_less_max(dve, o, heads(n), bank(2 * (n % 2), 2).rearrange("p (h k) -> p h k", h=HPG), mx3[t][:, g, :], HD ** -0.5)
                o(dve.tensor_tensor(mxx[t], mx3[t][:, 0, :], mx3[t][:, 1, :], ALU.max))
                o(dve.tensor_tensor(mxx[t], mxx[t], mx3[t][:, 2, :], ALU.max))
                o(dve.tensor_tensor(em3[t], mx3[t], rows_bc(mxx[t], 3), ALU.subtract), fn_asked)
            for t in range(TT):
                weigh(t)
            for t in range(TT):
                outs(t)
            post(dve, o, 7, 4, gB, post_done, tmpP)

        (dl_in, cv_ready, cs_ready, qk_ready) = (sem(n) for n in (
            "dl_in", "cv_ready", "cs_ready", "qk_ready"))
        (g_done, gc_ps, gr_in, gr_ps, df_ready, df_exp, kk_ps, kq_ps, kq_read) = (sem(n) for n in (
            "g_done", "gc_ps", "gr_in", "gr_ps", "df_ready", "df_exp", "kk_ps", "kq_ps", "kq_read"))
        (lm_ready, la_ps, la_ready, lx_ps, rhs_ready, uw_ps, uw_ready, kl_ready, st_ps, s_out, vn_ps, un_ready, o_ps, o_read) = (sem(n) for n in (
            "lm_ready", "la_ps", "la_ready", "lx_ps", "rhs_ready", "uw_ps", "uw_ready", "kl_ready", "st_ps", "s_out", "vn_ps", "un_ready", "o_ps", "o_read"))
        (onorm_in, on_ready, lev_in, L_ready, t_first, t_ready) = (sem(n) for n in (
            "onorm_in", "on_ready", "lev_in", "L_ready", "t_first", "t_ready"))
        NM = TT * DH
        CH = 3 * DH
        PADW = SEQ + TAPS - 1
        rawP = ar3(10240, CH * PADW, CH)
        conv = ar3(14920, CH * SEQ, CH)
        nat = ar3(10240, TT * CH * DD, TT * CH)
        qkT = ar3(14848, 2 * DH * SEQ, 2 * DH)
        zN = ar3(19528, TT * TW, TT)
        oN = ar3(21064, NM * DD, NM)
        qmD = ar3(6144, 512, 2)
        Lm = ar3(0, NM * P, NM)
        Tm, TTm = ar3(4096, NM * P, NM), ar3(8192, NM * P, NM)
        intra = ar3(17920, NM * P, NM)
        scr = ar3(1536, NM * P, NM)
        Ab = [ar(6144 + 512 * n, 512) for n in range(3)]
        uD, wTD = ar3(0, NM * P, NM), ar3(4096, DH * P, DH)
        rhsD = ar3(1536, NM * P, DH)
        klD, stD = ar3(1536, DH * P, DH), ar3(2304, DH * P, DH)
        LEVELS = 7
        lev_at = names["before"][0]
        levC = CON[:, lev_at:lev_at + LEVELS * 2 * P]

        def level(n, d):
            return levC[:, (2 * n + d) * P:(2 * n + d + 1) * P]

        taps = sm(900, CH * TAPS).rearrange("p (c k) -> p c k", c=CH)
        gin = sm(990, TT * 4 * DH).rearrange("p (t d b h) -> p t d b h", t=TT, d=2, b=2)
        alog, dtb = sm(1038, 12), sm(1050, 12)
        gdl, gab, beta = (sm(1062 + 24 * n, 24).rearrange("p (t d h) -> p t d h", t=TT, d=2) for n in range(3))
        gcs, egc, ekl = (sm(1134 + 24 * n, 24).rearrange("p (t d h) -> p t d h", t=TT, d=2) for n in range(3))
        ssn = sm(1206, 24).rearrange("p (t h) -> p t h", t=TT)
        sso = sm(1230, 12)
        onr = ar(9728, DD)

        def merge4(x):
            return x.rearrange("p a b -> p (a b)")

        def pool_delta_loads(pool):
            for c in range(CH):
                dma(pool, taps[:, c, :], A["dn_conv_2"][0][:, c * P:(c + 1) * P].rearrange("k p -> p k"), dl_in)
            dma(pool, alog, row(A["dn_a_log_2"][0].rearrange("d h -> (d h)")), dl_in)
            dma(pool, dtb, row(A["dn_dt_bias_2"][0].rearrange("d h -> (d h)")), dl_in)

        def pool_s11(pool):
            pool.wait_ge(ffn_done, 2)
            pool_gains(pool, 1, ("norm_mix_pre_2", "norm_mix_post_2"))
            pool.wait_ge(mkv_ready, 4)
            dma(pool, levC, A["k_levels"], lev_in)
            for d in range(2):
                pool.wait_ge(L_ready, d + 1)
                for n in range(1, LEVELS):
                    masked = 3 * ((LEVELS - 1) * d + n - 1)
                    for b in range(3):
                        if n > 1:
                            pool.wait_ge(la_ps, masked - 3 + b + 1)
                        pool.tensor_tensor(scr[:, 4 * b:4 * b + 4, :], Lm[:, 4 * b:4 * b + 4, :], rows_bc(level(n, d), 4),
                                           ALU.mult).then_inc(lm_ready, 1)
            pool.wait_ge(o_read, 2)
            dma(pool, onr, row(A["dn_out_norm_2"][0]), onorm_in)
        DL_IN = 16 * (CH + 2)

        def pe_s11(pe):
            pe.wait_ge(ffn_done, 2)
            pe_pre(pe, 2)
            pe.wait_ge(mkv_ready, 4)
            w = arrived(pe, pc_dw[0])
            for t in range(TT):
                for k in range(KD):
                    pe.matmul(bank(0)[:, t * 24:(t + 1) * 24], hT2[:, k, t * P:(t + 1) * P], w[:, k, 0:24], start=(k == 0), stop=(k == KD - 1))
            for c in range(2):
                for k in range(KD):
                    m = pe.matmul(bank(1)[:, c * SEQ:(c + 1) * SEQ], w[:, k, 24 + c * P:24 + (c + 1) * P], hT2[:, k, :], start=(k == 0), stop=(k == KD - 1))
            m.then_inc(proj_ps, 1)
            pe.wait_ge(proj_ev, 12)
            pe_mem_scores(pe, 1, qmD)
            pe_cols(pe, arrived(pe, pc_dw[1]), 4, hT2, KD, proj_ps)
            pe.wait_ge(sc_sub, 13)
            pe_cols(pe, arrived(pe, pc_dw[2]), 0, hT2, KD, proj_ps)
            pe.wait_ge(proj_ev, 13)
            pe_mem_probs(pe, 1)
            pe.wait_ge(sc_sub, 14)
            pe_cols(pe, arrived(pe, pc_dw[3]), 2, hT2, KD, proj_ps)
            pe.wait_ge(prT_ready, 14)
            pe_cols(pe, arrived(pe, pc_dw[4]), 4, hT2, KD, proj_ps)
            w = arrived(pe, pc_dw[5])
            pe.wait_ge(pv_ev, 14)
            for c in range(2):
                for k in range(KD):
                    pe.matmul(bank(6)[:, c * SEQ:(c + 1) * SEQ], w[:, k, c * P:(c + 1) * P], hT2[:, k, :], start=(k == 0), stop=(k == KD - 1))
            for t in range(TT):
                for k in range(KD):
                    m = pe.matmul(bank(7)[:, t * SEQ:(t + 1) * SEQ], hT2[:, k, t * P:(t + 1) * P], w[:, k, 256:512], start=(k == 0), stop=(k == KD - 1))
            m.then_inc(proj_ps, 1)
            pe.wait_ge(proj_ev, 14)
            pe_rows(pe, arrived(pe, pc_dw[6]), (0, 1), hT2, KD, proj_ps)
            pe.wait_ge(proj_ev, 19)
            pe.wait_ge(cs_ready, 3)
            for b in range(NT):
                if b >= 8:
                    pe.wait_ge(turned, D_BASE + b - 7)
                for j in range(4):
                    n = 4 * b + j
                    t, c = n // CH, n % CH
                    m = pe.transpose(bank(b % 8)[:, j * P:(j + 1) * P], conv[:, c, t * P:(t + 1) * P], ident)
                m.then_inc(turn_ps, 1)
            pe.wait_ge(g_done, 1)
            pe.wait_ge(turned, D_BASE + NT)
            for t in range(TT):
                pe.matmul(bank(7)[:, t * 12:t * 12 + 6], con("upto"), gdl[:, t, 0, :], start=True, stop=True)
                pe.matmul(bank(7)[:, t * 12 + 6:t * 12 + 12], con("from"), gdl[:, t, 1, :], start=True, stop=True)
            m = pe.matmul(bank(7)[:, 24:48], con("ones"), gdl.rearrange("p t d h -> p (t d h)"), start=True, stop=True)
            m.then_inc(gc_ps, 1)
            pe.wait_ge(qk_ready, 1)
            for b in range(6):
                for j in range(4):
                    n = 4 * b + j
                    t, c = n // (2 * DH), n % (2 * DH)
                    m = pe.transpose(bank(b)[:, j * P:(j + 1) * P], nat[:, t * CH + c, :], ident)
                m.then_inc(turn_ps, 1)
            pe.wait_ge(turned, D_BASE + NT + QT)
            pe.wait_ge(fn_asked, 5)
            for d in range(2):
                pe_delta(pe, d)
            pe.wait_ge(on_ready, 1)
            for b in range(3):
                for j in range(4):
                    t, h = (4 * b + j) // DH, (4 * b + j) % DH
                    m = pe.transpose(bank(b)[:, j * P:(j + 1) * P], oN[:, t * DH + h, :], ident)
                m.then_inc(turn_ps, 1)
            pe.wait_ge(turned, D_BASE + NT + QT + OT)
            pe_out(pe, 1)

        def mh(m):
            return m // DH, m % DH

        def pe_delta(pe, d):
            first, second = (0, 1) if d == 0 else (1, 0)
            pe.wait_ge(gr_in, d + 1)
            for b in range(3):
                m = pe.matmul(bank(b), con("ones"), merge4(scr[:, 4 * b:4 * b + 4, :]), start=True, stop=True)
            m.then_inc(gr_ps, 1)
            for b in range(3):
                for j in range(4):
                    t, h = mh(4 * b + j)
                    m = pe.matmul(bank(3 + b)[:, j * P:(j + 1) * P], qkT[:, DH + h, t * P:(t + 1) * P], qkT[:, h, t * P:(t + 1) * P], start=True, stop=True)
            m.then_inc(kq_ps, 1)
            pe.wait_ge(df_ready, 2 * d + 2)
            for b in range(3):
                for j in range(4):
                    t, h = mh(4 * b + j)
                    m = pe.matmul(bank(b)[:, j * P:(j + 1) * P], qkT[:, DH + h, t * P:(t + 1) * P], qkT[:, DH + h, t * P:(t + 1) * P], start=True, stop=True)
            m.then_inc(kk_ps, 1)
            pe.wait_ge(kq_read, d + 1)
            for b in range(3):
                pe.wait_ge(t_first, 3 * d + b + 1)
                for j in range(4):
                    m = pe.transpose(bank(3 + b)[:, j * P:(j + 1) * P], Tm[:, 4 * b + j, :], ident)
                m.then_inc(lx_ps, 1)
            for n in range(1, LEVELS):
                done = 3 * (LEVELS * d + n)
                masked = 3 * ((LEVELS - 1) * d + n - 1)
                for b in range(3):
                    pe.wait_ge(lm_ready, masked + b + 1)
                    pe.wait_ge(t_ready, done - 3 + b + 1)
                    for j in range(4):
                        m_ = 4 * b + j
                        m = pe.matmul(bank(b)[:, j * P:(j + 1) * P], scr[:, m_, :], TTm[:, m_, :], start=True, stop=True)
                    m.then_inc(la_ps, 1)
                for b in range(3):
                    pe.wait_ge(la_ready, masked + b + 1)
                    for j in range(4):
                        m_ = 4 * b + j
                        m = pe.matmul(bank(3 + b)[:, j * P:(j + 1) * P], Tm[:, m_, :], Ab[b][:, j * P:(j + 1) * P], start=True, stop=True)
                    for j in range(4):
                        m_ = 4 * b + j
                        if n < LEVELS - 1:
                            m = pe.matmul(bank(b)[:, j * P:(j + 1) * P], Ab[b][:, j * P:(j + 1) * P], Tm[:, m_, :], start=True, stop=True)
                    m.then_inc(lx_ps, 1)
            pe.wait_ge(t_ready, 3 * LEVELS * (d + 1))
            for t in range(TT):
                pe.wait_ge(rhs_ready, 2 * d + t + 1)
                for h in range(DH):
                    m_ = t * DH + h
                    m = pe.matmul(bank(m_ // 4)[:, (m_ % 4) * P:(m_ % 4 + 1) * P], TTm[:, m_, :], rhsD[:, h, 0:P], start=True, stop=True)
                if t == second:
                    for h in range(DH):
                        m = pe.matmul(bank(3 + h // 4)[:, (h % 4) * P:(h % 4 + 1) * P], rhsD[:, h, P:2 * P], TTm[:, t * DH + h, :], start=True, stop=True)
                m.then_inc(uw_ps, 1)
            pe.wait_ge(uw_ready, d + 1)
            pe.wait_ge(kl_ready, d + 1)
            for h in range(DH):
                m = pe.matmul(bank(5 + h // 4)[:, (h % 4) * P:(h % 4 + 1) * P], klD[:, h, :], uD[:, first * DH + h, :], start=True, stop=True)
            m.then_inc(st_ps, 1)
            pe.wait_ge(s_out, d + 1)
            for h in range(DH):
                m = pe.matmul(bank(3 + h // 4)[:, (h % 4) * P:(h % 4 + 1) * P], wTD[:, h, :], stD[:, h, :], start=True, stop=True)
            for h in range(DH):
                m = pe.matmul(bank(h // 4)[:, (h % 4) * P:(h % 4 + 1) * P], qkT[:, h, second * P:(second + 1) * P], stD[:, h, :], start=True, stop=True)
            m.then_inc(vn_ps, 1)
            pe.wait_ge(un_ready, d + 1)
            for i, t in enumerate((first, second)):
                for h in range(DH):
                    m = pe.matmul(bank(4 + 2 * i + h // 4)[:, (h % 4) * P:(h % 4 + 1) * P], intra[:, t * DH + h, :], uD[:, t * DH + h, :], start=True, stop=True)
            m.then_inc(o_ps, 1)
            pe.wait_ge(o_read, d + 1)

        def act_s11(act, o):
            act.wait_ge(ffn_done, 2)
            o(act.copy(kvNow, kvKept), mkv_ready)
            act_pre(act, o, 10, 2)
            def raw(n):
                act.wait_ge(proj_ps, 10 + n + 1)
                o(act.copy(rawP[:, 4 * n:4 * n + 4, 2:2 + SEQ], bank((4, 0, 2, 4)[n], 2).rearrange("p (c s) -> p c s", c=4)), proj_ev)

            def silu(n):
                act.wait_ge(cv_ready, DH * (n + 1))
                c = conv[:, DH * n:DH * (n + 1), :]
                o(act.activation(c, c, ACT.Silu), cs_ready)
            act.wait_ge(proj_ps, 10)
            o(act.copy(gin.rearrange("p t d b h -> p (t d b h)"), bank(0)[:, 0:48]), proj_ev)
            o(act.copy(qmD.rearrange("p c s -> p (c s)"), bank(1)), proj_ev)
            for n in (12, 13):
                act.wait_ge(sc_sub, n + 1)
                o(act.activation(probs_of(n), probs_of(n), ACT.Exp), sc_exp)
            raw(0)
            raw(1)
            act_probsT(act, o, 12)
            act_probsT(act, o, 13)
            act.wait_ge(fn_asked, 4)
            o(act.activation(beta, gin[:, :, :, 1, :], ACT.Sigmoid))
            o(act.activation(alog, alog, ACT.Exp))
            o(act.activation(gab, gab, ACT.Exp, scale=-1.0))
            o(act.activation(gab, gab, ACT.Ln, bias=1.0), fn_done)
            raw(2)
            silu(0)
            raw(3)
            silu(1)
            act.wait_ge(proj_ps, 15)
            o(act.copy(rawP[:, 16:18, 2:2 + SEQ], bank(6).rearrange("p (c s) -> p c s", c=2)), proj_ev)
            o(act.copy(zN[:, :, 0:256], bank(7).rearrange("p (t n) -> p t n", t=TT)), proj_ev)
            silu(2)
            act.wait_ge(proj_ps, 16)
            o(act.copy(zN[:, :, 256:768], bank(0, 2).rearrange("p (t n) -> p t n", t=TT)), proj_ev)
            for b in range(NT):
                act.wait_ge(turn_ps, D_BASE + b + 1)
                o(act.copy(merge4(nat[:, 4 * b:4 * b + 4, :]), bank(b % 8)), turned)
            act.wait_ge(fn_asked, 5)
            o(act.activation(egc, gcs, ACT.Exp))
            o(act.activation(ekl, ekl, ACT.Exp), fn_done)
            act.wait_ge(fn_asked, 6)
            o(act.activation(ssn, ssn, ACT.Sqrt), fn_done)
            for b in range(6):
                act.wait_ge(turn_ps, D_BASE + NT + b + 1)
                n = 4 * b
                t, c = n // (2 * DH), n % (2 * DH)
                o(act.copy(qkT[:, c:c + 4, t * P:(t + 1) * P], bank(b).rearrange("p (c s) -> p c s", c=4)), turned)
            for d in range(2):
                act_delta(act, o, d)
            act.wait_ge(fn_asked, 7)
            o(act.activation(sso, sso, ACT.Sqrt), fn_done)
            o(act.activation(zN, zN, ACT.Silu), fn_done)
            for b in range(3):
                act.wait_ge(turn_ps, D_BASE + NT + QT + b + 1)
                for j in range(4):
                    t, h = (4 * b + j) // DH, (4 * b + j) % DH
                    o(act.copy(yA[:, h, t * P:(t + 1) * P], bank(b)[:, j * P:(j + 1) * P]), turned if j == 3 else None)
            act.wait_ge(out_ps, 9)
            act_rms(act, o, [bank(4 + 2 * t, 2) for t in range(TT)], tmpJ, 11)

        def act_delta(act, o, d):
            second = 1 - d
            act.wait_ge(df_ready, 2 * d + 1)
            o(act.activation(intra, intra, ACT.Exp), df_exp)
            act.wait_ge(df_ready, 2 * d + 2)
            o(act.activation(Lm, Lm, ACT.Exp, scale=-1.0), df_exp)
            for n in range(1, LEVELS):
                masked = 3 * ((LEVELS - 1) * d + n - 1)
                for b in range(3):
                    act.wait_ge(la_ps, masked + b + 1)
                    if n > 1:
                        act.wait_ge(lx_ps, 3 * (LEVELS * d + n - 1) + b + 1)
                    o(act.copy(Ab[b], bank(b)), la_ready)
            act.wait_ge(uw_ps, 2 * d + 2)
            o(act.copy(merge4(uD), bank(0, 3)))
            o(act.copy(merge4(wTD), bank(3, 2)[:, 0:DH * P]), uw_ready)
            act.wait_ge(st_ps, d + 1)
            o(act.copy(merge4(stD), bank(5, 2)[:, 0:DH * P]), s_out)

        def dve_s11(dve, o):
            dve.wait_ge(dl_in, DL_IN)
            dve_pre(dve, o, 10, 2, 6)
            o(dve.memset(spread(rawP[:, 0, 0:1], [PADW, CH], [1, TAPS // 2]), 0.0))
            o(dve.memset(spread(rawP[:, 0, SEQ + TAPS // 2:SEQ + TAPS // 2 + 1], [PADW, CH], [1, TAPS // 2]), 0.0))
            for t in range(TT):
                dve_softmax(dve, o, t, 12 + t, HD ** -0.5, None)
            o(dve.tensor_tensor(gdl, gin[:, :, :, 0, :], rows_bc(dtb.rearrange("p (d h) -> p d h", d=2), TT), ALU.add))
            o(dve.tensor_scalar(gab, gdl, -1.0, None, ALU.mult))
            o(dve.tensor_tensor(gab, gab, gdl, ALU.max), fn_asked)
            o(dve.tensor_scalar(gdl, gdl, 0.0, None, ALU.max))

            def convolve(first, last):
                for c in range(first, last):
                    dve.wait_ge(proj_ev, 12 + c // 4 + 1)
                    o(dve.tensor_scalar(conv[:, c, :], rawP[:, c, 0:SEQ], taps[:, c, 0:1], None, ALU.mult))
                    for k in range(1, TAPS):
                        o(dve.scalar_tensor_tensor(conv[:, c, :], rawP[:, c, k:k + SEQ], taps[:, c, k:k + 1], conv[:, c, :], ALU.mult, ALU.add),
                          cv_ready if k == TAPS - 1 else None)
            convolve(0, 4)
            for t in range(TT):
                dve_pv(dve, o, t, 12 + t, yA[:, 6:8, t * P:(t + 1) * P])
            dve.wait_ge(fn_done, 4)
            o(dve.tensor_tensor(gdl, gdl, gab, ALU.add))
            o(dve.tensor_tensor(gdl, gdl, rows_bc(alog.rearrange("p (d h) -> p d h", d=2), TT), ALU.mult))
            o(dve.tensor_scalar(gdl, gdl, -1.0, None, ALU.mult), g_done)
            convolve(4, CH)
            dve.wait_ge(gc_ps, 1)
            o(dve.tensor_copy(gcs.rearrange("p t d h -> p (t d h)"), bank(7)[:, 0:24]))
            o(dve.tensor_tensor(ekl.rearrange("p t d h -> p (t d h)"), bank(7)[:, 24:48], gcs.rearrange("p t d h -> p (t d h)"), ALU.subtract), fn_asked)
            sq = Tm
            for t in range(TT):
                x = nat[:, t * CH:t * CH + 2 * DH, :]
                o(dve.tensor_tensor(sq, x, x, ALU.mult))
                o(dve.tensor_reduce(ssn[:, t, :], sq, AX.X, ALU.add))
            o(dve.tensor_scalar(ssn, ssn, EPS, None, ALU.add), fn_asked)
            dve.wait_ge(fn_done, 6)
            o(dve.reciprocal(ssn, ssn))
            o(dve.tensor_scalar(ssn[:, :, 0:DH], ssn[:, :, 0:DH], DD ** -0.5, None, ALU.mult))
            for t in range(TT):
                x = nat[:, t * CH:t * CH + 2 * DH, :]
                o(dve.tensor_tensor(x, x, cols_bc(ssn[:, t, :], DD), ALU.mult), qk_ready if t == TT - 1 else None)
            o(dve.memset(oN, 0.0))
            dve.wait_ge(fn_done, 5)
            dve.wait_ge(turned, D_BASE + NT + QT)
            for d in range(2):
                dve_delta(dve, o, d)
            sq = Lm
            o(dve.tensor_tensor(sq, oN, oN, ALU.mult))
            o(dve.tensor_reduce(sso, sq, AX.X, ALU.add))
            o(dve.tensor_scalar(sso, sso, 1.0 / DD, EPS, ALU.mult, ALU.add), fn_asked)
            dve.wait_ge(fn_done, 7)
            o(dve.reciprocal(sso, sso))
            o(dve.tensor_tensor(oN, oN, cols_bc(sso, DD), ALU.mult))
            dve.wait_ge(onorm_in, 16)
            o(dve.tensor_tensor(oN, oN, rows_bc(onr, NM), ALU.mult))
            dve.wait_ge(fn_done, 8)
            o(dve.tensor_tensor(merge4(oN), merge4(oN), merge4(zN), ALU.mult), on_ready)
            post(dve, o, 11, 4, gB, post_done, tmpP)

        def dve_delta(dve, o, d):
            first, second = (0, 1) if d == 0 else (1, 0)
            def per(x):
                return bass.AP(x.tensor, x.offset + d * DH, [list(x.ap[0]), [2 * DH, TT], [1, DH]])
            def wide(x):
                y = per(x)
                return bass.AP(y.tensor, y.offset, [list(v) for v in y.ap] + [[0, P]])
            def four(x):
                return x.rearrange("p (t h) n -> p t h n", t=TT)
            tri = con("upto") if d == 0 else con("from")
            tri4 = bass.AP(tri.tensor, tri.offset, [list(tri.ap[0]), [0, TT], [0, DH], [1, P]])
            o(dve.tensor_tensor(four(scr), tri4, wide(gdl), ALU.mult), gr_in)
            dve.wait_ge(gr_ps, d + 1)
            o(dve.tensor_tensor(four(Tm), bank(0, 3).rearrange("p (t h n) -> p t h n", t=TT, h=DH), wide(gcs), ALU.subtract))
            o(dve.tensor_scalar(intra, Tm, 0.0, None, ALU.min), df_ready)
            o(dve.tensor_scalar(Lm, Tm, 0.0, None, ALU.max), df_ready)
            dve.wait_ge(df_exp, 2 * d + 1)
            o(dve.tensor_tensor(intra, intra, rows_bc(tri, NM), ALU.mult))
            dve.wait_ge(kq_ps, d + 1)
            o(dve.tensor_tensor(merge4(intra), merge4(intra), bank(3, 3), ALU.mult), kq_read)
            dve.wait_ge(df_exp, 2 * d + 2)
            o(dve.tensor_tensor(four(Lm), four(Lm), wide(beta), ALU.mult))
            dve.wait_ge(kk_ps, d + 1)
            o(dve.tensor_tensor(merge4(Lm), merge4(Lm), bank(0, 3), ALU.mult))
            dve.wait_ge(lev_in, 16)
            def group(x, b):
                return x[:, 4 * b:4 * b + 4, :]
            for b in range(3):
                o(dve.tensor_tensor(group(Tm, b), group(Lm, b), rows_bc(level(0, d), 4), ALU.mult), L_ready if b == 0 else None)
                o(dve.tensor_tensor(group(Tm, b), rows_bc(ident, 4), group(Tm, b), ALU.subtract), t_first)
            for n in range(LEVELS):
                for b in range(3):
                    dve.wait_ge(lx_ps, 3 * (LEVELS * d + n) + b + 1)
                    tt, tm = merge4(group(TTm, b)), merge4(group(Tm, b))
                    if n == 0:
                        o(dve.tensor_copy(tt, bank(3 + b)), t_ready)
                    elif n < LEVELS - 1:
                        o(dve.tensor_tensor(tt, tt, bank(3 + b), ALU.subtract))
                        o(dve.tensor_tensor(tm, tm, bank(b), ALU.subtract), t_ready)
                    else:
                        o(dve.tensor_tensor(tt, tt, bank(3 + b), ALU.subtract), t_ready)
            for t in range(TT):
                if t:
                    dve.wait_ge(uw_ps, 2 * d + t)
                b3 = beta[:, t, d, :]
                o(dve.tensor_tensor(rhsD[:, :, 0:P], nat[:, t * CH + 2 * DH:(t + 1) * CH, :], cols_bc(b3, P), ALU.mult))
                o(dve.tensor_tensor(sso[:, 0:DH], b3, egc[:, t, d, :], ALU.mult))
                o(dve.tensor_tensor(rhsD[:, :, P:2 * P], nat[:, t * CH + DH:t * CH + 2 * DH, :], cols_bc(sso[:, 0:DH], P), ALU.mult), rhs_ready)
            dve.wait_ge(uw_ps, 2 * d + 2)
            o(dve.tensor_tensor(klD, nat[:, first * CH + DH:first * CH + 2 * DH, :], cols_bc(ekl[:, first, d, :], P), ALU.mult), kl_ready)
            dve.wait_ge(vn_ps, d + 1)
            u2 = merge4(uD[:, second * DH:(second + 1) * DH, :])
            o(dve.tensor_tensor(u2, u2, bank(3, 2)[:, 0:DH * P], ALU.subtract), un_ready)
            inter = klD
            o(dve.tensor_tensor(inter, bank(0, 2)[:, 0:DH * P].rearrange("p (h n) -> p h n", h=DH), cols_bc(egc[:, second, d, :], P), ALU.mult))
            def o_of(t):
                return oN[:, t * DH:(t + 1) * DH, :]
            o(dve.tensor_tensor(o_of(second), o_of(second), inter, ALU.add))
            dve.wait_ge(o_ps, d + 1)
            o(dve.tensor_tensor(merge4(o_of(first)), merge4(o_of(first)), bank(4, 2)[:, 0:DH * P], ALU.add))
            o(dve.tensor_tensor(merge4(o_of(second)), merge4(o_of(second)), bank(6, 2)[:, 0:DH * P], ALU.add), o_read)

        def store_out(sp):
            for t in range(TT):
                sp.wait_ge(ffn_done, 2 + t + 1)
                sp.dma_start(out[0, t * P:(t + 1) * P, :], x3[:, t, :]).then_inc(out_stored, 16)
            sp.wait_ge(out_stored, 16 * TT)

        block = ctx.enter_context(nc.Block())

        @block.sync
        def _(sp):
            sp_first(sp)
            sp_s7(sp)
            stream(sp, LAST, LAST + 2)
            sp.wait_ge(ff_ps, 1)
            sp.wait_ge(gain_in, 32)
            stream(sp, LAST + 2, len(pieces))
            store_out(sp)

        @block.gpsimd
        def _(pool):
            pool_s0(pool)
            pool_bias_store(pool)
            pool_s6(pool)
            pool_s9(pool)
            pool_ffn(pool, 0)
            pool_delta_loads(pool)
            pool_s11(pool)
            pool_ffn(pool, 1)

        @block.scalar
        def _(act):
            o = Ordered(act, act_order)
            act_s0(act, o)
            act_s1(act, o)
            act_s2(act, o)
            act_s4(act, o)
            act_s3(act, o)
            act_s5(act, o)
            act_s6(act, o)
            act_s7(act)
            act_s8(act, o)
            act_s9(act, o)
            act_ffn(act, o, 0, 8)
            act_s11(act, o)
            act_ffn(act, o, 1, 12)

        @block.vector
        def _(dve):
            o = Ordered(dve, dve_order)
            dve_s0(dve, o)
            dve_s1(dve, o)
            dve_tables(dve, o)
            dve_s2(dve, o)
            dve_s4(dve, o)
            dve_s3(dve, o)
            dve_s5(dve, o)
            dve_s6(dve, o)
            dve_s7(dve)
            dve_s8(dve, o)
            dve_s9(dve, o)
            dve_ffn(dve, o, 0, 8)
            dve_s11(dve, o)
            dve_ffn(dve, o, 1, 12)

        @block.tensor
        def _(pe):
            pe_s0(pe)
            pe_s1(pe)
            pe_s2(pe)
            pe_s4(pe)
            pe_s3(pe)
            pe_s5(pe)
            pe_s6(pe)
            pe_s7(pe)
            pe_s8(pe)
            pe_s9(pe)
            pe_ffn(pe, 0)
            pe_s11(pe)
            pe_ffn(pe, 1)



def kernel(**inputs):
    import concourse.bacc as bacc
    from concourse.bass_utils import run_bass_kernel_spmd

    nc = bacc.Bacc("TRN2", target_bir_lowering=False, num_devices=1)
    arrays = {name: np.ascontiguousarray(a) for name, a in inputs.items()}
    arrays["ffn_w_gate_up_2"] = paired(arrays["ffn_w_gate_up_2"])
    arrays["k_main"], names, arrays["k_levels"], arrays["k_hot"] = shape_constants()
    A, fed = {}, {}
    for name, a in arrays.items():
        fed[f"in_{name}"] = a
        A[name] = nc.dram_tensor(f"in_{name}", a.shape, mybir.dt.from_np(a.dtype), kind="ExternalInput").ap()
    out = nc.dram_tensor("out", (1, SEQ, D), mybir.dt.float32, kind="ExternalOutput").ap()
    block_kernel(nc, A, out, names)
    r = run_bass_kernel_spmd(nc, [fed], core_ids=[0])
    return r.results[0]["out"]
```
